# Optimizing a Trainium2 kernel written in Bass

```python
import math
import jax, jax.numpy as jnp
from jax import lax
import numpy as np

D_MODEL = 1024
BATCH = 1
SEQ = 1024
DEPTH = 2

GRID_W = 64
CTX_LEN = 256
N_MIXERS = 2
N_RET = (DEPTH + N_MIXERS - 1) // N_MIXERS
N_POOL = DEPTH // N_MIXERS
RET_HEADS = 4
RET_QK_DIM = D_MODEL // RET_HEADS
RET_V_DIM = 2 * D_MODEL // RET_HEADS
RET_QK_TOTAL = RET_HEADS * RET_QK_DIM
RET_V_TOTAL = RET_HEADS * RET_V_DIM
RET_CHUNK = 128
POOL_WINDOWS = (2, 4, 8, 16)
POOL_GROUP = D_MODEL // len(POOL_WINDOWS)
FFN_HIDDEN = ((8 * D_MODEL + 3 * 256 - 1) // (3 * 256)) * 256
ROPE_THETA = 10000.0
EPS = 1e-6
GN_EPS = 1e-5

kernel_name = "hybrid_retention_pool_dit_trunk"

def _rmsnorm(x, w):
    x32 = x.astype(jnp.float32)
    y = x32 * lax.rsqrt(jnp.mean(x32 * x32, axis=-1, keepdims=True) + EPS)
    return (y * w.astype(jnp.float32)).astype(x.dtype)

def _modulate(h, shift, scale):
    return h * (1.0 + scale) + shift

def _rope(x, pos):
    d = x.shape[-1]
    inv = ROPE_THETA ** (-jnp.arange(0, d, 2, dtype=jnp.float32) / d)
    ang = pos[:, None] * inv[None, :]
    cos = jnp.cos(ang)[None, :, None, :].astype(x.dtype)
    sin = jnp.sin(ang)[None, :, None, :].astype(x.dtype)
    x1, x2 = x[..., : d // 2], x[..., d // 2:]
    return jnp.concatenate([x1 * cos - x2 * sin, x1 * sin + x2 * cos], axis=-1)

def _axial_rope(x, row, col):
    half = x.shape[-1] // 2
    return jnp.concatenate([_rope(x[..., :half], row), _rope(x[..., half:], col)], axis=-1)

def _retention_direction(q, k, v, log_g, s0, strict):
    bsz, length, heads, _ = q.shape
    dv = v.shape[-1]
    n_chunks = length // RET_CHUNK

    def to_chunks(t):
        return t.astype(jnp.float32).reshape(bsz, n_chunks, RET_CHUNK, heads, t.shape[-1]).transpose(1, 0, 3, 2, 4)

    qc, kc, vc = to_chunks(q), to_chunks(k), to_chunks(v)
    idx = jnp.arange(RET_CHUNK, dtype=jnp.float32)
    diff = idx[:, None] - idx[None, :]
    mask = (diff > 0) if strict else (diff >= 0)
    intra = jnp.where(mask, jnp.exp(log_g[:, None, None] * jnp.where(mask, diff, 0.0)), 0.0)
    q_decay = jnp.exp(log_g[:, None] * (idx + 1.0))[..., None]
    k_decay = jnp.exp(log_g[:, None] * (RET_CHUNK - 1.0 - idx))[..., None]
    chunk_decay = jnp.exp(log_g * RET_CHUNK)[:, None, None]

    def step(state, xs):
        qb, kb, vb = xs
        scores = jnp.einsum('bhid,bhjd->bhij', qb, kb) * intra
        out = (jnp.einsum('bhij,bhje->bhie', scores, vb)
               + jnp.einsum('bhid,bhde->bhie', qb * q_decay, state))
        state = state * chunk_decay + jnp.einsum('bhjd,bhje->bhde', kb * k_decay, vb)
        return state, out

    s_fin, out = lax.scan(step, s0.astype(jnp.float32), (qc, kc, vc))
    out = out.transpose(1, 0, 3, 2, 4).reshape(bsz, length, heads, dv)
    return out, s_fin

def _retention_output(y, g, gn_w, w_out, dtype):
    mu = jnp.mean(y, axis=-1, keepdims=True)
    var = jnp.mean(jnp.square(y - mu), axis=-1, keepdims=True)
    yn = ((y - mu) * lax.rsqrt(var + GN_EPS)).reshape(y.shape[0], y.shape[1], -1) * gn_w.astype(jnp.float32)
    return (jax.nn.silu(g.astype(jnp.float32)) * yn).astype(dtype) @ w_out

def _split_proj(p):
    bsz, length, _ = p.shape
    q = p[..., :RET_QK_TOTAL].reshape(bsz, length, RET_HEADS, RET_QK_DIM)
    k = p[..., RET_QK_TOTAL:2 * RET_QK_TOTAL].reshape(bsz, length, RET_HEADS, RET_QK_DIM)
    v = p[..., 2 * RET_QK_TOTAL:2 * RET_QK_TOTAL + RET_V_TOTAL].reshape(bsz, length, RET_HEADS, RET_V_DIM)
    g = p[..., 2 * RET_QK_TOTAL + RET_V_TOTAL:]
    return q, k, v, g

def _retention_mixer(h_lat, h_ctx, w_in, log_decay, gn_w, w_out, row, col, ctx_out):
    bsz = h_lat.shape[0]
    n_ctx = h_ctx.shape[1]
    lg = -jnp.abs(log_decay.astype(jnp.float32))
    q_scale = RET_QK_DIM ** -0.5
    zeros = jnp.zeros((bsz, RET_HEADS, RET_QK_DIM, RET_V_DIM), jnp.float32)
    flip = lambda t: jnp.flip(t, axis=1)

    if ctx_out:
        qc, kc, vc, gc = _split_proj(h_ctx @ w_in)
        qc = qc * q_scale
        yc_f, s_f = _retention_direction(qc, kc, vc, lg[0], zeros, False)
        yc_b, s_b = _retention_direction(flip(qc), flip(kc), flip(vc), lg[1], zeros, True)
        y_ctx = _retention_output(yc_f + flip(yc_b), gc, gn_w, w_out, h_ctx.dtype)
    else:
        p_kv = h_ctx @ w_in[:, RET_QK_TOTAL:2 * RET_QK_TOTAL + RET_V_TOTAL]
        kc = p_kv[..., :RET_QK_TOTAL].reshape(bsz, n_ctx, RET_HEADS, RET_QK_DIM).astype(jnp.float32)
        vc = p_kv[..., RET_QK_TOTAL:].reshape(bsz, n_ctx, RET_HEADS, RET_V_DIM).astype(jnp.float32)
        m = jnp.arange(n_ctx, dtype=jnp.float32)
        w_f = jnp.exp((n_ctx - 1.0 - m)[:, None] * lg[0][None, :])[None, :, :, None]
        w_b = jnp.exp(m[:, None] * lg[1][None, :])[None, :, :, None]
        s_f = jnp.einsum('blhd,blhe->bhde', kc * w_f, vc)
        s_b = jnp.einsum('blhd,blhe->bhde', kc * w_b, vc)
        y_ctx = None

    q, k, v, g = _split_proj(h_lat @ w_in)
    q = _axial_rope(q, row, col) * q_scale
    k = _axial_rope(k, row, col)
    y_f, _ = _retention_direction(q, k, v, lg[0], s_f, False)
    y_b, _ = _retention_direction(flip(q), flip(k), flip(v), lg[1], s_b, True)
    y_lat = _retention_output(y_f + flip(y_b), g, gn_w, w_out, h_lat.dtype)
    return y_lat, y_ctx

def _pool_mixer(h, pool_w, pool_scale):
    length = h.shape[1]
    hf = h.astype(jnp.float32)
    cs = jnp.concatenate([jnp.zeros_like(hf[:, :1]), jnp.cumsum(hf, axis=1)], axis=1)
    t = jnp.arange(length)
    outs = []
    for gi, w in enumerate(POOL_WINDOWS):
        sl = slice(gi * POOL_GROUP, (gi + 1) * POOL_GROUP)
        lo = jnp.clip(t - w // 2, 0, length)
        hi = jnp.clip(t + w // 2, 0, length)
        csg = cs[:, :, sl]
        mean = (csg[:, hi] - csg[:, lo]) / (hi - lo).astype(jnp.float32)[None, :, None]
        outs.append(jnp.einsum('bld,de->ble', (mean - hf[:, :, sl]).astype(h.dtype), pool_w[gi]))
    return jnp.concatenate(outs, axis=-1) * pool_scale

def _swiglu(h, w_in, w_out):
    a, b = jnp.split(h @ w_in, 2, axis=-1)
    return (jax.nn.silu(a) * b) @ w_out

def setup_inputs(seed: int = 0) -> dict:
    key = jax.random.key(seed)
    ks = jax.random.split(key, 18)
    nrm = jax.random.normal
    f32 = jnp.float32
    base_decay = np.log(1.0 - 2.0 ** (-5.0 - np.arange(RET_HEADS))).astype(np.float32)
    return {
        "x": nrm(ks[0], (BATCH, SEQ, D_MODEL), f32),
        "c": nrm(ks[1], (BATCH, D_MODEL), f32),
        "ctx": nrm(ks[2], (BATCH, CTX_LEN, D_MODEL), f32),
        "c_ctx": nrm(ks[3], (D_MODEL,), f32),
        "ada_w": nrm(ks[4], (DEPTH, D_MODEL, 6 * D_MODEL), f32) * (0.5 * D_MODEL ** -0.5),
        "ada_b": 0.01 * nrm(ks[5], (DEPTH, 6 * D_MODEL), f32),
        "norm1_w": 1.0 + 0.05 * nrm(ks[6], (DEPTH, D_MODEL), f32),
        "norm2_w": 1.0 + 0.05 * nrm(ks[7], (DEPTH, D_MODEL), f32),
        "ret_w_in": nrm(ks[8], (N_RET, D_MODEL, 2 * RET_QK_TOTAL + 2 * RET_V_TOTAL), f32) * D_MODEL ** -0.5,
        "ret_log_decay": jnp.asarray(base_decay)[None, None, :] * (1.0 + 0.1 * nrm(ks[9], (N_RET, 2, RET_HEADS), f32)),
        "ret_gn_w": 1.0 + 0.05 * nrm(ks[10], (N_RET, RET_V_TOTAL), f32),
        "ret_w_out": nrm(ks[11], (N_RET, RET_V_TOTAL, D_MODEL), f32) * RET_V_TOTAL ** -0.5,
        "pool_w": nrm(ks[12], (N_POOL, len(POOL_WINDOWS), POOL_GROUP, POOL_GROUP), f32) * POOL_GROUP ** -0.5,
        "pool_scale": 1.0 + 0.05 * nrm(ks[13], (N_POOL, D_MODEL), f32),
        "ffn_w_in": nrm(ks[14], (DEPTH, D_MODEL, 2 * FFN_HIDDEN), f32) * D_MODEL ** -0.5,
        "ffn_w_out": nrm(ks[15], (DEPTH, FFN_HIDDEN, D_MODEL), f32) * FFN_HIDDEN ** -0.5,
        "final_norm_w": 1.0 + 0.05 * nrm(ks[16], (D_MODEL,), f32),
    }

def reference(x, c, ctx, c_ctx, ada_w, ada_b, norm1_w, norm2_w, ret_w_in, ret_log_decay, ret_gn_w,
              ret_w_out, pool_w, pool_scale, ffn_w_in, ffn_w_out, final_norm_w):
    n_lat = x.shape[1]
    ROWS = n_lat // GRID_W
    row = jnp.repeat(jnp.arange(ROWS), GRID_W).astype(jnp.float32)
    col = jnp.tile(jnp.arange(GRID_W), ROWS).astype(jnp.float32)
    silu_c = jax.nn.silu(c)
    silu_cc = jax.nn.silu(c_ctx)
    x_lat, x_ctx = x, ctx
    for i in range(DEPTH):
        last = i == DEPTH - 1
        use_ret = (i % N_MIXERS) == 0
        j = i // N_MIXERS
        ctx_needed = (not last) or use_ret
        sh1, sc1, g1, sh2, sc2, g2 = jnp.split((silu_c @ ada_w[i] + ada_b[i])[:, None, :], 6, axis=-1)
        h_lat = _modulate(_rmsnorm(x_lat, norm1_w[i]), sh1, sc1)
        if ctx_needed:
            csh1, csc1, cg1, csh2, csc2, cg2 = jnp.split(silu_cc @ ada_w[i] + ada_b[i], 6, axis=-1)
            h_ctx = _modulate(_rmsnorm(x_ctx, norm1_w[i]), csh1, csc1)
        if use_ret:
            y_lat, y_ctx = _retention_mixer(h_lat, h_ctx, ret_w_in[j], ret_log_decay[j], ret_gn_w[j],
                                            ret_w_out[j], row, col, not last)
        else:
            y_lat = _pool_mixer(h_lat, pool_w[j], pool_scale[j])
            y_ctx = None if last else _pool_mixer(h_ctx, pool_w[j], pool_scale[j])
        x_lat = x_lat + g1 * y_lat
        x_lat = x_lat + g2 * _swiglu(_modulate(_rmsnorm(x_lat, norm2_w[i]), sh2, sc2), ffn_w_in[i], ffn_w_out[i])
        if not last:
            x_ctx = x_ctx + cg1 * y_ctx
            x_ctx = x_ctx + cg2 * _swiglu(_modulate(_rmsnorm(x_ctx, norm2_w[i]), csh2, csc2),
                                          ffn_w_in[i], ffn_w_out[i])
    return _rmsnorm(x_lat, final_norm_w)


_drawn_inputs = setup_inputs


def setup_inputs(seed=0):
    import zlib

    import numpy as np

    out = dict(_drawn_inputs(seed))
    spreads = {}
    factors = {'ada_b': 3.194, 'norm2_w': 2.693, 'ret_gn_w': 5.393, 'pool_scale': 4.462}
    for name, (base, spread) in spreads.items():
        noise = np.random.default_rng([zlib.crc32(name.encode()), seed]).standard_normal(out[name].shape)
        drawn = base * np.exp(spread * noise) if base else spread * noise
        out[name] = __import__('jax').numpy.asarray(drawn.astype(out[name].dtype))
    for name, factor in factors.items():
        out[name] = (out[name] * factor).astype(out[name].dtype)
    return out
```

```python
from contextlib import ExitStack

import numpy as np

import concourse.bass as bass
from concourse import mybir

F32 = mybir.dt.float32
F32R = mybir.dt.float32r
ALU = mybir.AluOpType
ACT = mybir.ActivationFunctionType

P = 128
D = 1024
KD = D // P
SEQ = 1024
HALF = 512
GRID_W = 64
CTX = 256
CT = CTX // P
CHUNK = 128
NC = SEQ // CHUNK
HEADS = 4
DK = D // HEADS
DV = 2 * D // HEADS
KV = 2 * D // P
HID = 2816
IT = HID // (2 * P)
WINDOWS = (2, 4, 8, 16)
PAD = 8
EPS = 1e-6
GN_EPS = 1e-5
ADA_PIECES = 24

V_N1, V_N2, V_FIN, V_PS, V_C, V_AB = 0, 16, 32, 40, 48, 64
V_ALL = V_AB + 96
DECAYS = 10
F_Q, F_K, F_CHUNK, F_CTX, B_Q, B_K, B_CHUNK, B_CTX = 0, 1, 2, 3, 5, 6, 7, 8


class Tally:

    def __init__(self, sem, per, credit=False, unit=1):
        self.sem, self.per, self.credit, self.unit = sem, per, credit, unit

    def at(self, r, n):
        return r * (self.per * self.unit) + (n + self.per * self.credit) * self.unit


def pay(eng, *tallies):
    for t in tallies:
        eng.sem_inc(t.sem, t.per * t.unit)


def mm3(nc, out, w_hi, w_lo, x_hi, x_lo, first, last):
    nc.tensor.matmul(out, w_hi, x_hi, start=first, stop=False)
    nc.tensor.matmul(out, w_hi, x_lo, start=False, stop=False)
    return nc.tensor.matmul(out, w_lo, x_hi, start=False, stop=last)


def f32(ap):
    return ap.bitcast(F32)


def wide(ap, *dims):
    return ap.broadcast_to([P, *dims])


class Norms:

    def __init__(self, sem):
        self.squared = Tally(sem("norm_squared"), KD)
        self.summed = Tally(sem("norm_summed"), KD)
        self.total = Tally(sem("norm_total"), 1)
        self.mean = Tally(sem("norm_mean"), 1)
        self.rstd = Tally(sem("norm_rstd"), 1)
        self.diag = Tally(sem("norm_diagonal"), 1)
        self.spread = Tally(sem("norm_spread"), 1)
        self.scaled = Tally(sem("norm_scaled"), KD)
        self.hi = Tally(sem("norm_hi"), KD)
        self.lo = Tally(sem("norm_lo"), KD)
        self.ones = sem("norm_ones")
        self.ident_in = sem("norm_ident_in")

    def buffers(self, sb, name, n):
        return dict(n=n, sq=sb(f"{name}_sq", [P, 2, n]), acc=sb(f"{name}_acc", [P, n]),
                    t=sb(f"{name}_t", [P, 2, n]), ms=sb(f"{name}_ms", [P, n // P]), rs=sb(f"{name}_rs", [P, n // P]),
                    dg=sb(f"{name}_dg", [P, n]), ones=sb(f"{name}_ones", [P, P]), ident=sb(f"{name}_ident", [P, P]))

    def act_squares(self, nc, act, r, b, x):
        for k in range(KD):
            if k >= 2:
                act.wait_ge(self.summed.sem, self.summed.at(r, k - 1))
            nc.scalar.activation(b["sq"][:, k % 2, :], x[:, k, :], ACT.Square).then_inc(self.squared.sem, 1)

    def dve_sum(self, nc, dve, r, b):
        for k in range(KD):
            dve.wait_ge(self.squared.sem, self.squared.at(r, k + 1))
            if k == 0:
                nc.vector.tensor_copy(b["acc"][:, :], b["sq"][:, 0, :]).then_inc(self.summed.sem, 1)
            else:
                dve.wait_ge(self.summed.sem, self.summed.at(r, k))
                nc.vector.tensor_tensor(b["acc"][:, :], b["acc"][:, :], b["sq"][:, k % 2, :],
                                        ALU.add).then_inc(self.summed.sem, 1)

    def load(self, sp, b, ident, r):
        sp.dma_start(b["ident"][:, :], ident).then_inc(self.ident_in, 16)

    def dve_ones(self, nc, b):
        nc.vector.memset(b["ones"][:, :], 1.0).then_inc(self.ones, 1)

    def pe_total(self, nc, pe, r, b, ps):
        pe.wait_ge(self.ones, r + 1)
        pe.wait_ge(self.summed.sem, self.summed.at(r, KD))
        for j in range(b["n"] // P):
            mm = nc.tensor.matmul(ps[:, 0, j:j + 1], b["acc"][:, j * P:(j + 1) * P], b["ones"][:, 0:1],
                                  start=True, stop=True)
        mm.then_inc(self.total.sem, 1)

    def dve_mean(self, nc, dve, r, b, ps):
        dve.wait_ge(self.total.sem, self.total.at(r, 1))
        nc.vector.tensor_scalar(b["ms"][:, :], ps[:, 0, 0:b["n"] // P], 1.0 / D, EPS, ALU.mult, ALU.add
                                ).then_inc(self.mean.sem, 1)

    def pool_rstd(self, nc, pool, r, b, minus_half):
        pool.wait_ge(self.mean.sem, self.mean.at(r, 1))
        nc.gpsimd.tensor_tensor(b["rs"][:, :], b["ms"][:, :], wide(minus_half[:, 0:1], b["n"] // P),
                                ALU.pow).then_inc(self.rstd.sem, 1)

    def dve_diag(self, nc, dve, r, b):
        dve.wait_ge(self.ident_in, 16 * (r + 1))
        dve.wait_ge(self.rstd.sem, self.rstd.at(r, 1))
        n = b["n"] // P
        nc.vector.tensor_tensor(b["dg"][:, :].rearrange("p (j t) -> p j t", t=P),
                                b["ident"][:, :].unsqueeze(1).broadcast_to([P, n, P]),
                                b["rs"][:, :].unsqueeze(2).broadcast_to([P, n, P]), ALU.mult
                                ).then_inc(self.diag.sem, 1)

    def pe_spread(self, nc, pe, r, b, ps):
        pe.wait_ge(self.diag.sem, self.diag.at(r, 1))
        w = min(b["n"], HALF)
        for s in range(0, b["n"], w):
            mm = nc.tensor.matmul(ps[:, s // HALF, 0:w], b["ones"][:, :], b["dg"][:, s:s + w], start=True, stop=True)
        mm.then_inc(self.spread.sem, 1)

    def rstd_of(self, b, ps):
        return ps[:, 0, 0:b["n"]] if b["n"] <= HALF else ps[:, 0:2, :].rearrange("p s n -> p (s n)")

    def dve_scale(self, nc, dve, r, b, ps, x, gain, shift, lo, hi):
        dve.wait_ge(self.spread.sem, self.spread.at(r, 1))
        lr = r - (r > 3)
        for k in range(KD + 1):
            if k < KD:
                if k >= 2:
                    dve.wait_ge(self.hi.sem, self.hi.at(r, k - 1))
                    if lo is not None:
                        dve.wait_ge(self.lo.sem, self.lo.at(lr, k - 1))
                nc.vector.scalar_tensor_tensor(b["t"][:, k % 2, :], x[:, k, :], gain[:, k:k + 1],
                                               self.rstd_of(b, ps),
                                               ALU.mult, ALU.mult).then_inc(self.scaled.sem, 1)
            if k and lo is not None:
                dve.wait_ge(self.scaled.sem, self.scaled.at(r, k))
                dve.wait_ge(self.hi.sem, self.hi.at(r, k))
                nc.vector.scalar_tensor_tensor(lo[:, k - 1, :], b["t"][:, (k - 1) % 2, :], shift(k - 1),
                                               f32(hi[:, k - 1, :]), ALU.add, ALU.subtract).then_inc(self.lo.sem, 1)

    def act_shift(self, nc, act, r, b, shift, out):
        for k in range(KD):
            act.wait_ge(self.scaled.sem, self.scaled.at(r, k + 1))
            nc.scalar.activation(out(k), b["t"][:, k % 2, :], ACT.Identity, bias=shift(k)).then_inc(self.hi.sem, 1)


def build(nc, a, out):
    with ExitStack() as whole:
        build_phases(nc, a, out, whole)


def build_phases(nc, a, out, whole):
    def sem(name):
        return whole.enter_context(nc.semaphore(name))

    def scope_sb(stack):
        return lambda name, shape, dt=F32: stack.enter_context(nc.sbuf_tensor(name, shape, dt))

    keep = scope_sb(whole)
    ps = whole.enter_context(nc.psum_tensor("ps", [P, 8, HALF], F32))
    vecs = keep("vecs", [P, V_ALL])
    mod = keep("mod", [P, 96, 2])
    gain = keep("gain", [P, 6, KD])
    gps = keep("gps", [P, KD])
    minus_half = keep("minus_half", [P, 1])

    def part(layer, n, ctx=0):
        return lambda k: mod[:, layer * 48 + n * 8 + k, ctx:ctx + 1]

    s0_dram = nc.dram_tensor("s0_dram", [HEADS, 2, P, 2 * DV], F32, kind="Internal").ap()
    head_dram = nc.dram_tensor("head_dram", [HEADS, P, DECAYS + P], F32, kind="Internal").ap()
    y_dram = nc.dram_tensor("y_dram", [NC, P, HEADS * DV], F32, kind="Internal").ap()

    norms = Norms(sem)
    with ExitStack() as first:
        sb1 = scope_sb(first)
        hh = sb1("hh", [P, KD, SEQ], F32R)
        hl = sb1("hl", [P, KD, SEQ], F32R)
        with ExitStack() as second:
            sb2 = scope_sb(second)
            ch = sb2("ch", [P, KD, CTX], F32R)
            cl = sb2("cl", [P, KD, CTX], F32R)
            phase_conditioning(nc, a, sem, scope_sb, ps, norms, vecs, mod, gain, gps, minus_half, part,
                               hh, hl, ch, cl, head_dram)
            phase_context_states(nc, a, sem, scope_sb, ps, ch, cl, head_dram, s0_dram)
        phase_retention(nc, a, sem, scope_sb, ps, minus_half, hh, hl, s0_dram, head_dram, y_dram)
    x = keep("x", [P, KD, SEQ])
    phase_retention_out(nc, a, sem, scope_sb, ps, part, x, y_dram)
    ffn = Ffn(sem, keep)
    phase_ffn(nc, a, scope_sb, ps, norms, ffn, 0, part, gain, minus_half, x)
    phase_pool(nc, a, sem, scope_sb, ps, norms, part, gain, gps, minus_half, x)
    phase_ffn(nc, a, scope_sb, ps, norms, ffn, 1, part, gain, minus_half, x)
    phase_final(nc, a, sem, scope_sb, ps, norms, vecs, minus_half, x, out)


def phase_conditioning(nc, a, sem, scope_sb, ps, norms, vecs, mod, gain, gps, minus_half, part,
                       hh, hl, ch, cl, head_dram):
    with ExitStack() as st:
        sb = scope_sb(st)
        xT = sb("xT", [P, KD, SEQ])
        cT = sb("cT", [P, KD, CTX])
        nb = norms.buffers(sb, "n0", SEQ)
        nbc = norms.buffers(sb, "nc", CTX)
        ada = sb("ada", [P, 2, KD, 2 * P])
        cs = sb("cs", [P, KD, 2])
        expo = sb("expo", [P, 10])
        dist = sb("dist", [P, 2, P])
        lg = sb("lg", [P, 2 * HEADS])
        arg = sb("arg", [P, HEADS, P])
        heads = sb("heads", [P, HEADS, DECAYS + P])

        small_in, x_in, ctx_in = sem("small_in"), sem("x_in"), sem("ctx_in")
        ada_in = [Tally(sem(f"ada_in{q}"), 1, unit=16) for q in range(2)]
        ada_mm = Tally(sem("ada_mm"), 2, credit=True)
        ada_out = Tally(sem("ada_out"), 2, credit=True)
        ready = sem("consts_ready")
        c_silu = sem("c_silu")
        decay_step = sem("decay_step")
        decays, arg_done, mask_done, mask_out = sem("decays"), sem("arg_done"), sem("mask_done"), sem("mask_out")
        gains = sem("gains")
        PIECES = 2 * ADA_PIECES

        with nc.Block() as block:
            @block.sync
            def _(sp):
                pay(sp, ada_mm, ada_out)
                sp.dma_start(vecs[:, :], a["vecs"]).then_inc(small_in, 16)
                sp.dma_start(lg[:, :], a["log_decay"].partition_broadcast(P)).then_inc(small_in, 16)
                sp.dma_start(expo[:, :], a["expo"]).then_inc(small_in, 16)
                sp.dma_start(dist[:, :, :], a["dist"]).then_inc(small_in, 16)
                norms.load(sp, nbc, a["ident"], 0)
                norms.load(sp, nb, a["ident"], 1)
                sp.dma_start(cT[:, :, :], a["ctxT"]).then_inc(ctx_in, 16)
                sp.dma_start(xT[:, :, :], a["xT"]).then_inc(x_in, 16)
                with sp.Fori(0, PIECES // 2) as i:
                    for q in range(2):
                        sp.wait_ge(ada_mm.sem, ada_mm.at(i, q - 1))
                        sp.dma_start(ada[:, q, :, :], a["ada"][bass.ds(i * 2 + q, 1)]
                                     .rearrange("o p k n -> p (o k) n")).then_inc(ada_in[q].sem, 16)
                sp.wait_ge(mask_out, 16)

            @block.scalar
            def _(act):
                act.wait_ge(ready, 1)
                act.wait_ge(decays, 1)
                for h in range(HEADS):
                    for d, (e0, e1) in enumerate(((0, 5), (5, 10))):
                        nc.scalar.activation(heads[:, h, e0:e1], expo[:, e0:e1], ACT.Exp,
                                             scale=lg[:, d * HEADS + h:d * HEADS + h + 1]).then_inc(decay_step, 1)
                act.wait_ge(arg_done, HEADS)
                nc.scalar.activation(heads[:, :, DECAYS:], arg[:, :, :], ACT.Exp).then_inc(mask_done, 1)
                act.wait_ge(mask_done, 1)
                act.wait_ge(decay_step, 2 * HEADS)
                act.dma_start(head_dram.rearrange("h p n -> p h n"), heads[:, :, :]).then_inc(mask_out, 16)
                nc.scalar.activation(cs[:, :, :].rearrange("p k c -> p (k c)"), vecs[:, V_C:V_C + 16],
                                     ACT.Silu).then_inc(c_silu, 1)
                act.wait_ge(ctx_in, 16)
                norms.act_squares(nc, act, 0, nbc, cT)
                act.wait_ge(x_in, 16)
                norms.act_squares(nc, act, 1, nb, xT)
                norms.act_shift(nc, act, 0, nbc, part(0, 0, 1), lambda k: ch[:, k, :])
                norms.act_shift(nc, act, 1, nb, part(0, 0), lambda k: hh[:, k, :])

            @block.vector
            def _(dve):
                norms.dve_ones(nc, nbc)
                norms.dve_ones(nc, nb)
                nc.vector.memset(minus_half[:, :], -0.5).then_inc(ready, 1)
                dve.wait_ge(small_in, 64)
                neg = sem("log_decay_negated")
                nc.vector.tensor_scalar(arg[:, 0, 0:8], lg[:, :], -1.0, None, ALU.mult).then_inc(neg, 1)
                dve.wait_ge(neg, 1)
                nc.vector.tensor_tensor(lg[:, :], lg[:, :], arg[:, 0, 0:8], ALU.min).then_inc(decays, 1)
                dve.wait_ge(decays, 1)
                back = sem("backward_exponent")
                for h in range(HEADS):
                    nc.vector.tensor_scalar(arg[:, h, :], dist[:, 1, :], lg[:, HEADS + h:HEADS + h + 1], None,
                                            ALU.mult).then_inc(back, 1)
                for h in range(HEADS):
                    dve.wait_ge(back, h + 1)
                    nc.vector.scalar_tensor_tensor(arg[:, h, :], dist[:, 0, :], lg[:, h:h + 1], arg[:, h, :],
                                                   ALU.mult, ALU.add).then_inc(arg_done, 1)
                norms.dve_sum(nc, dve, 0, nbc)
                norms.dve_sum(nc, dve, 1, nb)
                norms.dve_mean(nc, dve, 0, nbc, ps[:, 4:6, :])
                norms.dve_mean(nc, dve, 1, nb, ps[:, 6:8, :])
                norms.dve_diag(nc, dve, 0, nbc)
                norms.dve_diag(nc, dve, 1, nb)
                with dve.Fori(0, PIECES // 2) as i:
                    for q in range(2):
                        dve.wait_ge(ada_mm.sem, ada_mm.at(i, q + 1))
                        nc.vector.tensor_tensor(
                            mod[:, bass.ds(i * 4 + 2 * q, 2), :],
                            ps[:, q, 0:4].rearrange("p (j c) -> p j c", c=2),
                            vecs[:, bass.ds(i * 4 + (V_AB + 2 * q), 2)].unsqueeze(2).broadcast_to([P, 2, 2]),
                            ALU.add).then_inc(ada_out.sem, 1)
                dve.wait_ge(ada_out.sem, ada_out.at(PIECES // 2 - 1, 2))
                for n, (w, layer, p, c) in enumerate(((V_N1, 0, 1, 0), (V_N2, 0, 4, 0), (V_N1 + 8, 1, 1, 0),
                                                      (V_N2 + 8, 1, 4, 0), (V_N1, 0, 1, 1))):
                    nc.vector.scalar_tensor_tensor(gain[:, n, :], mod[:, layer * 48 + p * 8:layer * 48 + p * 8 + 8, c],
                                                   1.0, vecs[:, w:w + 8], ALU.add, ALU.mult).then_inc(gains, 1)
                nc.vector.tensor_tensor(gps[:, :], mod[:, 48 + 16:48 + 24, 0], vecs[:, V_PS:V_PS + 8],
                                        ALU.mult).then_inc(gains, 1)
                dve.wait_ge(gains, 6)
                norms.dve_scale(nc, dve, 0, nbc, ps[:, 4:6, :], cT, gain[:, 4, :], part(0, 0, 1), cl, ch)
                norms.dve_scale(nc, dve, 1, nb, ps[:, 6:8, :], xT, gain[:, 0, :], part(0, 0), hl, hh)

            @block.tensor
            def _(pe):
                pe.wait_ge(ready, 1)
                norms.pe_total(nc, pe, 0, nbc, ps[:, 4:6, :])
                norms.pe_total(nc, pe, 1, nb, ps[:, 6:8, :])
                norms.pe_spread(nc, pe, 0, nbc, ps[:, 4:6, :])
                norms.pe_spread(nc, pe, 1, nb, ps[:, 6:8, :])
                pe.wait_ge(c_silu, 1)
                with pe.Fori(0, PIECES // 2) as i:
                    for q in range(2):
                        pe.wait_ge(ada_in[q].sem, ada_in[q].at(i, 1))
                        pe.wait_ge(ada_out.sem, ada_out.at(i, q - 1))
                        for j in range(2):
                            for k in range(KD):
                                mm = nc.tensor.matmul(ps[:, q, 2 * j:2 * j + 2], ada[:, q, k, j * P:(j + 1) * P],
                                                      cs[:, k, :], start=k == 0, stop=k == KD - 1)
                        mm.then_inc(ada_mm.sem, 1)

            @block.gpsimd
            def _(pool):
                pool.wait_ge(ready, 1)
                norms.pool_rstd(nc, pool, 0, nbc, minus_half)
                norms.pool_rstd(nc, pool, 1, nb, minus_half)


def phase_context_states(nc, a, sem, scope_sb, ps, ch, cl, head_dram, s0_dram):
    with ExitStack() as st:
        sb = scope_sb(st)
        WK = DK + DV
        RAW = 4
        raw = sb("raw1", [P, RAW, WK])
        wh = sb("wh1", [P, KD, WK], F32R)
        wl = sb("wl1", [P, KD, WK], F32R)
        vh = sb("vh1", [P, CT, DV], F32R)
        vl = sb("vl1", [P, CT, DV], F32R)
        kh = sb("kh1", [P, 2, CT, DK], F32R)
        kl = sb("kl1", [P, 2, CT, DK], F32R)
        s0 = sb("s0", [P, 2, 2 * DV])
        hd = sb("hd1", [P, DECAYS])

        raw_in = [Tally(sem(f"ctx_raw_in{q}"), 2, unit=32) for q in range(RAW)]
        hd_in = Tally(sem("ctx_decays_in"), 1, unit=16)
        w_hi = Tally(sem("ctx_w_hi"), KD)
        w_lo = Tally(sem("ctx_w_lo"), KD, credit=True)
        proj = Tally(sem("ctx_proj"), CT, credit=True)
        hi = Tally(sem("ctx_kv_hi"), 3 * CT)
        lo = Tally(sem("ctx_kv_lo"), 3 * CT, credit=True)
        states = Tally(sem("ctx_states"), 2, credit=True)
        copied = [Tally(sem(f"ctx_copied{d}"), 1, credit=True) for d in range(2)]
        stored = [Tally(sem(f"ctx_stored{d}"), 1, credit=True, unit=16) for d in range(2)]

        with nc.Block() as block:
            @block.sync
            def _(sp):
                pay(sp, w_lo, proj, lo, states, *copied, *stored)
                with sp.Fori(0, HEADS) as h:
                    for k in range(KD):
                        sp.wait_ge(w_lo.sem, w_lo.at(h, k + 1 - RAW))
                        sp.dma_start(raw[:, k % RAW, 0:DK], a["ret_w"][bass.ds(h * 3, 1), k, :, DK:2 * DK]
                                     .rearrange("o p n -> (o p) n")).then_inc(raw_in[k % RAW].sem, 16)
                        sp.dma_start(raw[:, k % RAW, DK:WK], a["ret_w"][bass.ds(h * 3 + 1, 1), k, :, :]
                                     .rearrange("o p n -> (o p) n")).then_inc(raw_in[k % RAW].sem, 16)
                        if k == RAW - 1:
                            sp.wait_ge(lo.sem, lo.at(h, 0))
                            sp.dma_start(hd[:, :], head_dram[bass.ds(h, 1), :, 0:DECAYS]
                                         .rearrange("o p n -> (o p) n")).then_inc(hd_in.sem, 16)

            @block.gpsimd
            def _(pool):
                with pool.Fori(0, HEADS) as h:
                    for k in range(KD):
                        pool.wait_ge(w_hi.sem, w_hi.at(h, k + 1))
                        nc.gpsimd.tensor_tensor(wl[:, k, :], raw[:, k % RAW, :], f32(wh[:, k, :]),
                                                ALU.subtract).then_inc(w_lo.sem, 1)

            @block.scalar
            def _(act):
                with act.Fori(0, HEADS) as h:
                    act.wait_ge(proj.sem, proj.at(h, 0))
                    for k in range(KD):
                        act.wait_ge(raw_in[k % RAW].sem, raw_in[k % RAW].at(h, k // RAW + 1))
                        nc.scalar.activation(wh[:, k, :], raw[:, k % RAW, :], ACT.Copy).then_inc(w_hi.sem, 1)
                    act.wait_ge(states.sem, states.at(h, 0))
                    act.wait_ge(hd_in.sem, hd_in.at(h, 1))
                    for t in range(CT):
                        act.wait_ge(proj.sem, proj.at(h, t + 1))
                        nc.scalar.activation(vh[:, t, :], ps[:, 2 + t, :], ACT.Copy).then_inc(hi.sem, 1)
                        for d, e in enumerate((F_CTX, B_CTX)):
                            nc.scalar.activation(kh[:, d, t, :], ps[:, t, 0:DK], ACT.Copy,
                                                 scale=hd[:, e + t:e + t + 1]).then_inc(hi.sem, 1)
                    act.wait_ge(stored[0].sem, stored[0].at(h, 0))
                    act.wait_ge(states.sem, states.at(h, 1))
                    nc.scalar.activation(s0[:, 0, :], ps[:, 4:6, :].rearrange("p t n -> p (t n)"),
                                         ACT.Copy).then_inc(copied[0].sem, 1)
                    for d in range(2):
                        act.wait_ge(copied[d].sem, copied[d].at(h, 1))
                        act.dma_start(s0_dram[bass.ds(h, 1), d].rearrange("o p n -> (o p) n"),
                                      s0[:, d, :]).then_inc(stored[d].sem, 16)
                for d in range(2):
                    act.wait_ge(stored[d].sem, stored[d].at(HEADS - 1, 1))

            @block.vector
            def _(dve):
                with dve.Fori(0, HEADS) as h:
                    for t in range(CT):
                        dve.wait_ge(hi.sem, hi.at(h, 3 * t + 1))
                        nc.vector.tensor_tensor(vl[:, t, :], ps[:, 2 + t, :], f32(vh[:, t, :]),
                                                ALU.subtract).then_inc(lo.sem, 1)
                        dve.wait_ge(hi.sem, hi.at(h, 3 * t + 3))
                        for d, e in enumerate((F_CTX, B_CTX)):
                            nc.vector.scalar_tensor_tensor(kl[:, d, t, :], ps[:, t, 0:DK], hd[:, e + t:e + t + 1],
                                                           f32(kh[:, d, t, :]), ALU.mult,
                                                           ALU.subtract).then_inc(lo.sem, 1)
                    dve.wait_ge(stored[1].sem, stored[1].at(h, 0))
                    dve.wait_ge(states.sem, states.at(h, 2))
                    nc.vector.tensor_copy(s0[:, 1, :], ps[:, 6:8, :].rearrange("p t n -> p (t n)")
                                          ).then_inc(copied[1].sem, 1)

            @block.tensor
            def _(pe):
                with pe.Fori(0, HEADS) as h:
                    for t in range(CT):
                        if t == 0:
                            pe.wait_ge(lo.sem, lo.at(h, 0))
                        tok = slice(t * P, (t + 1) * P)
                        for k in range(KD):
                            if t == 0:
                                pe.wait_ge(w_lo.sem, w_lo.at(h, k + 1))
                            mm3(nc, ps[:, t, 0:DK], ch[:, k, tok], cl[:, k, tok], wh[:, k, 0:DK], wl[:, k, 0:DK],
                                k == 0, k == KD - 1)
                            mm = mm3(nc, ps[:, 2 + t, :], ch[:, k, tok], cl[:, k, tok], wh[:, k, DK:WK],
                                     wl[:, k, DK:WK], k == 0, k == KD - 1)
                        mm.then_inc(proj.sem, 1)
                    pe.wait_ge(lo.sem, lo.at(h, 3 * CT))
                    for d in range(2):
                        pe.wait_ge(copied[d].sem, copied[d].at(h, 0))
                        for dt in range(2):
                            for t in range(CT):
                                cols = slice(dt * P, (dt + 1) * P)
                                mm = mm3(nc, ps[:, 4 + 2 * d + dt, :], kh[:, d, t, cols], kl[:, d, t, cols],
                                         vh[:, t, :], vl[:, t, :], t == 0, t == CT - 1)
                        mm.then_inc(states.sem, 1)


def phase_retention(nc, a, sem, scope_sb, ps, minus_half, hh, hl, s0_dram, head_dram, y_dram):
    with ExitStack() as st:
        sb = scope_sb(st)
        RAW = 4
        BLOCKS = 3
        raw = sb("raw2", [P, RAW, DV])
        wh = sb("wh2", [P, KD, DV], F32R)
        wl = sb("wl2", [P, KD, DV], F32R)
        qTh = sb("qTh", [P, 2, SEQ], F32R)
        qTl = sb("qTl", [P, 2, SEQ], F32R)
        kn = sb("kn", [P, NC, DK])
        vh = sb("vh2", [P, NC, DV], F32R)
        vl = sb("vl2", [P, NC, DV], F32R)
        y = sb("y", [P, NC, DV])
        S = sb("S", [P, 2, DV])
        Sh = sb("Sh", [P, 2, DV], F32R)
        Sl = sb("Sl", [P, 2, DV], F32R)
        kdh = sb("kdh", [P, DK], F32R)
        kdl = sb("kdl", [P, DK], F32R)
        cosr, sinr = sb("cosr", [P, NC, 64]), sb("sinr", [P, NC, 64])
        cosc, sinc = sb("cosc", [P, 64]), sb("sinc", [P, 64])
        ident = sb("ident2", [P, P])
        hd = sb("hd2", [P, DECAYS + P])
        gn = sb("gn", [P, DV])
        t1 = sb("t1", [P, DV])
        t2 = sb("t2", [P, DV])
        kTh = sb("kTh", [P, 2, P], F32R)
        kTl = sb("kTl", [P, 2, P], F32R)
        pf = sb("pf", [P, P])
        ph = sb("ph", [P, P], F32R)
        pl = sb("pl", [P, P], F32R)
        stats = sb("stats", [P, 6])
        mv = sb("mv", [P, 2])
        ve = sb("ve", [P, 1])
        rstd = sb("rstd", [P, 1])
        warm = sb("warm2", [P, 1])
        PT, SC, PV, QS, U = 2, 3, 4, 5, 6

        const_in = sem("ret_const_in")
        raw_in = [Tally(sem(f"ret_raw_in{q}"), BLOCKS * KD // RAW, unit=16) for q in range(RAW)]
        w_hi = Tally(sem("ret_w_hi"), BLOCKS * KD)
        w_lo = Tally(sem("ret_w_lo"), BLOCKS * KD, credit=True)
        w_used = Tally(sem("ret_w_used"), BLOCKS * (KD - 1), credit=True)
        proj = Tally(sem("ret_proj"), BLOCKS * NC, credit=True)
        hd_in = Tally(sem("ret_head_in"), 1, unit=16)
        gn_in = Tally(sem("ret_gn_in"), 1, unit=16)
        s_in = Tally(sem("ret_state_in"), 2, unit=16)
        rope_cos = Tally(sem("rope_cos"), 2 * NC)
        rope_sin = Tally(sem("rope_sin"), 2 * NC)
        rope_out = Tally(sem("rope_out"), 4 * NC)
        qT_mm = Tally(sem("qT_mm"), NC, credit=True)
        qT_hi = Tally(sem("qT_hi"), NC, credit=True)
        qT_lo = Tally(sem("qT_lo"), NC, credit=True)
        kT_mm = Tally(sem("kT_mm"), NC, credit=True)
        kT_hi = Tally(sem("kT_hi"), NC)
        kT_lo = Tally(sem("kT_lo"), NC, credit=True)
        kd_hi = Tally(sem("kd_hi"), 2 * (NC - 1))
        kd_lo = Tally(sem("kd_lo"), 2 * (NC - 1), credit=True)
        v_hi = Tally(sem("v_hi"), NC)
        v_lo = Tally(sem("v_lo"), NC)
        score_mm = Tally(sem("score_mm"), NC)
        p_f = Tally(sem("p_masked"), NC, credit=True)
        p_hi = Tally(sem("p_hi"), NC)
        p_lo = Tally(sem("p_lo"), NC, credit=True)
        qs_mm = Tally(sem("qs_mm"), 2 * NC, credit=True)
        pv_mm = Tally(sem("pv_mm"), NC, credit=True)
        y_pv = Tally(sem("y_pv"), NC, credit=True)
        y_f = Tally(sem("y_forward"), NC, credit=True)
        y_b = Tally(sem("y_backward"), NC, credit=True)
        u_mm = Tally(sem("u_mm"), 2 * (NC - 1), credit=True)
        s_f32 = Tally(sem("s_updated"), 2 * (NC - 1), credit=True)
        s_hi = Tally(sem("s_hi"), 2 * NC, credit=True)
        s_lo = Tally(sem("s_lo"), 2 * NC, credit=True)
        silu = Tally(sem("g_silu"), NC, credit=True)
        gated = Tally(sem("g_weighted"), NC, credit=True)
        st_done = Tally(sem("y_stats"), NC)
        ag_done = Tally(sem("y_mean_var"), NC)
        ve_done = Tally(sem("y_var_eps"), NC)
        rs_done = Tally(sem("y_rstd"), NC)
        yn_done = Tally(sem("y_normed"), NC, credit=True)
        yg_done = Tally(sem("y_gated"), NC, credit=True)
        stored = Tally(sem("y_stored"), NC, credit=True, unit=16)

        def order(d):
            return list(range(NC)) if d == 0 else list(range(NC - 1, -1, -1))

        def load_slice(sp, h, b, k):
            n = b * KD + k
            sp.wait_ge(w_lo.sem, w_lo.at(h, n + 1 - RAW))
            sp.dma_start(raw[:, k % RAW, :], a["ret_w"][bass.ds(h * BLOCKS + b, 1), k, :, :]
                         .rearrange("o p n -> (o p) n")).then_inc(raw_in[k % RAW].sem, 16)

        with nc.Block() as block:
            @block.sync
            def _(sp):
                pay(sp, w_lo, w_used, proj, qT_mm, qT_hi, qT_lo, kT_mm, kT_lo, kd_lo, p_f, p_lo,
                    qs_mm, pv_mm, y_pv, y_f, y_b, u_mm, s_f32, s_hi, s_lo, silu, gated, yn_done, yg_done, stored)
                for dst, name in ((cosr[:, :, :], "cosr"), (sinr[:, :, :], "sinr"), (cosc[:, :], "cosc"),
                                  (sinc[:, :], "sinc"), (ident[:, :], "ident")):
                    sp.dma_start(dst, a[name]).then_inc(const_in, 16)
                with sp.Fori(0, HEADS) as h:
                    for k in range(KD):
                        load_slice(sp, h, 0, k)
                    sp.wait_ge(y_b.sem, y_b.at(h, 0))
                    sp.dma_start(hd[:, :], head_dram[bass.ds(h, 1)].rearrange("o p n -> (o p) n")
                                 ).then_inc(hd_in.sem, 16)
                    sp.wait_ge(s_lo.sem, s_lo.at(h, 0))
                    sp.dma_start(S[:, :, :].rearrange("p t n -> p (t n)"), s0_dram[bass.ds(h, 1), 0]
                                 .rearrange("o p n -> (o p) n")).then_inc(s_in.sem, 16)
                    sp.wait_ge(gated.sem, gated.at(h, 0))
                    sp.dma_start(gn[:, :], a["gn"][bass.ds(h, 1)].rearrange("o p n -> (o p) n")
                                 ).then_inc(gn_in.sem, 16)
                    for b in (1, 2):
                        for k in range(KD):
                            load_slice(sp, h, b, k)
                    sp.wait_ge(s_lo.sem, s_lo.at(h, NC))
                    sp.dma_start(S[:, :, :].rearrange("p t n -> p (t n)"), s0_dram[bass.ds(h, 1), 1]
                                 .rearrange("o p n -> (o p) n")).then_inc(s_in.sem, 16)

            def split_hi(act, h, b):
                for k in range(KD):
                    n = b * KD + k
                    if k < KD - 1:
                        act.wait_ge(w_used.sem, w_used.at(h, (b - 1) * (KD - 1) + k + 1))
                    else:
                        act.wait_ge(proj.sem, proj.at(h, b * NC))
                    act.wait_ge(raw_in[k % RAW].sem, raw_in[k % RAW].at(h, n // RAW + 1))
                    nc.scalar.activation(wh[:, k, :], raw[:, k % RAW, :], ACT.Copy).then_inc(w_hi.sem, 1)

            def split_lo(pool, h, b):
                for k in range(KD):
                    pool.wait_ge(w_hi.sem, w_hi.at(h, b * KD + k + 1))
                    nc.gpsimd.tensor_tensor(wl[:, k, :], raw[:, k % RAW, :], f32(wh[:, k, :]),
                                            ALU.subtract).then_inc(w_lo.sem, 1)

            @block.gpsimd
            def _(pool):
                with pool.Fori(0, HEADS) as h:
                    for b in range(BLOCKS):
                        split_lo(pool, h, b)
                    for m, c in enumerate(order(1)):
                        if m == 0:
                            pool.wait_ge(gn_in.sem, gn_in.at(h, 1))
                        pool.wait_ge(silu.sem, silu.at(h, m + 1))
                        nc.gpsimd.tensor_tensor(t1[:, :], t1[:, :], gn[:, :], ALU.mult).then_inc(gated.sem, 1)
                        pool.wait_ge(ve_done.sem, ve_done.at(h, m + 1))
                        nc.gpsimd.tensor_tensor(rstd[:, :], ve[:, :], minus_half[:, :],
                                                ALU.pow).then_inc(rs_done.sem, 1)

            @block.scalar
            def _(act):
                act.wait_ge(const_in, 16 * 5)
                nc.scalar.activation(warm[:, :], minus_half[:, :], ACT.Silu)

                def split_state(h, d, m):
                    if m == 0:
                        act.wait_ge(s_in.sem, s_in.at(h, d + 1))
                    else:
                        act.wait_ge(s_f32.sem, s_f32.at(h, d * (NC - 1) + m))
                    act.wait_ge(qs_mm.sem, qs_mm.at(h, d * NC + m))
                    nc.scalar.activation(Sh[:, :, :], S[:, :, :], ACT.Copy).then_inc(s_hi.sem, 1)

                def decay_keys(h, d, m, c):
                    n = d * (NC - 1) + m
                    act.wait_ge(u_mm.sem, u_mm.at(h, n))
                    act.wait_ge(rope_out.sem, rope_out.at(h, 4 * (c + 1)))
                    e = F_K if d == 0 else B_K
                    nc.scalar.activation(kdh[:, :], kn[:, c, :], ACT.Copy,
                                         scale=hd[:, e:e + 1]).then_inc(kd_hi.sem, 1)

                with act.Fori(0, HEADS) as h:
                    split_hi(act, h, 0)
                    for c in range(NC):
                        if c == NC - 1:
                            split_hi(act, h, 1)
                        if c >= 1:
                            act.wait_ge(qT_mm.sem, qT_mm.at(h, c))
                            nc.scalar.activation(qTh[:, :, (c - 1) * P:c * P],
                                                 ps[:, PT, 0:DK].rearrange("p (t n) -> p t n", t=2),
                                                 ACT.Copy, scale=DK ** -0.5).then_inc(qT_hi.sem, 1)
                    act.wait_ge(hd_in.sem, hd_in.at(h, 1))
                    split_state(h, 0, 0)
                    for c in range(NC):
                        if c == NC - 1:
                            split_hi(act, h, 2)
                        if c < NC - 1:
                            decay_keys(h, 0, c, c)
                        act.wait_ge(proj.sem, proj.at(h, NC + c + 1))
                        nc.scalar.activation(vh[:, c, :], ps[:, (NC + c) % 2, :], ACT.Copy).then_inc(v_hi.sem, 1)
                        if c == 0:
                            act.wait_ge(qT_mm.sem, qT_mm.at(h, NC))
                            nc.scalar.activation(qTh[:, :, (NC - 1) * P:NC * P],
                                                 ps[:, PT, 0:DK].rearrange("p (t n) -> p t n", t=2),
                                                 ACT.Copy, scale=DK ** -0.5).then_inc(qT_hi.sem, 1)
                        act.wait_ge(kT_mm.sem, kT_mm.at(h, c + 1))
                        nc.scalar.activation(kTh[:, :, :], ps[:, PT, 0:DK].rearrange("p (t n) -> p t n", t=2),
                                             ACT.Copy).then_inc(kT_hi.sem, 1)
                        act.wait_ge(p_f.sem, p_f.at(h, c + 1))
                        nc.scalar.activation(ph[:, :], pf[:, :], ACT.Copy).then_inc(p_hi.sem, 1)
                        act.wait_ge(pv_mm.sem, pv_mm.at(h, c + 1))
                        nc.scalar.activation(y[:, c, :], ps[:, PV, :], ACT.Copy).then_inc(y_pv.sem, 1)
                        if c < NC - 1:
                            split_state(h, 0, c + 1)
                    split_state(h, 1, 0)
                    for m, c in enumerate(order(1)):
                        if m < NC - 1:
                            decay_keys(h, 1, m, c)
                        act.wait_ge(proj.sem, proj.at(h, 2 * NC + m + 1))
                        act.wait_ge(yg_done.sem, yg_done.at(h, m))
                        nc.scalar.activation(t1[:, :], ps[:, m % 2, :], ACT.Silu).then_inc(silu.sem, 1)
                        if m >= 1:
                            act.dma_start(y_dram[c + 1, :, bass.ds(h * DV, DV)], t2[:, :]).then_inc(stored.sem, 16)
                        if m < NC - 1:
                            split_state(h, 1, m + 1)
                    act.wait_ge(yg_done.sem, yg_done.at(h, NC))
                    act.dma_start(y_dram[0, :, bass.ds(h * DV, DV)], t2[:, :]).then_inc(stored.sem, 16)
                act.wait_ge(stored.sem, stored.at(HEADS - 1, NC))

            @block.vector
            def _(dve):
                def state_lo(h, d, m):
                    dve.wait_ge(s_hi.sem, s_hi.at(h, d * NC + m + 1))
                    nc.vector.tensor_tensor(Sl[:, :, :], S[:, :, :], f32(Sh[:, :, :]), ALU.subtract
                                            ).then_inc(s_lo.sem, 1)

                def keys_lo(h, d, m, c):
                    n = d * (NC - 1) + m
                    dve.wait_ge(kd_hi.sem, kd_hi.at(h, n + 1))
                    e = F_K if d == 0 else B_K
                    nc.vector.scalar_tensor_tensor(kdl[:, :], kn[:, c, :], hd[:, e:e + 1], f32(kdh[:, :]),
                                                   ALU.mult, ALU.subtract).then_inc(kd_lo.sem, 1)

                def update(h, d, m):
                    n = d * (NC - 1) + m
                    dve.wait_ge(s_lo.sem, s_lo.at(h, d * NC + m + 1))
                    dve.wait_ge(u_mm.sem, u_mm.at(h, n + 1))
                    e = F_CHUNK if d == 0 else B_CHUNK
                    nc.vector.scalar_tensor_tensor(S[:, :, :], S[:, :, :], hd[:, e:e + 1], ps[:, U:U + 2, :],
                                                   ALU.mult, ALU.add).then_inc(s_f32.sem, 1)

                def qT_lo_half(h, c):
                    dve.wait_ge(qT_hi.sem, qT_hi.at(h, c + 1))
                    nc.vector.scalar_tensor_tensor(qTl[:, :, c * P:(c + 1) * P],
                                                   ps[:, PT, 0:DK].rearrange("p (t n) -> p t n", t=2), DK ** -0.5,
                                                   f32(qTh[:, :, c * P:(c + 1) * P]), ALU.mult,
                                                   ALU.subtract).then_inc(qT_lo.sem, 1)

                dve.wait_ge(const_in, 16 * 5)
                with dve.Fori(0, HEADS) as h:
                    for c in range(NC):
                        dve.wait_ge(proj.sem, proj.at(h, c + 1))
                        if c == 0:
                            dve.wait_ge(stored.sem, stored.at(h, 0))
                        else:
                            dve.wait_ge(qT_mm.sem, qT_mm.at(h, c))
                            dve.wait_ge(rope_out.sem, rope_out.at(h, 4 * c))
                        src = ps[:, c % 2, :].rearrange("p (s f x n) -> p s f x n", s=2, f=2, x=2)
                        v1 = t1[:, :].rearrange("p (s f x n) -> p s f x n", s=2, f=2, x=2)
                        v2 = t2[:, :].rearrange("p (s f x n) -> p s f x n", s=2, f=2, x=2)
                        for f, (co, si) in enumerate(((cosr[:, c, :], sinr[:, c, :]), (cosc[:, :], sinc[:, :]))):
                            rep = lambda ap: ap.unsqueeze(1).unsqueeze(1).broadcast_to([P, 2, 2, 64])
                            nc.vector.tensor_tensor(v1[:, :, f], src[:, :, f], rep(co),
                                                    ALU.mult).then_inc(rope_cos.sem, 1)
                            nc.vector.tensor_tensor(v2[:, :, f], src[:, :, f, ::-1, :], rep(si),
                                                    ALU.mult).then_inc(rope_sin.sem, 1)
                        dve.wait_ge(rope_cos.sem, rope_cos.at(h, 2 * c + 2))
                        dve.wait_ge(rope_sin.sem, rope_sin.at(h, 2 * c + 2))
                        kout = kn[:, c, :].rearrange("p (f x n) -> p f x n", f=2, x=2)
                        for s, dst in enumerate((v1[:, 0], kout)):
                            for x, op in enumerate((ALU.subtract, ALU.add)):
                                nc.vector.tensor_tensor(dst[:, :, x], v1[:, s, :, x], v2[:, s, :, x],
                                                               op).then_inc(rope_out.sem, 1)
                        if c >= 1:
                            qT_lo_half(h, c - 1)
                    dve.wait_ge(hd_in.sem, hd_in.at(h, 1))
                    state_lo(h, 0, 0)
                    for c in range(NC):
                        if c < NC - 1:
                            keys_lo(h, 0, c, c)
                        dve.wait_ge(v_hi.sem, v_hi.at(h, c + 1))
                        nc.vector.tensor_tensor(vl[:, c, :], ps[:, (NC + c) % 2, :], f32(vh[:, c, :]),
                                                ALU.subtract).then_inc(v_lo.sem, 1)
                        if c == 0:
                            qT_lo_half(h, NC - 1)
                        dve.wait_ge(kT_hi.sem, kT_hi.at(h, c + 1))
                        nc.vector.tensor_tensor(kTl[:, :, :], ps[:, PT, 0:DK].rearrange("p (t n) -> p t n", t=2),
                                                f32(kTh[:, :, :]), ALU.subtract).then_inc(kT_lo.sem, 1)
                        dve.wait_ge(score_mm.sem, score_mm.at(h, c + 1))
                        dve.wait_ge(p_lo.sem, p_lo.at(h, c))
                        nc.vector.tensor_tensor(pf[:, :], ps[:, SC, 0:P], hd[:, DECAYS:], ALU.mult
                                                ).then_inc(p_f.sem, 1)
                        dve.wait_ge(p_hi.sem, p_hi.at(h, c + 1))
                        nc.vector.tensor_tensor(pl[:, :], pf[:, :], f32(ph[:, :]), ALU.subtract
                                                ).then_inc(p_lo.sem, 1)
                        dve.wait_ge(qs_mm.sem, qs_mm.at(h, c + 1))
                        dve.wait_ge(y_pv.sem, y_pv.at(h, c + 1))
                        nc.vector.scalar_tensor_tensor(y[:, c, :], ps[:, QS, :], hd[:, F_Q:F_Q + 1], y[:, c, :],
                                                       ALU.mult, ALU.add).then_inc(y_f.sem, 1)
                        if c < NC - 1:
                            update(h, 0, c)
                            state_lo(h, 0, c + 1)
                    state_lo(h, 1, 0)
                    for m, c in enumerate(order(1)):
                        if m < NC - 1:
                            keys_lo(h, 1, m, c)
                        dve.wait_ge(qs_mm.sem, qs_mm.at(h, NC + m + 1))
                        if m == 0:
                            dve.wait_ge(y_f.sem, y_f.at(h, NC))
                        nc.vector.scalar_tensor_tensor(y[:, c, :], ps[:, QS, :], hd[:, B_Q:B_Q + 1], y[:, c, :],
                                                       ALU.mult, ALU.add).then_inc(y_b.sem, 1)
                        if m < NC - 1:
                            update(h, 1, m)
                        dve.wait_ge(y_b.sem, y_b.at(h, m + 1))
                        nc.vector.bn_stats(stats[:, :], y[:, c, :]).then_inc(st_done.sem, 1)
                        dve.wait_ge(st_done.sem, st_done.at(h, m + 1))
                        if m < NC - 1:
                            state_lo(h, 1, m + 1)
                        else:
                            nc.vector.memset(ve[:, :], 0.0)
                        nc.vector.bn_aggr(mv[:, :], stats[:, :]).then_inc(ag_done.sem, 1)
                        dve.wait_ge(ag_done.sem, ag_done.at(h, m + 1))
                        nc.vector.tensor_scalar(ve[:, :], mv[:, 1:2], GN_EPS, None, ALU.add).then_inc(ve_done.sem, 1)
                        dve.wait_ge(rs_done.sem, rs_done.at(h, m + 1))
                        nc.vector.tensor_scalar(y[:, c, :], y[:, c, :], mv[:, 0:1], rstd[:, :], ALU.subtract,
                                                ALU.mult).then_inc(yn_done.sem, 1)
                        dve.wait_ge(yn_done.sem, yn_done.at(h, m + 1))
                        dve.wait_ge(gated.sem, gated.at(h, m + 1))
                        dve.wait_ge(stored.sem, stored.at(h, m))
                        nc.vector.tensor_tensor(t2[:, :], y[:, c, :], t1[:, :], ALU.mult).then_inc(yg_done.sem, 1)

            @block.tensor
            def _(pe):
                def project(h, b, m, c):
                    n = b * NC + m
                    if 2 <= n < NC + 2:
                        pe.wait_ge(rope_sin.sem, rope_sin.at(h, 2 * (n - 1)))
                    elif NC + 2 <= n < 2 * NC + 2:
                        pe.wait_ge(v_lo.sem, v_lo.at(h, n - 1 - NC))
                    else:
                        pe.wait_ge(silu.sem, silu.at(h, n - 1 - 2 * NC if n >= 2 else n - 1))
                    tok = slice(c * P, (c + 1) * P)
                    for k in range(KD):
                        if m == 0:
                            pe.wait_ge(w_lo.sem, w_lo.at(h, b * KD + k + 1))
                        mm = mm3(nc, ps[:, n % 2, :], hh[:, k, tok], hl[:, k, tok], wh[:, k, :], wl[:, k, :],
                                 k == 0, k == KD - 1)
                        if m == NC - 1 and k < KD - 1:
                            mm.then_inc(w_used.sem, 1)
                    mm.then_inc(proj.sem, 1)

                def turn_q(h, c):
                    pe.wait_ge(rope_out.sem, rope_out.at(h, 4 * c + 2))
                    pe.wait_ge(kT_lo.sem, kT_lo.at(h, 0)) if c == 0 else pe.wait_ge(qT_lo.sem, qT_lo.at(h, c))
                    for t in range(2):
                        mm = nc.tensor.transpose(ps[:, PT, t * P:(t + 1) * P], t1[:, t * P:(t + 1) * P], ident[:, :])
                    mm.then_inc(qT_mm.sem, 1)

                def turn_k(h, c):
                    if c == 0:
                        pe.wait_ge(qT_lo.sem, qT_lo.at(h, NC))
                    else:
                        pe.wait_ge(kT_lo.sem, kT_lo.at(h, c))
                    pe.wait_ge(rope_out.sem, rope_out.at(h, 4 * c + 4))
                    for t in range(2):
                        mm = nc.tensor.transpose(ps[:, PT, t * P:(t + 1) * P], kn[:, c, t * P:(t + 1) * P], ident[:, :])
                    mm.then_inc(kT_mm.sem, 1)

                def read_state(h, d, m, c):
                    pe.wait_ge(s_lo.sem, s_lo.at(h, d * NC + m + 1))
                    if d == 0:
                        pe.wait_ge(y_b.sem, y_b.at(h, 0)) if m == 0 else pe.wait_ge(y_f.sem, y_f.at(h, m))
                    else:
                        pe.wait_ge(y_f.sem, y_f.at(h, NC)) if m == 0 else pe.wait_ge(y_b.sem, y_b.at(h, m))
                    for t in range(2):
                        mm = mm3(nc, ps[:, QS, :], qTh[:, t, c * P:(c + 1) * P], qTl[:, t, c * P:(c + 1) * P],
                                 Sh[:, t, :], Sl[:, t, :], t == 0, t == 1)
                    mm.then_inc(qs_mm.sem, 1)

                def make_update(h, d, m, c):
                    n = d * (NC - 1) + m
                    pe.wait_ge(kd_lo.sem, kd_lo.at(h, n + 1))
                    pe.wait_ge(s_f32.sem, s_f32.at(h, n))
                    for t in range(2):
                        mm = mm3(nc, ps[:, U + t, :], kdh[:, t * P:(t + 1) * P], kdl[:, t * P:(t + 1) * P],
                                 vh[:, c, :], vl[:, c, :], True, True)
                    mm.then_inc(u_mm.sem, 1)

                pe.wait_ge(const_in, 16 * 5)
                with pe.Fori(0, HEADS) as h:
                    for c in range(NC):
                        project(h, 0, c, c)
                        if c >= 1:
                            turn_q(h, c - 1)
                    for c in range(NC):
                        project(h, 1, c, c)
                        if c == 0:
                            turn_q(h, NC - 1)
                            turn_k(h, 0)
                        pe.wait_ge(kT_lo.sem, kT_lo.at(h, c + 1))
                        if c == 0:
                            pe.wait_ge(qT_lo.sem, qT_lo.at(h, NC))
                        pe.wait_ge(p_f.sem, p_f.at(h, c))
                        for t in range(2):
                            mm = mm3(nc, ps[:, SC, 0:P], kTh[:, t, :], kTl[:, t, :], qTh[:, t, c * P:(c + 1) * P],
                                     qTl[:, t, c * P:(c + 1) * P], t == 0, t == 1)
                        mm.then_inc(score_mm.sem, 1)
                        read_state(h, 0, c, c)
                        pe.wait_ge(p_lo.sem, p_lo.at(h, c + 1))
                        pe.wait_ge(v_lo.sem, v_lo.at(h, c + 1))
                        pe.wait_ge(y_pv.sem, y_pv.at(h, c))
                        mm3(nc, ps[:, PV, :], ph[:, :], pl[:, :], vh[:, c, :], vl[:, c, :], True,
                            True).then_inc(pv_mm.sem, 1)
                        if c < NC - 1:
                            turn_k(h, c + 1)
                            make_update(h, 0, c, c)
                    for m, c in enumerate(order(1)):
                        project(h, 2, m, c)
                        read_state(h, 1, m, c)
                        if m < NC - 1:
                            make_update(h, 1, m, c)


def phase_retention_out(nc, a, sem, scope_sb, ps, part, x, y_dram):
    with ExitStack() as st:
        sb = scope_sb(st)
        RAW = 4
        SL = KV // RAW
        yn = sb("yn", [P, 2, HEADS * DV])
        yh = sb("yh", [P, KV, SEQ], F32R)
        yl = sb("yl", [P, KV, SEQ], F32R)
        raw = sb("raw3", [P, RAW, SL, P])
        wh = sb("wh3", [P, RAW, SL, P], F32R)
        wl = sb("wl3", [P, RAW, SL, P], F32R)
        ident = sb("ident3", [P, P])

        ident_in, x_in = sem("ident_in"), sem("x_in3")
        y_in = [sem(f"y_in{q}") for q in range(2)]
        turned, turned_hi, turned_lo = sem("y_turned"), sem("y_turned_hi"), sem("y_turned_lo")
        raw_in = [Tally(sem(f"out_raw_in{q}"), 1, unit=16) for q in range(RAW)]
        w_hi = Tally(sem("out_w_hi"), RAW)
        w_lo = Tally(sem("out_w_lo"), RAW, credit=True)
        out_mm = Tally(sem("out_mm"), 1, credit=True)
        w_used = Tally(sem("out_w_used"), RAW - 1, credit=True)
        added = sem("out_added")
        GROUPS = NC * RAW

        with nc.Block() as block:
            @block.sync
            def _(sp):
                pay(sp, w_lo, w_used, out_mm)
                sp.sem_inc(added, 2)
                sp.dma_start(ident[:, :], a["ident"]).then_inc(ident_in, 16)
                for c in range(NC):
                    if c >= 2:
                        sp.wait_ge(turned, RAW * (c - 1))
                    sp.dma_start(yn[:, c % 2, :], y_dram[c]).then_inc(y_in[c % 2], 16)
                sp.dma_start(x[:, :, :], a["xT"]).then_inc(x_in, 16)
                with sp.Fori(0, KD) as m:
                    for q in range(RAW):
                        sp.wait_ge(w_lo.sem, w_lo.at(m, q + 1 - RAW))
                        sp.dma_start(raw[:, q, :, :], a["ret_out"][bass.ds(m, 1), q]
                                     .rearrange("o p t n -> (o p) t n")).then_inc(raw_in[q].sem, 16)

            @block.gpsimd
            def _(pool):
                with pool.Fori(0, KD) as m:
                    for q in range(RAW):
                        pool.wait_ge(w_hi.sem, w_hi.at(m, q + 1))
                        nc.gpsimd.tensor_tensor(wl[:, q], raw[:, q], f32(wh[:, q]), ALU.subtract).then_inc(w_lo.sem, 1)

            @block.scalar
            def _(act):
                for g in range(GROUPS):
                    c, q = g // RAW, g % RAW
                    act.wait_ge(turned, g + 1)
                    nc.scalar.activation(yh[:, q * SL:(q + 1) * SL, c * P:(c + 1) * P],
                                         ps[:, q, :].rearrange("p (t n) -> p t n", n=P), ACT.Copy
                                         ).then_inc(turned_hi, 1)
                with act.Fori(0, KD) as m:
                    for q in range(RAW):
                        if q < RAW - 1:
                            act.wait_ge(w_used.sem, w_used.at(m, q + 1 - (RAW - 1)))
                        else:
                            act.wait_ge(out_mm.sem, out_mm.at(m, 0))
                        act.wait_ge(raw_in[q].sem, raw_in[q].at(m, 1))
                        nc.scalar.activation(wh[:, q], raw[:, q], ACT.Copy).then_inc(w_hi.sem, 1)

            @block.vector
            def _(dve):
                for g in range(GROUPS):
                    c, q = g // RAW, g % RAW
                    dve.wait_ge(turned_hi, g + 1)
                    nc.vector.tensor_tensor(yl[:, q * SL:(q + 1) * SL, c * P:(c + 1) * P],
                                            ps[:, q, :].rearrange("p (t n) -> p t n", n=P),
                                            f32(yh[:, q * SL:(q + 1) * SL, c * P:(c + 1) * P]),
                                            ALU.subtract).then_inc(turned_lo, 1)
                dve.wait_ge(x_in, 16)
                for m in range(KD):
                    b = 4 + 2 * (m % 2)
                    dve.wait_ge(out_mm.sem, out_mm.at(m, 1))
                    nc.vector.scalar_tensor_tensor(x[:, m, :], ps[:, b:b + 2, :].rearrange("p s n -> p (s n)"),
                                                   part(0, 2)(m), x[:, m, :], ALU.mult, ALU.add
                                                   ).then_inc(added, 1)

            @block.tensor
            def _(pe):
                pe.wait_ge(ident_in, 16)
                for g in range(GROUPS):
                    c, q = g // RAW, g % RAW
                    if q == 0:
                        pe.wait_ge(y_in[c % 2], 16 * (c // 2 + 1))
                    if g >= RAW:
                        pe.wait_ge(turned_lo, g + 1 - RAW)
                    for t in range(SL):
                        e = (q * SL + t) * P
                        mm = nc.tensor.transpose(ps[:, q, t * P:(t + 1) * P], yn[:, c % 2, e:e + P], ident[:, :])
                    mm.then_inc(turned, 1)
                pe.wait_ge(turned_lo, GROUPS)
                with pe.Fori(0, KD // 2) as i:
                    for r in range(2):
                        m = i * 2 + r
                        b = 4 + 2 * r
                        pe.wait_ge(added, i * 2 + (r + 1))
                        for q in range(RAW):
                            pe.wait_ge(w_lo.sem, w_lo.at(m, q + 1))
                            for t in range(SL):
                                kt = q * SL + t
                                for s in range(2):
                                    tok = slice(s * HALF, (s + 1) * HALF)
                                    mm = mm3(nc, ps[:, b + s, :], wh[:, q, t, :], wl[:, q, t, :], yh[:, kt, tok],
                                             yl[:, kt, tok], kt == 0, kt == KV - 1)
                            if q < RAW - 1:
                                mm.then_inc(w_used.sem, 1)
                        mm.then_inc(out_mm.sem, 1)


class Ffn:

    A0, O0, O1, B0, A1, B1 = range(6)
    SLOT = {A0: 0, B0: 1, A1: 2, B1: 3}

    def __init__(self, sem, keep):
        self.raw = keep("ffn_raw", [P, 3, KD * P])
        self.wih = keep("ffn_wih", [P, 4, KD * P], F32R)
        self.wil = keep("ffn_wil", [P, 4, KD * P], F32R)
        self.raw_in = [sem(f"ffn_raw_in{q}") for q in range(3)]
        self.w_hi, self.w_lo = sem("ffn_w_hi"), sem("ffn_w_lo")
        self.in_mm = Tally(sem("ffn_in_mm"), 4)
        self.silu = Tally(sem("ffn_silu"), 2)
        self.u = Tally(sem("ffn_u"), 2)
        self.u_hi = Tally(sem("ffn_u_hi"), 2)
        self.u_lo = Tally(sem("ffn_u_lo"), 2)
        self.out_mm = Tally(sem("ffn_out_mm"), KD, credit=True)
        self.added = Tally(sem("ffn_added"), KD, credit=True)

    def split(self, j, r):
        if isinstance(j, int) and j == 0:
            return {self.A0: 1, self.B0: 2, self.A1: 3, self.B1: 4}[r]
        if isinstance(j, int) and j == 2 * IT:
            return j * 6 + r - 2
        return j * 6 + (r - 1)

    def loaded(self, j, r):
        if isinstance(j, int) and j == 0:
            return 16 * {self.A0: 1, self.B0: 2, self.A1: 1, self.B1: 1}[r]
        return j * 32 + 16 * (r // 3 + 1 - (r % 3 > 0))


def phase_ffn(nc, a, scope_sb, ps, norms, f, layer, part, gain, minus_half, x):
    with ExitStack() as st:
        sb = scope_sb(st)
        hh = sb(f"fhh{layer}", [P, KD, SEQ], F32R)
        hl = sb(f"fhl{layer}", [P, KD, SEQ], F32R)
        with ExitStack() as tmp:
            nb = norms.buffers(scope_sb(tmp), f"fn{layer}", SEQ)
            run_norm(nc, norms, 2 + 2 * layer, nb, a["ident"], ps, x, gain[:, 1 + 2 * layer, :], part(layer, 3), minus_half,
                     lambda k: hh[:, k, :], hl, hh)
        raw, wih, wil = f.raw, f.wih, f.wil
        woh = sb(f"woh{layer}", [P, 2, D], F32R)
        wol = sb(f"wol{layer}", [P, 2, D], F32R)
        uf = sb(f"uf{layer}", [P, 2, SEQ])
        uh = sb(f"uh{layer}", [P, 2, SEQ], F32R)
        ul = sb(f"ul{layer}", [P, 2, SEQ], F32R)
        INB, OUTB = 0, 4
        j0 = IT * layer
        last = layer == 1

        def halves_of(r):
            if r in (f.O0, f.O1):
                return woh[:, r - f.O0, :], wol[:, r - f.O0, :]
            return wih[:, f.SLOT[r], :], wil[:, f.SLOT[r], :]

        def before(j, r):
            return (j, r - 3) if r >= 3 else (j - 1, r + 3)

        first_rs = (f.A0, f.B0, f.A1, f.B1)
        all_rs = tuple(range(6))
        end_rs = (f.O0, f.O1)

        def blocks(eng, do):
            if not last:
                for r in first_rs:
                    do(0, r)
            with eng.Fori(j0 + 1, j0 + IT + (0 if last else 1)) as j:
                for r in all_rs:
                    do(j, r)
            if last:
                for r in end_rs:
                    do(2 * IT, r)

        with nc.Block() as block:
            @block.sync
            def _(sp):
                if not last:
                    pay(sp, f.out_mm, f.added)

                def load(j, r):
                    if not (isinstance(j, int) and j == 0 and r in (f.A0, f.A1, f.B1)):
                        sp.wait_ge(f.w_lo, f.split(*before(j, r)))
                    src = a["ffn"][j, r] if isinstance(j, int) else a["ffn"][bass.ds(j, 1), r].rearrange(
                        "o p n -> (o p) n")
                    sp.dma_start(raw[:, r % 3, :], src).then_inc(f.raw_in[r % 3], 16)
                blocks(sp, load)

            @block.gpsimd
            def _(pool):
                def split_lo(j, r):
                    hi, lo = halves_of(r)
                    pool.wait_ge(f.w_hi, f.split(j, r))
                    nc.gpsimd.tensor_tensor(lo, raw[:, r % 3, :], f32(hi), ALU.subtract).then_inc(f.w_lo, 1)
                blocks(pool, split_lo)

            @block.scalar
            def _(act):
                def split_hi(j, r):
                    hi, lo = halves_of(r)
                    if r in (f.O0, f.O1):
                        act.wait_ge(f.out_mm.sem, f.out_mm.at(j - 1, 0))
                    elif not (isinstance(j, int) and j == 0):
                        act.wait_ge(f.in_mm.sem, f.in_mm.at(j - 1, f.SLOT[r] + 1))
                    act.wait_ge(f.raw_in[r % 3], f.loaded(j, r))
                    nc.scalar.activation(hi, raw[:, r % 3, :], ACT.Copy).then_inc(f.w_hi, 1)

                def gate(i, t):
                    act.wait_ge(f.in_mm.sem, f.in_mm.at(i, 2 * t + 1))
                    nc.scalar.activation(uf[:, t, :], ps[:, INB:INB + 2, :].rearrange("p s n -> p (s n)"),
                                         ACT.Silu).then_inc(f.silu.sem, 1)

                def u_hi(i, t):
                    act.wait_ge(f.u.sem, f.u.at(i, t + 1))
                    nc.scalar.activation(uh[:, t, :], uf[:, t, :], ACT.Copy).then_inc(f.u_hi.sem, 1)

                def iteration(i, rs):
                    gate(i, 0)
                    for r in rs:
                        if r in (f.A0, f.O0, f.O1):
                            split_hi(i + 1, r)
                    u_hi(i, 0)
                    if f.B0 in rs:
                        split_hi(i + 1, f.B0)
                    gate(i, 1)
                    if f.A1 in rs:
                        split_hi(i + 1, f.A1)
                    u_hi(i, 1)
                    if f.B1 in rs:
                        split_hi(i + 1, f.B1)

                if not last:
                    for r in first_rs:
                        split_hi(0, r)
                with act.Fori(j0, j0 + IT - (1 if last else 0)) as i:
                    iteration(i, all_rs)
                if last:
                    iteration(2 * IT - 1, end_rs)

            @block.vector
            def _(dve):
                def output(i):
                    for m in range(KD):
                        b = OUTB + 2 * (m % 2)
                        dve.wait_ge(f.out_mm.sem, f.out_mm.at(i, m + 1))
                        nc.vector.scalar_tensor_tensor(x[:, m, :], ps[:, b:b + 2, :].rearrange("p s n -> p (s n)"),
                                                       part(layer, 5)(m), x[:, m, :], ALU.mult, ALU.add
                                                       ).then_inc(f.added.sem, 1)

                def product(i, t):
                    dve.wait_ge(f.in_mm.sem, f.in_mm.at(i, 2 * t + 2))
                    dve.wait_ge(f.silu.sem, f.silu.at(i, t + 1))
                    nc.vector.tensor_tensor(uf[:, t, :], ps[:, INB + 2:INB + 4, :].rearrange("p s n -> p (s n)"),
                                            uf[:, t, :], ALU.mult).then_inc(f.u.sem, 1)
                    dve.wait_ge(f.u_hi.sem, f.u_hi.at(i, t + 1))
                    nc.vector.tensor_tensor(ul[:, t, :], uf[:, t, :], f32(uh[:, t, :]), ALU.subtract
                                            ).then_inc(f.u_lo.sem, 1)

                for t in range(2):
                    product(j0, t)
                with dve.Fori(j0 + 1, j0 + IT) as i:
                    output(i - 1)
                    for t in range(2):
                        product(i, t)
                output(j0 + IT - 1)
                dve.wait_ge(f.added.sem, f.added.at(j0 + IT - 1, KD))

            @block.tensor
            def _(pe):
                def project(i, n):
                    r = (f.A0, f.B0, f.A1, f.B1)[n]
                    pe.wait_ge(f.w_lo, f.split(i, r))
                    if n >= 2:
                        pe.wait_ge((f.silu, f.u)[n % 2].sem, (f.silu, f.u)[n % 2].at(i, 1))
                    elif not (isinstance(i, int) and i == 0):
                        pe.wait_ge((f.silu, f.u)[n % 2].sem, (f.silu, f.u)[n % 2].at(i, 0))
                    for k in range(KD):
                        for s in range(2):
                            tok = slice(s * HALF, (s + 1) * HALF)
                            cols = slice(k * P, (k + 1) * P)
                            mm = mm3(nc, ps[:, INB + 2 * (n % 2) + s, :], wih[:, n, cols], wil[:, n, cols],
                                     hh[:, k, tok], hl[:, k, tok], k == 0, k == KD - 1)
                    mm.then_inc(f.in_mm.sem, 1)

                def output(i):
                    pe.wait_ge(f.u_lo.sem, f.u_lo.at(i, 2))
                    pe.wait_ge(f.w_lo, f.split(i + 1, f.O1))
                    for m in range(KD):
                        pe.wait_ge(f.added.sem, f.added.at(i, m - 1))
                        for s in range(2):
                            tok = slice(s * HALF, (s + 1) * HALF)
                            cols = slice(m * P, (m + 1) * P)
                            for t in range(2):
                                mm = mm3(nc, ps[:, OUTB + 2 * (m % 2) + s, :], woh[:, t, cols], wol[:, t, cols],
                                         uh[:, t, tok], ul[:, t, tok], t == 0, t == 1)
                        mm.then_inc(f.out_mm.sem, 1)

                for n in range(4):
                    project(j0, n)
                with pe.Fori(j0 + 1, j0 + IT) as i:
                    project(i, 0)
                    output(i - 1)
                    for n in range(1, 4):
                        project(i, n)
                output(j0 + IT - 1)


def run_norm(nc, norms, r, nb, ident, ps, x, gain, shift, minus_half, out, lo, hi):
    with nc.Block() as block:
        @block.sync
        def _(sp):
            norms.load(sp, nb, ident, r)

        @block.scalar
        def _(act):
            norms.act_squares(nc, act, r, nb, x)
            norms.act_shift(nc, act, r, nb, shift, out)

        @block.vector
        def _(dve):
            norms.dve_ones(nc, nb)
            norms.dve_sum(nc, dve, r, nb)
            norms.dve_mean(nc, dve, r, nb, ps)
            norms.dve_diag(nc, dve, r, nb)
            norms.dve_scale(nc, dve, r, nb, ps, x, gain, shift, lo, hi)

        @block.tensor
        def _(pe):
            norms.pe_total(nc, pe, r, nb, ps)
            norms.pe_spread(nc, pe, r, nb, ps)

        @block.gpsimd
        def _(pool):
            norms.pool_rstd(nc, pool, r, nb, minus_half)


def phase_pool(nc, a, sem, scope_sb, ps, norms, part, gain, gps, minus_half, x):
    with ExitStack() as st:
        sb = scope_sb(st)
        h = sb("ph_h", [P, KD, PAD + SEQ + PAD])
        with ExitStack() as tmp:
            nb = norms.buffers(scope_sb(tmp), "pn", SEQ)
            run_norm(nc, norms, 3, nb, a["ident"], ps, x, gain[:, 2, :], part(1, 0), minus_half,
                     lambda k: h[:, k, PAD:PAD + SEQ], None, None)
        sums = sb("sums", [P, 2, PAD + SEQ + PAD])
        d = sb("d", [P, 2, SEQ])
        dh = sb("dh", [P, 4, SEQ], F32R)
        dl = sb("dl", [P, 4, SEQ], F32R)
        raw = sb("praw", [P, KD, 2 * P])
        wh = sb("pwh", [P, KD, 2 * P], F32R)
        wl = sb("pwl", [P, KD, 2 * P], F32R)
        edge = sb("edge", [P, 4, 2, PAD])
        pw_in, w_hi, w_lo = sem("pool_in"), sem("pool_w_hi"), sem("pool_w_lo")
        zero, level, diff, fix, fixed = (sem(f"pool_{n}") for n in ("pads", "level", "diff", "edge_mean", "edges"))
        d_hi, d_lo, mm_done, added = sem("pool_d_hi"), sem("pool_d_lo"), sem("pool_mm"), sem("pool_added")

        with nc.Block() as block:
            @block.sync
            def _(sp):
                sp.dma_start(raw[:, :, :], a["pool_w"]).then_inc(pw_in, 16)
                sp.dma_start(edge[:, :, :, :], a["edge"]).then_inc(pw_in, 16)

            @block.gpsimd
            def _(pool):
                pool.wait_ge(w_hi, 1)
                nc.gpsimd.tensor_tensor(wl[:, :, :], raw[:, :, :], f32(wh[:, :, :]), ALU.subtract).then_inc(w_lo, 1)

            @block.scalar
            def _(act):
                act.wait_ge(pw_in, 32)
                nc.scalar.activation(wh[:, :, :], raw[:, :, :], ACT.Copy).then_inc(w_hi, 1)
                for k in range(KD):
                    act.wait_ge(fixed, 2 * (k + 1))
                    act.wait_ge(diff, k + 1)
                    if k >= 4:
                        act.wait_ge(mm_done, 2 * (k // 2 - 1))
                    nc.scalar.activation(dh[:, k % 4, :], d[:, k % 2, :], ACT.Copy).then_inc(d_hi, 1)

            @block.vector
            def _(dve):
                nc.vector.memset(h[:, :, 0:PAD], 0.0).then_inc(zero, 1)
                nc.vector.memset(h[:, :, PAD + SEQ:], 0.0).then_inc(zero, 1)
                dve.wait_ge(zero, 2)
                dve.wait_ge(pw_in, 32)
                levels = fixes = 0
                for k in range(KD):
                    g = k // 2
                    w = WINDOWS[g]
                    src, reach = h[:, k, :], 1
                    n = 0
                    while reach < w:
                        off = reach // 2
                        lo_t, hi_t = -(w // 2 - reach), SEQ + (w // 2 - reach)
                        dst = sums[:, n % 2, :]
                        if reach == 1:
                            a0, a1 = src[:, PAD + lo_t - 1:PAD + hi_t - 1], src[:, PAD + lo_t:PAD + hi_t]
                        else:
                            a0 = src[:, PAD + lo_t - off:PAD + hi_t - off]
                            a1 = src[:, PAD + lo_t + off:PAD + hi_t + off]
                        nc.vector.tensor_tensor(dst[:, PAD + lo_t:PAD + hi_t], a0, a1, ALU.add).then_inc(level, 1)
                        levels += 1
                        dve.wait_ge(level, levels)
                        src, reach, n = dst, 2 * reach, n + 1
                    if k >= 2:
                        dve.wait_ge(d_hi, k - 1)
                    nc.vector.scalar_tensor_tensor(d[:, k % 2, :], src[:, PAD:PAD + SEQ], 1.0 / w,
                                                   h[:, k, PAD:PAD + SEQ], ALU.mult, ALU.subtract).then_inc(diff, 1)
                    dve.wait_ge(diff, k + 1)
                    for s, at in enumerate((0, SEQ - w // 2)):
                        e = slice(PAD + at, PAD + at + w // 2)
                        nc.vector.tensor_tensor(d[:, k % 2, at:at + w // 2], src[:, e], edge[:, g, s, 0:w // 2],
                                                ALU.mult).then_inc(fix, 1)
                        fixes += 1
                        dve.wait_ge(fix, fixes)
                        nc.vector.tensor_tensor(d[:, k % 2, at:at + w // 2], d[:, k % 2, at:at + w // 2], h[:, k, e],
                                                ALU.subtract).then_inc(fixed, 1)
                    dve.wait_ge(d_hi, k + 1)
                    nc.vector.tensor_tensor(dl[:, k % 4, :], d[:, k % 2, :], f32(dh[:, k % 4, :]), ALU.subtract
                                            ).then_inc(d_lo, 1)
                for m in range(KD):
                    b = 2 * (m % 4)
                    dve.wait_ge(mm_done, m + 1)
                    nc.vector.scalar_tensor_tensor(x[:, m, :], ps[:, b:b + 2, :].rearrange("p s n -> p (s n)"),
                                                   gps[:, m:m + 1], x[:, m, :], ALU.mult, ALU.add).then_inc(added, 1)

            @block.tensor
            def _(pe):
                pe.wait_ge(w_lo, 1)
                for m in range(KD):
                    g, b = m // 2, 2 * (m % 4)
                    pe.wait_ge(d_lo, 2 * g + 2)
                    if m >= 4:
                        pe.wait_ge(added, m - 3)
                    for s in range(2):
                        tok = slice(s * HALF, (s + 1) * HALF)
                        for t in range(2):
                            cols = slice((m % 2) * P, (m % 2 + 1) * P)
                            e = (2 * g + t) % 4
                            mm = mm3(nc, ps[:, b + s, :], wh[:, 2 * g + t, cols], wl[:, 2 * g + t, cols],
                                     dh[:, e, tok], dl[:, e, tok], t == 0, t == 1)
                    mm.then_inc(mm_done, 1)


def phase_final(nc, a, sem, scope_sb, ps, norms, vecs, minus_half, x, out):
    with ExitStack() as st:
        sb = scope_sb(st)
        nb = norms.buffers(sb, "on", SEQ)
        stored = sem("out_stored")
        r = 5
        with nc.Block() as block:
            @block.sync
            def _(sp):
                norms.load(sp, nb, a["ident"], r)
                for k in range(KD):
                    sp.wait_ge(norms.scaled.sem, norms.scaled.at(r, k + 1))
                    sp.dma_start(out[:, k, :], x[:, k, :]).then_inc(stored, 16)
                sp.wait_ge(stored, 16 * KD)

            @block.scalar
            def _(act):
                norms.act_squares(nc, act, r, nb, x)

            @block.vector
            def _(dve):
                norms.dve_ones(nc, nb)
                norms.dve_sum(nc, dve, r, nb)
                norms.dve_mean(nc, dve, r, nb, ps)
                norms.dve_diag(nc, dve, r, nb)
                dve.wait_ge(norms.spread.sem, norms.spread.at(r, 1))
                for k in range(KD):
                    nc.vector.scalar_tensor_tensor(x[:, k, :], x[:, k, :], vecs[:, V_FIN + k:V_FIN + k + 1],
                                                   norms.rstd_of(nb, ps), ALU.mult, ALU.mult
                                                   ).then_inc(norms.scaled.sem, 1)

            @block.tensor
            def _(pe):
                norms.pe_total(nc, pe, r, nb, ps)
                norms.pe_spread(nc, pe, r, nb, ps)

            @block.gpsimd
            def _(pool):
                norms.pool_rstd(nc, pool, r, nb, minus_half)



def lay_out(inputs):
    g = {n: np.asarray(v) for n, v in inputs.items()}
    cols = lambda v: v.reshape(-1, P).T
    a = {}
    a["xT"] = g["x"].reshape(SEQ, KD, P).transpose(2, 1, 0)
    a["ctxT"] = g["ctx"].reshape(CTX, KD, P).transpose(2, 1, 0)
    both = np.stack([cols(g["c"]), cols(g["c_ctx"])], axis=2).reshape(P, 16)
    a["vecs"] = np.concatenate([cols(g["norm1_w"]), cols(g["norm2_w"]), cols(g["final_norm_w"]), cols(g["pool_scale"]),
                                both, cols(g["ada_b"])], axis=1)
    a["log_decay"] = g["ret_log_decay"].reshape(2 * HEADS)
    a["ada"] = (g["ada_w"].reshape(2, KD, P, ADA_PIECES, 2 * P).transpose(0, 3, 2, 1, 4)
                .reshape(2 * ADA_PIECES, P, KD, 2 * P))
    w = g["ret_w_in"][0].reshape(KD, P, 6 * D)
    parts = []
    for h in range(HEADS):
        q, k = w[:, :, h * DK:(h + 1) * DK], w[:, :, D + h * DK:D + (h + 1) * DK]
        v, gg = (w[:, :, 2 * D + o + h * DV:2 * D + o + (h + 1) * DV] for o in (0, 2 * D))
        parts += [np.concatenate([q, k], axis=2), v, gg]
    a["ret_w"] = np.stack(parts)
    a["gn"] = np.broadcast_to(g["ret_gn_w"].reshape(HEADS, 1, DV), (HEADS, P, DV))
    a["ret_out"] = g["ret_w_out"][0].reshape(4, KV // 4, P, KD, P).transpose(3, 0, 2, 1, 4)
    win = g["ffn_w_in"].reshape(2, KD, P, 2, IT, 2, P).transpose(0, 4, 3, 5, 2, 1, 6).reshape(2 * IT, 2, 2, P, KD * P)
    wout = g["ffn_w_out"].reshape(2 * IT, 2, P, D)
    f = np.zeros((2 * IT + 1, 6, P, D), np.float32)
    f[:-1, 0], f[:-1, 3], f[:-1, 4], f[:-1, 5] = win[:, 0, 0], win[:, 1, 0], win[:, 0, 1], win[:, 1, 1]
    f[1:, 1], f[1:, 2] = wout[:, 0], wout[:, 1]
    a["ffn"] = f
    a["pool_w"] = g["pool_w"][0].reshape(KD, P, 2 * P).transpose(1, 0, 2)
    i = np.arange(P, dtype=np.float32)
    full = np.full(P, float(CHUNK), np.float32)
    a["expo"] = np.stack([i + 1, CHUNK - 1 - i, full, CTX - 1 - i, CTX - 1 - P - i,
                          CHUNK - i, i, full, i, i + P], axis=1)
    j, q = i[:, None], i[None, :]
    a["dist"] = np.stack([np.maximum(q - j, 0), np.maximum(j - q, 0)], axis=1)
    a["ident"] = np.eye(P, dtype=np.float32)
    inv = np.float32(10000.0) ** (-np.arange(0, P, 2, dtype=np.float32) / np.float32(P))
    t = np.arange(SEQ).reshape(NC, P).T
    row = (t // GRID_W).astype(np.float32)[:, :, None] * inv
    col = (np.arange(P) % GRID_W).astype(np.float32)[:, None] * inv
    a["cosr"], a["sinr"], a["cosc"], a["sinc"] = np.cos(row), np.sin(row), np.cos(col), np.sin(col)
    edge = np.zeros((P, 4, 2, PAD), np.float32)
    for n, w in enumerate(WINDOWS):
        e = np.arange(w // 2)
        edge[:, n, 0, :w // 2] = 1 / (e + w // 2).astype(np.float32)
        edge[:, n, 1, :w // 2] = 1 / (w - e).astype(np.float32)
    a["edge"] = edge
    return {n: np.ascontiguousarray(v) for n, v in a.items()}


def kernel(**inputs):
    import concourse.bacc as bacc
    from concourse.bass_utils import run_bass_kernel_spmd

    nc = bacc.Bacc("TRN2", target_bir_lowering=False, num_devices=1)
    arrays = lay_out(inputs)
    a = {n: nc.dram_tensor(f"in_{n}", v.shape, F32, kind="ExternalInput").ap() for n, v in arrays.items()}
    out = nc.dram_tensor("out_0", (P, KD, SEQ), F32, kind="ExternalOutput").ap()
    build(nc, a, out)
    r = run_bass_kernel_spmd(nc, [{f"in_{n}": v for n, v in arrays.items()}], core_ids=[0])
    return r.results[0]["out_0"].transpose(2, 1, 0).reshape(1, SEQ, D)
```

```python
from contextlib import ExitStack

import numpy as np

import concourse.bass as bass
from concourse import mybir

F32 = mybir.dt.float32
F32R = mybir.dt.float32r
ALU = mybir.AluOpType
ACT = mybir.ActivationFunctionType

P = 128
D = 1024
KD = D // P
SEQ = 1024
HALF = 512
GRID_W = 64
CTX = 256
CT = CTX // P
CHUNK = 128
NC = SEQ // CHUNK
HEADS = 4
DK = D // HEADS
DV = 2 * D // HEADS
KV = 2 * D // P
HID = 2816
IT = HID // (2 * P)
WINDOWS = (2, 4, 8, 16)
PAD = 8
EPS = 1e-6
GN_EPS = 1e-5
ADA_FIRST = 2 * D // 512
ADA_LAYER1 = 6 * D // 512

V_N1, V_N2, V_FIN, V_PS, V_C, V_AB = 0, 16, 32, 40, 48, 64
V_ALL = V_AB + 96
DECAYS = 10
F_Q, F_K, F_CHUNK, F_CTX, B_Q, B_K, B_CHUNK, B_CTX = 0, 1, 2, 3, 5, 6, 7, 8


class Tally:

    def __init__(self, sem, per, credit=False, unit=1):
        self.sem, self.per, self.credit, self.unit = sem, per, credit, unit

    def at(self, r, n):
        return r * (self.per * self.unit) + (n + self.per * self.credit) * self.unit


def pay(eng, *tallies):
    for t in tallies:
        eng.sem_inc(t.sem, t.per * t.unit)


def mm3(nc, out, w_hi, w_lo, x_hi, x_lo, first, last):
    nc.tensor.matmul(out, w_hi, x_hi, start=first, stop=False)
    nc.tensor.matmul(out, w_hi, x_lo, start=False, stop=False)
    return nc.tensor.matmul(out, w_lo, x_hi, start=False, stop=last)


def f32(ap):
    return ap.bitcast(F32)


def wide(ap, *dims):
    return ap.broadcast_to([P, *dims])


class Norms:

    def __init__(self, sem):
        self.squared = Tally(sem("norm_squared"), KD)
        self.summed = Tally(sem("norm_summed"), KD)
        self.total = Tally(sem("norm_total"), 1)
        self.mean = Tally(sem("norm_mean"), 1)
        self.rstd = Tally(sem("norm_rstd"), 1)
        self.diag = Tally(sem("norm_diagonal"), 1)
        self.spread = Tally(sem("norm_spread"), 1)
        self.scaled = Tally(sem("norm_scaled"), KD)
        self.hi = Tally(sem("norm_hi"), KD)
        self.lo = Tally(sem("norm_lo"), KD)
        self.ones = sem("norm_ones")
        self.ident_in = sem("norm_ident_in")

    def buffers(self, sb, name, n, scaled=True):
        t = dict(t=sb(f"{name}_t", [P, 2, n])) if scaled else {}
        return dict(t, n=n, sq=sb(f"{name}_sq", [P, 2, n]), acc=sb(f"{name}_acc", [P, n]),
                    ms=sb(f"{name}_ms", [P, n // P]), rs=sb(f"{name}_rs", [P, n // P]),
                    dg=sb(f"{name}_dg", [P, n]), ones=sb(f"{name}_ones", [P, P]), ident=sb(f"{name}_ident", [P, P]))

    def act_squares(self, nc, act, r, b, x):
        for k in range(KD):
            if k >= 2:
                act.wait_ge(self.summed.sem, self.summed.at(r, k - 1))
            nc.scalar.activation(b["sq"][:, k % 2, :], x[:, k, :], ACT.Square).then_inc(self.squared.sem, 1)

    def dve_sum(self, nc, dve, r, b):
        for k in range(KD):
            dve.wait_ge(self.squared.sem, self.squared.at(r, k + 1))
            if k == 0:
                nc.vector.tensor_copy(b["acc"][:, :], b["sq"][:, 0, :]).then_inc(self.summed.sem, 1)
            else:
                dve.wait_ge(self.summed.sem, self.summed.at(r, k))
                nc.vector.tensor_tensor(b["acc"][:, :], b["acc"][:, :], b["sq"][:, k % 2, :],
                                        ALU.add).then_inc(self.summed.sem, 1)

    def load(self, sp, b, ident, r):
        sp.dma_start(b["ident"][:, :], ident).then_inc(self.ident_in, 16)

    def dve_ones(self, nc, b):
        nc.vector.memset(b["ones"][:, :], 1.0).then_inc(self.ones, 1)

    def pe_total(self, nc, pe, r, b, ps):
        pe.wait_ge(self.ones, r + 1)
        pe.wait_ge(self.summed.sem, self.summed.at(r, KD))
        for j in range(b["n"] // P):
            mm = nc.tensor.matmul(ps[:, 0, j:j + 1], b["acc"][:, j * P:(j + 1) * P], b["ones"][:, 0:1],
                                  start=True, stop=True)
        mm.then_inc(self.total.sem, 1)

    def dve_mean(self, nc, dve, r, b, ps):
        dve.wait_ge(self.total.sem, self.total.at(r, 1))
        nc.vector.tensor_scalar(b["ms"][:, :], ps[:, 0, 0:b["n"] // P], 1.0 / D, EPS, ALU.mult, ALU.add
                                ).then_inc(self.mean.sem, 1)

    def pool_rstd(self, nc, pool, r, b, minus_half):
        pool.wait_ge(self.mean.sem, self.mean.at(r, 1))
        nc.gpsimd.tensor_tensor(b["rs"][:, :], b["ms"][:, :], wide(minus_half[:, 0:1], b["n"] // P),
                                ALU.pow).then_inc(self.rstd.sem, 1)

    def dve_diag(self, nc, dve, r, b):
        dve.wait_ge(self.ident_in, 16 * (r + 1))
        dve.wait_ge(self.rstd.sem, self.rstd.at(r, 1))
        n = b["n"] // P
        nc.vector.tensor_tensor(b["dg"][:, :].rearrange("p (j t) -> p j t", t=P),
                                b["ident"][:, :].unsqueeze(1).broadcast_to([P, n, P]),
                                b["rs"][:, :].unsqueeze(2).broadcast_to([P, n, P]), ALU.mult
                                ).then_inc(self.diag.sem, 1)

    def pe_spread(self, nc, pe, r, b, ps):
        pe.wait_ge(self.diag.sem, self.diag.at(r, 1))
        w = min(b["n"], HALF)
        for s in range(0, b["n"], w):
            mm = nc.tensor.matmul(ps[:, s // HALF, 0:w], b["ones"][:, :], b["dg"][:, s:s + w], start=True, stop=True)
        mm.then_inc(self.spread.sem, 1)

    def rstd_of(self, b, ps):
        return ps[:, 0, 0:b["n"]] if b["n"] <= HALF else ps[:, 0:2, :].rearrange("p s n -> p (s n)")

    def dve_scale(self, nc, dve, r, b, ps, x, gain, shift, lo, hi):
        dve.wait_ge(self.spread.sem, self.spread.at(r, 1))
        lr = r - (r > 3)
        for k in range(KD + 1):
            if k < KD:
                if k >= 2:
                    dve.wait_ge(self.hi.sem, self.hi.at(r, k - 1))
                    if lo is not None:
                        dve.wait_ge(self.lo.sem, self.lo.at(lr, k - 1))
                nc.vector.scalar_tensor_tensor(b["t"][:, k % 2, :], x[:, k, :], gain[:, k:k + 1],
                                               self.rstd_of(b, ps),
                                               ALU.mult, ALU.mult).then_inc(self.scaled.sem, 1)
            if k and lo is not None:
                dve.wait_ge(self.scaled.sem, self.scaled.at(r, k))
                dve.wait_ge(self.hi.sem, self.hi.at(r, k))
                nc.vector.scalar_tensor_tensor(lo[:, k - 1, :], b["t"][:, (k - 1) % 2, :], shift(k - 1),
                                               f32(hi[:, k - 1, :]), ALU.add, ALU.subtract).then_inc(self.lo.sem, 1)

    def act_shift(self, nc, act, r, b, shift, out):
        for k in range(KD):
            act.wait_ge(self.scaled.sem, self.scaled.at(r, k + 1))
            nc.scalar.activation(out(k), b["t"][:, k % 2, :], ACT.Identity, bias=shift(k)).then_inc(self.hi.sem, 1)


def make_gain(nc, gain, mod, vecs, n, layer, p, c, w):
    at = layer * 48 + p * 8
    return nc.vector.scalar_tensor_tensor(gain[:, n, :], mod[:, at:at + 8, c], 1.0, vecs[:, w:w + 8],
                                          ALU.add, ALU.mult)


def build(nc, a, out):
    with ExitStack() as whole:
        build_phases(nc, a, out, whole)


def build_phases(nc, a, out, whole):
    def sem(name):
        return whole.enter_context(nc.semaphore(name))

    def scope_sb(stack):
        return lambda name, shape, dt=F32: stack.enter_context(nc.sbuf_tensor(name, shape, dt))

    keep = scope_sb(whole)
    ps = whole.enter_context(nc.psum_tensor("ps", [P, 8, HALF], F32))
    vecs = keep("vecs", [P, V_ALL])
    mod = keep("mod", [P, 96, 2])
    gain = keep("gain", [P, 6, KD])
    gps = keep("gps", [P, KD])
    minus_half = keep("minus_half", [P, 1])
    cs = keep("cs", [P, KD, 2])
    one = keep("one", [P, 1])

    def part(layer, n, ctx=0):
        return lambda k: mod[:, layer * 48 + n * 8 + k, ctx:ctx + 1]

    s0_dram = nc.dram_tensor("s0_dram", [HEADS, 2, P, 2 * DV], F32, kind="Internal").ap()
    head_dram = nc.dram_tensor("head_dram", [HEADS, P, DECAYS + P], F32, kind="Internal").ap()
    y_dram = nc.dram_tensor("y_dram", [NC, P, HEADS * DV], F32, kind="Internal").ap()

    norms = Norms(sem)
    with ExitStack() as first:
        sb1 = scope_sb(first)
        hh = sb1("hh", [P, KD, SEQ], F32R)
        hl = sb1("hl", [P, KD, SEQ], F32R)
        with ExitStack() as second:
            sb2 = scope_sb(second)
            ch = sb2("ch", [P, KD, CTX], F32R)
            cl = sb2("cl", [P, KD, CTX], F32R)
            xT = sb2("xT", [P, KD, SEQ])
            x_rstd = sb2("x_rstd", [P, SEQ])
            phase_conditioning(nc, a, sem, scope_sb, ps, norms, vecs, mod, gain, minus_half, one, cs, part,
                               xT, x_rstd, ch, cl, head_dram)
            phase_context_states(nc, a, sem, scope_sb, ps, norms, one, mod, gain, xT, x_rstd, hh, hl, ch, cl, head_dram,
                                 s0_dram)
        phase_retention(nc, a, sem, scope_sb, ps, minus_half, one, cs, mod, vecs, hh, hl, s0_dram, head_dram,
                        y_dram)
    x = keep("x", [P, KD, SEQ])
    phase_retention_out(nc, a, sem, scope_sb, ps, part, x, y_dram, gain, mod, vecs)
    ffn = Ffn(sem, keep)
    cond = (cs, one, mod, vecs, gps)
    phase_ffn(nc, a, scope_sb, ps, norms, ffn, 0, part, gain, minus_half, x, cond)
    phase_pool(nc, a, sem, scope_sb, ps, norms, part, gain, gps, minus_half, x)
    phase_ffn(nc, a, scope_sb, ps, norms, ffn, 1, part, gain, minus_half, x, cond)
    phase_final(nc, a, sem, scope_sb, ps, norms, vecs, minus_half, x, out)


def phase_conditioning(nc, a, sem, scope_sb, ps, norms, vecs, mod, gain, minus_half, one, cs, part,
                       xT, x_rstd, ch, cl, head_dram):
    with ExitStack() as st:
        sb = scope_sb(st)
        cT = sb("cT", [P, KD, CTX])
        nb = norms.buffers(sb, "n0", SEQ, scaled=False)
        nbc = norms.buffers(sb, "nc", CTX)
        ada = sb("ada", [P, 4, KD // 2, 512])
        cw = sb("cw", [P, KD, P])
        rows = sb("rows", [P, ADA_FIRST, 512])
        expo = sb("expo", [P, 10])
        dist = sb("dist", [P, 2, P])
        lg = sb("lg", [P, 2 * HEADS])
        arg = sb("arg", [P, HEADS, P])
        heads = sb("heads", [P, HEADS, DECAYS + P])
        ROWS, TURN, CPS, XPS = 0, 4, 5, 6

        small_in, ctx_in = sem("small_in"), sem("ctx_in")
        x_in = [sem(f"x_in{q}") for q in range(2)]
        ada_in = [sem(f"ada_in{q}") for q in range(4)]
        ada_mm, ada_rows, ada_turned, ada_out = sem("ada_mm"), sem("ada_rows"), sem("ada_turned"), sem("ada_out")
        ready = sem("consts_ready")
        c_silu, c_wide = sem("c_silu"), sem("c_wide")
        decay_step = sem("decay_step")
        decays, arg_done, mask_done, mask_out = sem("decays"), sem("arg_done"), sem("mask_done"), sem("mask_out")
        gains, rstd_row = sem("gains"), sem("rstd_row")

        with nc.Block() as block:
            @block.sync
            def _(sp):
                sp.dma_start(vecs[:, :], a["vecs"]).then_inc(small_in, 16)
                sp.dma_start(lg[:, :], a["log_decay"].partition_broadcast(P)).then_inc(small_in, 16)
                sp.dma_start(expo[:, :], a["expo"]).then_inc(small_in, 16)
                sp.dma_start(dist[:, :, :], a["dist"]).then_inc(small_in, 16)
                norms.load(sp, nbc, a["ident"], 0)
                norms.load(sp, nb, a["ident"], 1)
                sp.dma_start(cT[:, :, :], a["ctxT"]).then_inc(ctx_in, 16)
                for n in range(2 * ADA_FIRST):
                    if n >= 4:
                        sp.wait_ge(ada_mm, n - 3)
                    sp.dma_start(ada[:, n % 4, :, :], a["ada_first"][n // 2, n % 2]).then_inc(ada_in[n % 4], 16)
                for q in range(2):
                    t = slice(q * KD // 2, (q + 1) * KD // 2)
                    sp.dma_start(xT[:, t, :], a["xT"][:, t, :]).then_inc(x_in[q], 16)
                sp.wait_ge(mask_out, 16)

            @block.scalar
            def _(act):
                act.wait_ge(small_in, 64)
                nc.scalar.activation(cs[:, :, :].rearrange("p k c -> p (k c)"), vecs[:, V_C:V_C + 16],
                                     ACT.Silu).then_inc(c_silu, 1)
                act.wait_ge(decays, 1)
                for h in range(HEADS):
                    for d, (e0, e1) in enumerate(((0, 5), (5, 10))):
                        nc.scalar.activation(heads[:, h, e0:e1], expo[:, e0:e1], ACT.Exp,
                                             scale=lg[:, d * HEADS + h:d * HEADS + h + 1]).then_inc(decay_step, 1)
                act.wait_ge(arg_done, HEADS)
                nc.scalar.activation(heads[:, :, DECAYS:], arg[:, :, :], ACT.Exp).then_inc(mask_done, 1)
                act.wait_ge(mask_done, 1)
                act.wait_ge(decay_step, 2 * HEADS)
                act.dma_start(head_dram.rearrange("h p n -> p h n"), heads[:, :, :]).then_inc(mask_out, 16)
                act.wait_ge(ctx_in, 16)
                norms.act_squares(nc, act, 0, nbc, cT)
                for b in range(ADA_FIRST):
                    act.wait_ge(ada_mm, 2 * (b + 1))
                    nc.scalar.activation(rows[:, b, :], ps[:, ROWS + b % 2, :], ACT.Copy).then_inc(ada_rows, 1)
                norms.act_shift(nc, act, 0, nbc, part(0, 0, 1), lambda k: ch[:, k, :])
                act.wait_ge(x_in[0], 16)
                act.wait_ge(x_in[1], 16)
                norms.act_squares(nc, act, 1, nb, xT)
                act.wait_ge(norms.spread.sem, norms.spread.at(1, 1))
                nc.scalar.activation(x_rstd[:, :], norms.rstd_of(nb, ps[:, XPS:XPS + 2, :]), ACT.Copy
                                     ).then_inc(rstd_row, 1)

            @block.vector
            def _(dve):
                nc.vector.memset(cw[:, :, :], 0.0).then_inc(c_wide, 1)
                norms.dve_ones(nc, nbc)
                norms.dve_ones(nc, nb)
                nc.vector.memset(minus_half[:, :], -0.5).then_inc(ready, 1)
                nc.vector.memset(one[:, :], 1.0).then_inc(ready, 1)
                dve.wait_ge(small_in, 64)
                neg = sem("log_decay_negated")
                nc.vector.tensor_scalar(arg[:, 0, 0:8], lg[:, :], -1.0, None, ALU.mult).then_inc(neg, 1)
                dve.wait_ge(neg, 1)
                nc.vector.tensor_tensor(lg[:, :], lg[:, :], arg[:, 0, 0:8], ALU.min).then_inc(decays, 1)
                dve.wait_ge(c_silu, 1)
                dve.wait_ge(c_wide, 1)
                nc.vector.tensor_copy(cw[:, :, 0:2], cs[:, :, :]).then_inc(c_wide, 1)
                dve.wait_ge(decays, 1)
                back = sem("backward_exponent")
                for h in range(HEADS):
                    nc.vector.tensor_scalar(arg[:, h, :], dist[:, 1, :], lg[:, HEADS + h:HEADS + h + 1], None,
                                            ALU.mult).then_inc(back, 1)
                for h in range(HEADS):
                    dve.wait_ge(back, h + 1)
                    nc.vector.scalar_tensor_tensor(arg[:, h, :], dist[:, 0, :], lg[:, h:h + 1], arg[:, h, :],
                                                   ALU.mult, ALU.add).then_inc(arg_done, 1)
                norms.dve_sum(nc, dve, 0, nbc)
                norms.dve_mean(nc, dve, 0, nbc, ps[:, CPS:CPS + 1, :])
                norms.dve_diag(nc, dve, 0, nbc)
                for b in range(ADA_FIRST):
                    dve.wait_ge(ada_turned, b + 1)
                    nc.vector.tensor_tensor(mod[:, 4 * b:4 * b + 4, :], ps[:, TURN, 0:8].rearrange(
                        "p (j c) -> p j c", c=2), vecs[:, V_AB + 4 * b:V_AB + 4 * b + 4].unsqueeze(2)
                        .broadcast_to([P, 4, 2]), ALU.add).then_inc(ada_out, 1)
                dve.wait_ge(ada_out, ADA_FIRST)
                for n, c in ((0, 0), (4, 1)):
                    make_gain(nc, gain, mod, vecs, n, 0, 1, c, V_N1).then_inc(gains, 1)
                dve.wait_ge(gains, 2)
                norms.dve_scale(nc, dve, 0, nbc, ps[:, CPS:CPS + 1, :], cT, gain[:, 4, :], part(0, 0, 1), cl, ch)
                norms.dve_sum(nc, dve, 1, nb)
                norms.dve_mean(nc, dve, 1, nb, ps[:, XPS:XPS + 2, :])
                norms.dve_diag(nc, dve, 1, nb)

            @block.tensor
            def _(pe):
                def turn(b):
                    pe.wait_ge(ada_rows, b + 1)
                    if b:
                        pe.wait_ge(ada_out, b)
                    else:
                        pe.wait_ge(norms.ident_in, 32)
                    for j in range(4):
                        mm = nc.tensor.matmul(ps[:, TURN, 2 * j:2 * j + 2], rows[:, b, j * P:(j + 1) * P],
                                              nb["ident"][:, 0:2], start=True, stop=True)
                    mm.then_inc(ada_turned, 1)

                pe.wait_ge(c_wide, 2)
                for b in range(ADA_FIRST):
                    for q in range(2):
                        n = 2 * b + q
                        pe.wait_ge(ada_in[n % 4], 16 * (n // 4 + 1))
                        if q == 0 and b >= 2:
                            pe.wait_ge(ada_rows, b - 1)
                        for k in range(KD // 2):
                            kt = q * KD // 2 + k
                            mm = nc.tensor.matmul(ps[:, ROWS + b % 2, :], cw[:, kt, :], ada[:, n % 4, k, :],
                                                  start=kt == 0, stop=kt == KD - 1)
                        mm.then_inc(ada_mm, 1)
                    if b == 0:
                        norms.pe_total(nc, pe, 0, nbc, ps[:, CPS:CPS + 1, :])
                    else:
                        turn(b - 1)
                        if b == 1:
                            norms.pe_spread(nc, pe, 0, nbc, ps[:, CPS:CPS + 1, :])
                turn(ADA_FIRST - 1)
                norms.pe_total(nc, pe, 1, nb, ps[:, XPS:XPS + 2, :])
                norms.pe_spread(nc, pe, 1, nb, ps[:, XPS:XPS + 2, :])

            @block.gpsimd
            def _(pool):
                pool.wait_ge(ready, 1)
                norms.pool_rstd(nc, pool, 0, nbc, minus_half)
                norms.pool_rstd(nc, pool, 1, nb, minus_half)


def phase_context_states(nc, a, sem, scope_sb, ps, norms, one, mod, gain, xT, x_rstd, hh, hl, ch, cl, head_dram, s0_dram):
    with ExitStack() as st:
        sb = scope_sb(st)
        WK = DK + DV
        RAW = 4
        XT = KD // HEADS
        raw = sb("raw1", [P, RAW, WK])
        wh = sb("wh1", [P, KD, WK], F32R)
        wl = sb("wl1", [P, KD, WK], F32R)
        vh = sb("vh1", [P, CT, DV], F32R)
        vl = sb("vl1", [P, CT, DV], F32R)
        kh = sb("kh1", [P, 2, CT, DK], F32R)
        kl = sb("kl1", [P, 2, CT, DK], F32R)
        s0 = sb("s0", [P, 2, 2 * DV])
        hd = sb("hd1", [P, DECAYS])
        idle = sb("idle1", [P, XT])

        raw_in = [Tally(sem(f"ctx_raw_in{q}"), 2, unit=32) for q in range(RAW)]
        hd_in = Tally(sem("ctx_decays_in"), 1, unit=16)
        w_hi = Tally(sem("ctx_w_hi"), KD)
        w_lo = [Tally(sem(f"ctx_w_lo_{n}"), KD // 2, credit=True) for n in ("even", "odd")]
        w_used = Tally(sem("ctx_w_used"), KD - 1, credit=True)
        proj = Tally(sem("ctx_proj"), CT, credit=True)
        hi = Tally(sem("ctx_kv_hi"), 3 * CT)
        lo = Tally(sem("ctx_kv_lo"), 3 * CT, credit=True)
        states = Tally(sem("ctx_states"), 2, credit=True)
        copied = [Tally(sem(f"ctx_copied{d}"), 1, credit=True) for d in range(2)]
        stored = [Tally(sem(f"ctx_stored{d}"), 1, credit=True, unit=16) for d in range(2)]

        def lo_made(eng, h, k):
            eng.wait_ge(w_lo[k % 2].sem, w_lo[k % 2].at(h, k // 2 + 1))

        def tile(ap, h, j):
            return ap[:, bass.ds(h * XT + j, 1), :]

        def column(ap, h, j):
            return ap[:, bass.ds(h * XT + j, 1)]

        with nc.Block() as block:
            @block.sync
            def _(sp):
                pay(sp, *w_lo, w_used, proj, lo, states, *copied, *stored)
                with sp.Fori(0, HEADS) as h:
                    for k in range(KD):
                        lo_made(sp, h, k - RAW)
                        sp.dma_start(raw[:, k % RAW, 0:DK], a["ret_w"][bass.ds(h * 3, 1), k, :, DK:2 * DK]
                                     .rearrange("o p n -> (o p) n")).then_inc(raw_in[k % RAW].sem, 16)
                        sp.dma_start(raw[:, k % RAW, DK:WK], a["ret_w"][bass.ds(h * 3 + 1, 1), k, :, :]
                                     .rearrange("o p n -> (o p) n")).then_inc(raw_in[k % RAW].sem, 16)
                    sp.wait_ge(lo.sem, lo.at(h, 0))
                    sp.dma_start(hd[:, :], head_dram[bass.ds(h, 1), :, 0:DECAYS]
                                 .rearrange("o p n -> (o p) n")).then_inc(hd_in.sem, 16)

            @block.gpsimd
            def _(pool):
                with pool.Fori(0, HEADS) as h:
                    for k in range(0, KD, 2):
                        pool.wait_ge(w_hi.sem, w_hi.at(h, k + 1))
                        nc.gpsimd.tensor_tensor(wl[:, k, :], raw[:, k % RAW, :], f32(wh[:, k, :]),
                                                ALU.subtract).then_inc(w_lo[0].sem, 1)

            @block.scalar
            def _(act):
                def split_hi(h, ks):
                    for k in ks:
                        if k < KD - 1:
                            act.wait_ge(w_used.sem, w_used.at(h - 1, k + 1))
                        else:
                            act.wait_ge(proj.sem, proj.at(h - 1, CT))
                        act.wait_ge(raw_in[k % RAW].sem, raw_in[k % RAW].at(h, k // RAW + 1))
                        nc.scalar.activation(wh[:, k, :], raw[:, k % RAW, :], ACT.Copy).then_inc(w_hi.sem, 1)

                def kv_hi(h, t):
                    if t == 0:
                        act.wait_ge(states.sem, states.at(h, 0))
                        act.wait_ge(hd_in.sem, hd_in.at(h, 1))
                    act.wait_ge(proj.sem, proj.at(h, t + 1))
                    nc.scalar.activation(vh[:, t, :], ps[:, 2 + t, :], ACT.Copy).then_inc(hi.sem, 1)
                    for d, e in enumerate((F_CTX, B_CTX)):
                        nc.scalar.activation(kh[:, d, t, :], ps[:, t, 0:DK], ACT.Copy,
                                             scale=hd[:, e + t:e + t + 1]).then_inc(hi.sem, 1)

                def latent_hi(h):
                    for j in range(XT):
                        act.wait_ge(norms.scaled.sem, norms.scaled.at(1, h * XT + (j + 1)))
                        nc.scalar.activation(idle[:, j:j + 1], one[:, :], ACT.Copy)
                        nc.scalar.activation(tile(hh, h, j), tile(xT, h, j), ACT.Identity,
                                             bias=column(mod[:, :, 0], h, j)).then_inc(norms.hi.sem, 1)

                def copy_states(h):
                    act.wait_ge(stored[0].sem, stored[0].at(h, 0))
                    act.wait_ge(states.sem, states.at(h, 1))
                    nc.scalar.activation(s0[:, 0, :], ps[:, 4:6, :].rearrange("p t n -> p (t n)"),
                                         ACT.Copy).then_inc(copied[0].sem, 1)
                    for d in range(2):
                        act.wait_ge(copied[d].sem, copied[d].at(h, 1))
                        act.dma_start(s0_dram[bass.ds(h, 1), d].rearrange("o p n -> (o p) n"),
                                      s0[:, d, :]).then_inc(stored[d].sem, 16)

                split_hi(0, range(KD))
                kv_hi(0, 0)
                with act.Fori(0, HEADS - 1) as h:
                    split_hi(h + 1, range(KD // 2))
                    kv_hi(h, 1)
                    split_hi(h + 1, range(KD // 2, KD))
                    latent_hi(h)
                    copy_states(h)
                    kv_hi(h + 1, 0)
                kv_hi(HEADS - 1, 1)
                latent_hi(HEADS - 1)
                copy_states(HEADS - 1)
                for d in range(2):
                    act.wait_ge(stored[d].sem, stored[d].at(HEADS - 1, 1))

            @block.vector
            def _(dve):
                def split_odd(h, ks):
                    for k in ks:
                        dve.wait_ge(w_hi.sem, w_hi.at(h, k + 1))
                        nc.vector.tensor_tensor(wl[:, k, :], raw[:, k % RAW, :], f32(wh[:, k, :]),
                                                ALU.subtract).then_inc(w_lo[1].sem, 1)

                def kv_lo(h, t):
                    dve.wait_ge(hi.sem, hi.at(h, 3 * t + 1))
                    nc.vector.tensor_tensor(vl[:, t, :], ps[:, 2 + t, :], f32(vh[:, t, :]),
                                            ALU.subtract).then_inc(lo.sem, 1)
                    dve.wait_ge(hi.sem, hi.at(h, 3 * t + 3))
                    for d, e in enumerate((F_CTX, B_CTX)):
                        nc.vector.scalar_tensor_tensor(kl[:, d, t, :], ps[:, t, 0:DK], hd[:, e + t:e + t + 1],
                                                       f32(kh[:, d, t, :]), ALU.mult,
                                                       ALU.subtract).then_inc(lo.sem, 1)

                def latent_scaled(h):
                    for j in range(XT):
                        nc.vector.scalar_tensor_tensor(tile(xT, h, j), tile(xT, h, j), column(gain[:, 0, :], h, j),
                                                       x_rstd[:, :].unsqueeze(1), ALU.mult, ALU.mult
                                                       ).then_inc(norms.scaled.sem, 1)

                def latent_lo(h):
                    for j in range(XT):
                        dve.wait_ge(norms.scaled.sem, norms.scaled.at(1, h * XT + (j + 1)))
                        dve.wait_ge(norms.hi.sem, norms.hi.at(1, h * XT + (j + 1)))
                        nc.vector.scalar_tensor_tensor(tile(hl, h, j), tile(xT, h, j), column(mod[:, :, 0], h, j),
                                                       f32(tile(hh, h, j)), ALU.add, ALU.subtract
                                                       ).then_inc(norms.lo.sem, 1)

                def copy_states(h):
                    dve.wait_ge(stored[1].sem, stored[1].at(h, 0))
                    dve.wait_ge(states.sem, states.at(h, 2))
                    nc.vector.tensor_copy(s0[:, 1, :], ps[:, 6:8, :].rearrange("p t n -> p (t n)")
                                          ).then_inc(copied[1].sem, 1)

                split_odd(0, range(1, KD, 2))
                latent_scaled(0)
                kv_lo(0, 0)
                with dve.Fori(0, HEADS - 1) as h:
                    split_odd(h + 1, range(1, KD // 2, 2))
                    kv_lo(h, 1)
                    split_odd(h + 1, range(KD // 2 + 1, KD, 2))
                    latent_lo(h)
                    latent_scaled(h + 1)
                    copy_states(h)
                    kv_lo(h + 1, 0)
                kv_lo(HEADS - 1, 1)
                latent_lo(HEADS - 1)
                copy_states(HEADS - 1)

            @block.tensor
            def _(pe):
                def project(h, t):
                    pe.wait_ge(lo.sem, lo.at(h - 1, 3 * (t + 1)))
                    tok = slice(t * P, (t + 1) * P)
                    for k in range(KD):
                        if t == 0:
                            lo_made(pe, h, k)
                        mm3(nc, ps[:, t, 0:DK], ch[:, k, tok], cl[:, k, tok], wh[:, k, 0:DK], wl[:, k, 0:DK],
                            k == 0, k == KD - 1)
                        mm = mm3(nc, ps[:, 2 + t, :], ch[:, k, tok], cl[:, k, tok], wh[:, k, DK:WK],
                                 wl[:, k, DK:WK], k == 0, k == KD - 1)
                        if t == CT - 1 and k < KD - 1:
                            mm.then_inc(w_used.sem, 1)
                    mm.then_inc(proj.sem, 1)

                def make_states(h):
                    pe.wait_ge(lo.sem, lo.at(h, 3 * CT))
                    for d in range(2):
                        pe.wait_ge(copied[d].sem, copied[d].at(h, 0))
                        for dt in range(2):
                            for t in range(CT):
                                cols = slice(dt * P, (dt + 1) * P)
                                mm = mm3(nc, ps[:, 4 + 2 * d + dt, :], kh[:, d, t, cols], kl[:, d, t, cols],
                                         vh[:, t, :], vl[:, t, :], t == 0, t == CT - 1)
                        mm.then_inc(states.sem, 1)

                project(0, 0)
                with pe.Fori(0, HEADS - 1) as h:
                    project(h, 1)
                    project(h + 1, 0)
                    make_states(h)
                project(HEADS - 1, 1)
                make_states(HEADS - 1)


def phase_retention(nc, a, sem, scope_sb, ps, minus_half, one, cs, mod, vecs, hh, hl, s0_dram, head_dram, y_dram):
    with ExitStack() as st:
        sb = scope_sb(st)
        RAW = 4
        BLOCKS = 3
        raw = sb("raw2", [P, RAW, DV])
        wh = sb("wh2", [P, KD, DV], F32R)
        wl = sb("wl2", [P, KD, DV], F32R)
        qTh = sb("qTh", [P, 2, SEQ], F32R)
        qTl = sb("qTl", [P, 2, SEQ], F32R)
        kn = sb("kn", [P, NC, DK])
        vh = sb("vh2", [P, NC, DV], F32R)
        vl = sb("vl2", [P, NC, DV], F32R)
        y = sb("y", [P, NC, DV])
        S = sb("S", [P, 2, DV])
        Sh = sb("Sh", [P, 2, DV], F32R)
        Sl = sb("Sl", [P, 2, DV], F32R)
        kdh = sb("kdh", [P, DK], F32R)
        kdl = sb("kdl", [P, DK], F32R)
        cosr, sinr = sb("cosr", [P, NC, 64]), sb("sinr", [P, NC, 64])
        cosc, sinc = sb("cosc", [P, 64]), sb("sinc", [P, 64])
        ident = sb("ident2", [P, P])
        hd = sb("hd2", [P, DECAYS + P])
        gn = sb("gn", [P, DV])
        t1 = sb("t1", [P, DV])
        t2 = sb("t2", [P, DV])
        kTh = sb("kTh", [P, 2, P], F32R)
        kTl = sb("kTl", [P, 2, P], F32R)
        pf = sb("pf", [P, P])
        ph = sb("ph", [P, P], F32R)
        pl = sb("pl", [P, P], F32R)
        stats = sb("stats", [P, 6])
        mv = sb("mv", [P, 2])
        ve = sb("ve", [P, 1])
        rstd = sb("rstd", [P, 1])
        warm = sb("warm2", [P, 1])
        PT, SC, PV, QS, U = 2, 3, 4, 5, 6

        const_in = sem("ret_const_in")
        ADA = 2 * KD
        raw_in = [Tally(sem(f"ret_raw_in{q}"), (BLOCKS * KD + ADA) // RAW, unit=16) for q in range(RAW)]
        ada_step = Tally(sem("ret_ada_step"), ADA)
        ada_mm = Tally(sem("ret_ada_mm"), 1)
        ada_out = Tally(sem("ret_ada_out"), 1, credit=True)
        w_hi = Tally(sem("ret_w_hi"), BLOCKS * KD)
        w_lo = [Tally(sem(f"ret_w_lo_{n}"), BLOCKS * KD // 2, credit=True) for n in ("even", "odd")]
        w_used = Tally(sem("ret_w_used"), BLOCKS * (KD - 1), credit=True)
        proj = Tally(sem("ret_proj"), BLOCKS * NC, credit=True)
        hd_in = Tally(sem("ret_head_in"), 1, unit=16)
        gn_in = Tally(sem("ret_gn_in"), 1, unit=16)
        s_in = Tally(sem("ret_state_in"), 2, unit=16)
        rope_cos = Tally(sem("rope_cos"), 2 * NC)
        rope_sin = Tally(sem("rope_sin"), 2 * NC)
        rope_out = Tally(sem("rope_out"), 4 * NC)
        qT_mm = Tally(sem("qT_mm"), NC, credit=True)
        qT_hi = Tally(sem("qT_hi"), NC, credit=True)
        qT_lo = Tally(sem("qT_lo"), NC, credit=True)
        kT_mm = Tally(sem("kT_mm"), NC, credit=True)
        kT_hi = Tally(sem("kT_hi"), NC)
        kT_lo = Tally(sem("kT_lo"), NC, credit=True)
        kd_hi = Tally(sem("kd_hi"), 2 * (NC - 1))
        kd_lo = Tally(sem("kd_lo"), 2 * (NC - 1), credit=True)
        v_hi = Tally(sem("v_hi"), NC)
        v_lo = Tally(sem("v_lo"), NC)
        score_mm = Tally(sem("score_mm"), NC)
        p_f = Tally(sem("p_masked"), NC, credit=True)
        p_hi = Tally(sem("p_hi"), NC)
        p_lo = Tally(sem("p_lo"), NC, credit=True)
        qs_mm = Tally(sem("qs_mm"), 2 * NC, credit=True)
        pv_mm = Tally(sem("pv_mm"), NC, credit=True)
        y_pv = Tally(sem("y_pv"), NC, credit=True)
        y_f = Tally(sem("y_forward"), NC, credit=True)
        y_b = Tally(sem("y_backward"), NC, credit=True)
        u_mm = Tally(sem("u_mm"), 2 * (NC - 1), credit=True)
        s_f32 = Tally(sem("s_updated"), 2 * (NC - 1), credit=True)
        s_hi = Tally(sem("s_hi"), 2 * NC, credit=True)
        s_lo = Tally(sem("s_lo"), 2 * NC, credit=True)
        silu = Tally(sem("g_silu"), NC, credit=True)
        gated = Tally(sem("g_weighted"), NC, credit=True)
        st_done = Tally(sem("y_stats"), NC)
        ag_done = Tally(sem("y_mean_var"), NC)
        ve_done = Tally(sem("y_var_eps"), NC)
        rs_done = Tally(sem("y_rstd"), NC)
        yn_done = Tally(sem("y_normed"), NC, credit=True)
        yg_done = Tally(sem("y_gated"), NC, credit=True)
        stored = Tally(sem("y_stored"), NC, credit=True, unit=16)

        def order(d):
            return list(range(NC)) if d == 0 else list(range(NC - 1, -1, -1))

        def loaded(h, b, k):
            n = b * KD + k + (ADA if b else 0)
            return raw_in[k % RAW].at(h, n // RAW + 1)

        def lo_made(eng, h, n):
            w = w_lo[n % 2]
            eng.wait_ge(w.sem, w.at(h, n // 2 + 1))

        def load_slice(sp, h, b, k):
            if b == 1 and k < RAW:
                sp.wait_ge(ada_step.sem, ada_step.at(h, ADA - RAW + k + 1))
            else:
                lo_made(sp, h, b * KD + k - RAW)
            sp.dma_start(raw[:, k % RAW, :], a["ret_w"][bass.ds(h * BLOCKS + b, 1), k, :, :]
                         .rearrange("o p n -> (o p) n")).then_inc(raw_in[k % RAW].sem, 16)

        with nc.Block() as block:
            @block.sync
            def _(sp):
                pay(sp, *w_lo, w_used, proj, qT_mm, qT_hi, qT_lo, kT_mm, kT_lo, kd_lo, p_f, p_lo,
                    qs_mm, pv_mm, y_pv, y_f, y_b, u_mm, s_f32, s_hi, s_lo, silu, gated, yn_done, yg_done, stored, ada_out)
                for dst, name in ((cosr[:, :, :], "cosr"), (sinr[:, :, :], "sinr"), (cosc[:, :], "cosc"),
                                  (sinc[:, :], "sinc"), (ident[:, :], "ident")):
                    sp.dma_start(dst, a[name]).then_inc(const_in, 16)
                for k in range(KD):
                    load_slice(sp, 0, 0, k)
                with sp.Fori(0, HEADS) as h:
                    sp.wait_ge(y_b.sem, y_b.at(h, 0))
                    sp.dma_start(hd[:, :], head_dram[bass.ds(h, 1)].rearrange("o p n -> (o p) n")
                                 ).then_inc(hd_in.sem, 16)
                    sp.wait_ge(s_lo.sem, s_lo.at(h, 0))
                    sp.dma_start(S[:, :, :].rearrange("p t n -> p (t n)"), s0_dram[bass.ds(h, 1), 0]
                                 .rearrange("o p n -> (o p) n")).then_inc(s_in.sem, 16)
                    sp.wait_ge(gated.sem, gated.at(h, 0))
                    sp.dma_start(gn[:, :], a["gn"][bass.ds(h, 1)].rearrange("o p n -> (o p) n")
                                 ).then_inc(gn_in.sem, 16)
                    for n in range(ADA):
                        if n < RAW:
                            lo_made(sp, h, KD - RAW + n)
                        else:
                            sp.wait_ge(ada_step.sem, ada_step.at(h, n - RAW + 1))
                        sp.dma_start(raw[:, n % RAW, :], a["ada_rest"][bass.ds(h, 1), n]
                                     .rearrange("o p n -> (o p) n")).then_inc(raw_in[n % RAW].sem, 16)
                    for b in (1, 2):
                        for k in range(KD):
                            load_slice(sp, h, b, k)
                    sp.wait_ge(s_lo.sem, s_lo.at(h, NC))
                    sp.dma_start(S[:, :, :].rearrange("p t n -> p (t n)"), s0_dram[bass.ds(h, 1), 1]
                                 .rearrange("o p n -> (o p) n")).then_inc(s_in.sem, 16)
                    for k in range(KD):
                        load_slice(sp, h, BLOCKS, k)

            def split_hi(act, h, b, ks=range(KD)):
                for k in ks:
                    if k < KD - 1:
                        act.wait_ge(w_used.sem, w_used.at(h, (b - 1) * (KD - 1) + k + 1))
                    else:
                        act.wait_ge(proj.sem, proj.at(h, b * NC))
                    act.wait_ge(raw_in[k % RAW].sem, loaded(h, b, k))
                    nc.scalar.activation(wh[:, k, :], raw[:, k % RAW, :], ACT.Copy).then_inc(w_hi.sem, 1)

            def split_even(pool, h, b, ks=(0, 2, 4, 6)):
                for k in ks:
                    pool.wait_ge(w_hi.sem, w_hi.at(h, b * KD + k + 1))
                    nc.gpsimd.tensor_tensor(wl[:, k, :], raw[:, k % RAW, :], f32(wh[:, k, :]),
                                            ALU.subtract).then_inc(w_lo[0].sem, 1)

            def split_odd(dve, h, b, ks=(1, 3, 5, 7)):
                for k in ks:
                    dve.wait_ge(w_hi.sem, w_hi.at(h, b * KD + k + 1))
                    nc.vector.tensor_tensor(wl[:, k, :], raw[:, k % RAW, :], f32(wh[:, k, :]),
                                            ALU.subtract).then_inc(w_lo[1].sem, 1)

            @block.gpsimd
            def _(pool):
                split_even(pool, 0, 0)
                with pool.Fori(0, HEADS) as h:
                    for b in (1, 2):
                        split_even(pool, h, b)
                    for m, c in enumerate(order(1)):
                        if m == NC - 1:
                            split_even(pool, h, BLOCKS, (0, 2))
                        if m == 0:
                            pool.wait_ge(gn_in.sem, gn_in.at(h, 1))
                        pool.wait_ge(silu.sem, silu.at(h, m + 1))
                        nc.gpsimd.tensor_tensor(t1[:, :], t1[:, :], gn[:, :], ALU.mult).then_inc(gated.sem, 1)
                        if m == NC - 1:
                            split_even(pool, h, BLOCKS, (4, 6))
                        pool.wait_ge(ve_done.sem, ve_done.at(h, m + 1))
                        nc.gpsimd.tensor_tensor(rstd[:, :], ve[:, :], minus_half[:, :],
                                                ALU.pow).then_inc(rs_done.sem, 1)

            @block.scalar
            def _(act):
                act.wait_ge(const_in, 16 * 5)
                nc.scalar.activation(warm[:, :], minus_half[:, :], ACT.Silu)

                def split_state(h, d, m):
                    if m == 0:
                        act.wait_ge(s_in.sem, s_in.at(h, d + 1))
                    else:
                        act.wait_ge(s_f32.sem, s_f32.at(h, d * (NC - 1) + m))
                    act.wait_ge(qs_mm.sem, qs_mm.at(h, d * NC + m))
                    nc.scalar.activation(Sh[:, :, :], S[:, :, :], ACT.Copy).then_inc(s_hi.sem, 1)

                def decay_keys(h, d, m, c):
                    n = d * (NC - 1) + m
                    act.wait_ge(u_mm.sem, u_mm.at(h, n))
                    act.wait_ge(rope_out.sem, rope_out.at(h, 4 * (c + 1)))
                    e = F_K if d == 0 else B_K
                    nc.scalar.activation(kdh[:, :], kn[:, c, :], ACT.Copy,
                                         scale=hd[:, e:e + 1]).then_inc(kd_hi.sem, 1)

                def keys_turned(h, c):
                    act.wait_ge(kT_mm.sem, kT_mm.at(h, c + 1))
                    nc.scalar.activation(kTh[:, :, :], ps[:, SC, 0:DK].rearrange("p (t n) -> p t n", t=2),
                                         ACT.Copy).then_inc(kT_hi.sem, 1)

                split_hi(act, 0, 0)
                with act.Fori(0, HEADS) as h:
                    for c in range(NC):
                        if c == NC - 1:
                            split_hi(act, h, 1, range(KD // 2))
                        if c >= 1:
                            act.wait_ge(qT_mm.sem, qT_mm.at(h, c))
                            nc.scalar.activation(qTh[:, :, (c - 1) * P:c * P],
                                                 ps[:, PT, 0:DK].rearrange("p (t n) -> p t n", t=2),
                                                 ACT.Copy, scale=DK ** -0.5).then_inc(qT_hi.sem, 1)
                    split_hi(act, h, 1, range(KD // 2, KD))
                    act.wait_ge(hd_in.sem, hd_in.at(h, 1))
                    split_state(h, 0, 0)
                    for c in range(NC):
                        if c == NC - 1:
                            split_hi(act, h, 2, range(KD // 2))
                        if c < NC - 1:
                            decay_keys(h, 0, c, c)
                        if c == 0:
                            act.wait_ge(qT_mm.sem, qT_mm.at(h, NC))
                            nc.scalar.activation(qTh[:, :, (NC - 1) * P:NC * P],
                                                 ps[:, PT, 0:DK].rearrange("p (t n) -> p t n", t=2),
                                                 ACT.Copy, scale=DK ** -0.5).then_inc(qT_hi.sem, 1)
                            keys_turned(h, 0)
                        act.wait_ge(proj.sem, proj.at(h, NC + c + 1))
                        nc.scalar.activation(vh[:, c, :], ps[:, (NC + c) % 2, :], ACT.Copy).then_inc(v_hi.sem, 1)
                        act.wait_ge(p_f.sem, p_f.at(h, c + 1))
                        nc.scalar.activation(ph[:, :], pf[:, :], ACT.Copy).then_inc(p_hi.sem, 1)
                        act.wait_ge(pv_mm.sem, pv_mm.at(h, c + 1))
                        if c == 0:
                            act.wait_ge(stored.sem, stored.at(h, 0))
                        nc.scalar.activation(y[:, c, :], ps[:, PV, :], ACT.Copy).then_inc(y_pv.sem, 1)
                        if c < NC - 1:
                            keys_turned(h, c + 1)
                            split_state(h, 0, c + 1)
                    split_hi(act, h, 2, range(KD // 2, KD))
                    split_state(h, 1, 0)
                    for m, c in enumerate(order(1)):
                        if m == NC - 1:
                            split_hi(act, h, BLOCKS, range(KD // 2))
                        if m < NC - 1:
                            decay_keys(h, 1, m, c)
                        act.wait_ge(proj.sem, proj.at(h, 2 * NC + m + 1))
                        act.wait_ge(yg_done.sem, yg_done.at(h, m))
                        nc.scalar.activation(t1[:, :], ps[:, m % 2, :], ACT.Silu).then_inc(silu.sem, 1)
                        if m >= 1:
                            act.wait_ge(stored.sem, stored.at(h, m - 1))
                            act.dma_start(y_dram[c + 1, :, bass.ds(h * DV, DV)], y[:, c + 1, :]
                                          ).then_inc(stored.sem, 16)
                        if m < NC - 1:
                            split_state(h, 1, m + 1)
                    split_hi(act, h, BLOCKS, range(KD // 2, KD))
                    act.wait_ge(yg_done.sem, yg_done.at(h, NC))
                    act.wait_ge(stored.sem, stored.at(h, NC - 1))
                    act.dma_start(y_dram[0, :, bass.ds(h * DV, DV)], y[:, 0, :]).then_inc(stored.sem, 16)
                act.wait_ge(stored.sem, stored.at(HEADS - 1, NC))

            @block.vector
            def _(dve):
                def state_lo(h, d, m):
                    dve.wait_ge(s_hi.sem, s_hi.at(h, d * NC + m + 1))
                    nc.vector.tensor_tensor(Sl[:, :, :], S[:, :, :], f32(Sh[:, :, :]), ALU.subtract
                                            ).then_inc(s_lo.sem, 1)

                def keys_lo(h, d, m, c):
                    n = d * (NC - 1) + m
                    dve.wait_ge(kd_hi.sem, kd_hi.at(h, n + 1))
                    e = F_K if d == 0 else B_K
                    nc.vector.scalar_tensor_tensor(kdl[:, :], kn[:, c, :], hd[:, e:e + 1], f32(kdh[:, :]),
                                                   ALU.mult, ALU.subtract).then_inc(kd_lo.sem, 1)

                def update(h, d, m):
                    n = d * (NC - 1) + m
                    dve.wait_ge(s_lo.sem, s_lo.at(h, d * NC + m + 1))
                    dve.wait_ge(u_mm.sem, u_mm.at(h, n + 1))
                    e = F_CHUNK if d == 0 else B_CHUNK
                    nc.vector.scalar_tensor_tensor(S[:, :, :], S[:, :, :], hd[:, e:e + 1], ps[:, U:U + 2, :],
                                                   ALU.mult, ALU.add).then_inc(s_f32.sem, 1)

                def qT_lo_half(h, c):
                    dve.wait_ge(qT_hi.sem, qT_hi.at(h, c + 1))
                    nc.vector.scalar_tensor_tensor(qTl[:, :, c * P:(c + 1) * P],
                                                   ps[:, PT, 0:DK].rearrange("p (t n) -> p t n", t=2), DK ** -0.5,
                                                   f32(qTh[:, :, c * P:(c + 1) * P]), ALU.mult,
                                                   ALU.subtract).then_inc(qT_lo.sem, 1)

                def keys_turned_lo(h, c):
                    dve.wait_ge(kT_hi.sem, kT_hi.at(h, c + 1))
                    nc.vector.tensor_tensor(kTl[:, :, :], ps[:, SC, 0:DK].rearrange("p (t n) -> p t n", t=2),
                                            f32(kTh[:, :, :]), ALU.subtract).then_inc(kT_lo.sem, 1)

                dve.wait_ge(const_in, 16 * 5)
                split_odd(dve, 0, 0)
                with dve.Fori(0, HEADS) as h:
                    for c in range(NC):
                        if c == NC - 1:
                            split_odd(dve, h, 1, (1, 3))
                        dve.wait_ge(proj.sem, proj.at(h, c + 1))
                        if c == 0:
                            dve.wait_ge(yg_done.sem, yg_done.at(h, 0))
                        else:
                            dve.wait_ge(qT_mm.sem, qT_mm.at(h, c))
                            dve.wait_ge(rope_out.sem, rope_out.at(h, 4 * c))
                        src = ps[:, c % 2, :].rearrange("p (s f x n) -> p s f x n", s=2, f=2, x=2)
                        v1 = t1[:, :].rearrange("p (s f x n) -> p s f x n", s=2, f=2, x=2)
                        v2 = t2[:, :].rearrange("p (s f x n) -> p s f x n", s=2, f=2, x=2)
                        for f, (co, si) in enumerate(((cosr[:, c, :], sinr[:, c, :]), (cosc[:, :], sinc[:, :]))):
                            rep = lambda ap: ap.unsqueeze(1).unsqueeze(1).broadcast_to([P, 2, 2, 64])
                            nc.vector.tensor_tensor(v1[:, :, f], src[:, :, f], rep(co),
                                                    ALU.mult).then_inc(rope_cos.sem, 1)
                            nc.vector.tensor_tensor(v2[:, :, f], src[:, :, f, ::-1, :], rep(si),
                                                    ALU.mult).then_inc(rope_sin.sem, 1)
                        dve.wait_ge(rope_cos.sem, rope_cos.at(h, 2 * c + 2))
                        dve.wait_ge(rope_sin.sem, rope_sin.at(h, 2 * c + 2))
                        kout = kn[:, c, :].rearrange("p (f x n) -> p f x n", f=2, x=2)
                        for s, dst in enumerate((v1[:, 0], kout)):
                            for x, op in enumerate((ALU.subtract, ALU.add)):
                                nc.vector.tensor_tensor(dst[:, :, x], v1[:, s, :, x], v2[:, s, :, x],
                                                               op).then_inc(rope_out.sem, 1)
                        if c == NC - 1:
                            split_odd(dve, h, 1, (5,))
                        if c >= 1:
                            qT_lo_half(h, c - 1)
                        if c == 0:
                            dve.wait_ge(stored.sem, stored.at(h, 2 - NC))
                        for n in range(3 * c, min(3 * c + 3, ADA)):
                            q, k = n // KD, n % KD
                            acc = y[:, NC - 2 + q, :]
                            dve.wait_ge(raw_in[n % RAW].sem, raw_in[n % RAW].at(h, (KD + n) // RAW + 1))
                            if k == 0:
                                nc.vector.tensor_scalar(acc, raw[:, n % RAW, :], cs[:, 0, 0:1], None,
                                                        ALU.mult).then_inc(ada_step.sem, 1)
                            else:
                                dve.wait_ge(ada_step.sem, ada_step.at(h, n))
                                nc.vector.scalar_tensor_tensor(acc, raw[:, n % RAW, :], cs[:, k, 0:1], acc,
                                                               ALU.mult, ALU.add).then_inc(ada_step.sem, 1)
                    split_odd(dve, h, 1, (7,))
                    dve.wait_ge(hd_in.sem, hd_in.at(h, 1))
                    state_lo(h, 0, 0)
                    for c in range(NC):
                        if c == NC - 1:
                            split_odd(dve, h, 2, (1, 3))
                        if c < NC - 1:
                            keys_lo(h, 0, c, c)
                        if c == 0:
                            qT_lo_half(h, NC - 1)
                            keys_turned_lo(h, 0)
                        dve.wait_ge(v_hi.sem, v_hi.at(h, c + 1))
                        nc.vector.tensor_tensor(vl[:, c, :], ps[:, (NC + c) % 2, :], f32(vh[:, c, :]),
                                                ALU.subtract).then_inc(v_lo.sem, 1)
                        if c == 1:
                            dve.wait_ge(ada_mm.sem, ada_mm.at(h, 1))
                            nc.vector.tensor_tensor(mod[:, bass.ds(h * 8 + 16, 8), 0], ps[:, PT, 0:8],
                                                    vecs[:, bass.ds(h * 8 + (V_AB + 16), 8)], ALU.add
                                                    ).then_inc(ada_out.sem, 1)
                        dve.wait_ge(score_mm.sem, score_mm.at(h, c + 1))
                        dve.wait_ge(p_lo.sem, p_lo.at(h, c))
                        nc.vector.tensor_tensor(pf[:, :], ps[:, SC, 0:P], hd[:, DECAYS:], ALU.mult
                                                ).then_inc(p_f.sem, 1)
                        dve.wait_ge(p_hi.sem, p_hi.at(h, c + 1))
                        nc.vector.tensor_tensor(pl[:, :], pf[:, :], f32(ph[:, :]), ALU.subtract
                                                ).then_inc(p_lo.sem, 1)
                        dve.wait_ge(qs_mm.sem, qs_mm.at(h, c + 1))
                        dve.wait_ge(y_pv.sem, y_pv.at(h, c + 1))
                        nc.vector.scalar_tensor_tensor(y[:, c, :], ps[:, QS, :], hd[:, F_Q:F_Q + 1], y[:, c, :],
                                                       ALU.mult, ALU.add).then_inc(y_f.sem, 1)
                        if c < NC - 1:
                            keys_turned_lo(h, c + 1)
                            update(h, 0, c)
                            state_lo(h, 0, c + 1)
                    split_odd(dve, h, 2, (5, 7))
                    state_lo(h, 1, 0)
                    for m, c in enumerate(order(1)):
                        if m == NC - 1:
                            split_odd(dve, h, BLOCKS, (1, 3))
                        if m < NC - 1:
                            keys_lo(h, 1, m, c)
                        dve.wait_ge(qs_mm.sem, qs_mm.at(h, NC + m + 1))
                        if m == 0:
                            dve.wait_ge(y_f.sem, y_f.at(h, NC))
                        nc.vector.scalar_tensor_tensor(y[:, c, :], ps[:, QS, :], hd[:, B_Q:B_Q + 1], y[:, c, :],
                                                       ALU.mult, ALU.add).then_inc(y_b.sem, 1)
                        if m < NC - 1:
                            update(h, 1, m)
                        dve.wait_ge(y_b.sem, y_b.at(h, m + 1))
                        nc.vector.bn_stats(stats[:, :], y[:, c, :]).then_inc(st_done.sem, 1)
                        dve.wait_ge(st_done.sem, st_done.at(h, m + 1))
                        if m < NC - 1:
                            state_lo(h, 1, m + 1)
                        else:
                            nc.vector.memset(ve[:, :], 0.0)
                        nc.vector.bn_aggr(mv[:, :], stats[:, :]).then_inc(ag_done.sem, 1)
                        dve.wait_ge(ag_done.sem, ag_done.at(h, m + 1))
                        nc.vector.tensor_scalar(ve[:, :], mv[:, 1:2], GN_EPS, None, ALU.add).then_inc(ve_done.sem, 1)
                        if m == NC - 1:
                            split_odd(dve, h, BLOCKS, (5, 7))
                        dve.wait_ge(rs_done.sem, rs_done.at(h, m + 1))
                        nc.vector.tensor_scalar(y[:, c, :], y[:, c, :], mv[:, 0:1], rstd[:, :], ALU.subtract,
                                                ALU.mult).then_inc(yn_done.sem, 1)
                        dve.wait_ge(yn_done.sem, yn_done.at(h, m + 1))
                        dve.wait_ge(gated.sem, gated.at(h, m + 1))
                        nc.vector.tensor_tensor(y[:, c, :], y[:, c, :], t1[:, :], ALU.mult).then_inc(yg_done.sem, 1)

            @block.tensor
            def _(pe):
                def project(h, b, m, c):
                    n = b * NC + m
                    if 2 <= n < NC + 2:
                        pe.wait_ge(rope_sin.sem, rope_sin.at(h, 2 * (n - 1)))
                    elif NC + 2 <= n < 2 * NC + 2:
                        pe.wait_ge(v_lo.sem, v_lo.at(h, n - 1 - NC))
                    else:
                        pe.wait_ge(silu.sem, silu.at(h, n - 1 - 2 * NC if n >= 2 else n - 1))
                    tok = slice(c * P, (c + 1) * P)
                    for k in range(KD):
                        if b == 1 and m == 0 and k == 5:
                            turn_q(h, NC - 1)
                            turn_k(h, 0)
                        if m == 0:
                            lo_made(pe, h, b * KD + k)
                        mm = mm3(nc, ps[:, n % 2, :], hh[:, k, tok], hl[:, k, tok], wh[:, k, :], wl[:, k, :],
                                 k == 0, k == KD - 1)
                        if m == NC - 1 and k < KD - 1:
                            mm.then_inc(w_used.sem, 1)
                    mm.then_inc(proj.sem, 1)

                def turn_q(h, c):
                    pe.wait_ge(rope_out.sem, rope_out.at(h, 4 * c + 2))
                    pe.wait_ge(qT_lo.sem, qT_lo.at(h, c))
                    if c == 0:
                        pe.wait_ge(ada_out.sem, ada_out.at(h, 0))
                    for t in range(2):
                        mm = nc.tensor.transpose(ps[:, PT, t * P:(t + 1) * P], t1[:, t * P:(t + 1) * P], ident[:, :])
                    mm.then_inc(qT_mm.sem, 1)

                def turn_k(h, c):
                    pe.wait_ge(p_f.sem, p_f.at(h, c))
                    pe.wait_ge(rope_out.sem, rope_out.at(h, 4 * c + 4))
                    for t in range(2):
                        mm = nc.tensor.transpose(ps[:, SC, t * P:(t + 1) * P], kn[:, c, t * P:(t + 1) * P], ident[:, :])
                    mm.then_inc(kT_mm.sem, 1)

                def read_state(h, d, m, c):
                    pe.wait_ge(s_lo.sem, s_lo.at(h, d * NC + m + 1))
                    if d == 0:
                        pe.wait_ge(y_b.sem, y_b.at(h, 0)) if m == 0 else pe.wait_ge(y_f.sem, y_f.at(h, m))
                    else:
                        pe.wait_ge(y_f.sem, y_f.at(h, NC)) if m == 0 else pe.wait_ge(y_b.sem, y_b.at(h, m))
                    for t in range(2):
                        mm = mm3(nc, ps[:, QS, :], qTh[:, t, c * P:(c + 1) * P], qTl[:, t, c * P:(c + 1) * P],
                                 Sh[:, t, :], Sl[:, t, :], t == 0, t == 1)
                    mm.then_inc(qs_mm.sem, 1)

                def make_update(h, d, m, c):
                    n = d * (NC - 1) + m
                    pe.wait_ge(kd_lo.sem, kd_lo.at(h, n + 1))
                    pe.wait_ge(s_f32.sem, s_f32.at(h, n))
                    for t in range(2):
                        mm = mm3(nc, ps[:, U + t, :], kdh[:, t * P:(t + 1) * P], kdl[:, t * P:(t + 1) * P],
                                 vh[:, c, :], vl[:, c, :], True, True)
                    mm.then_inc(u_mm.sem, 1)

                pe.wait_ge(const_in, 16 * 5)
                with pe.Fori(0, HEADS) as h:
                    for c in range(NC):
                        project(h, 0, c, c)
                        if c >= 1:
                            turn_q(h, c - 1)
                    for c in range(NC):
                        project(h, 1, c, c)
                        pe.wait_ge(kT_lo.sem, kT_lo.at(h, c + 1))
                        if c == 0:
                            pe.wait_ge(qT_lo.sem, qT_lo.at(h, NC))
                        pe.wait_ge(p_f.sem, p_f.at(h, c))
                        for t in range(2):
                            mm = mm3(nc, ps[:, SC, 0:P], kTh[:, t, :], kTl[:, t, :], qTh[:, t, c * P:(c + 1) * P],
                                     qTl[:, t, c * P:(c + 1) * P], t == 0, t == 1)
                        mm.then_inc(score_mm.sem, 1)
                        if c == 1:
                            pe.wait_ge(ada_step.sem, ada_step.at(h, ADA))
                            for t in range(8):
                                mm = nc.tensor.matmul(ps[:, PT, t:t + 1],
                                                      y[:, NC - 2 + t // 4, (t % 4) * P:(t % 4 + 1) * P], one[:, :],
                                                      start=True, stop=True)
                            mm.then_inc(ada_mm.sem, 1)
                        read_state(h, 0, c, c)
                        pe.wait_ge(p_lo.sem, p_lo.at(h, c + 1))
                        pe.wait_ge(v_lo.sem, v_lo.at(h, c + 1))
                        pe.wait_ge(y_pv.sem, y_pv.at(h, c))
                        mm3(nc, ps[:, PV, :], ph[:, :], pl[:, :], vh[:, c, :], vl[:, c, :], True,
                            True).then_inc(pv_mm.sem, 1)
                        if c < NC - 1:
                            turn_k(h, c + 1)
                            make_update(h, 0, c, c)
                    for m, c in enumerate(order(1)):
                        project(h, 2, m, c)
                        read_state(h, 1, m, c)
                        if m < NC - 1:
                            make_update(h, 1, m, c)


def phase_retention_out(nc, a, sem, scope_sb, ps, part, x, y_dram, gain, mod, vecs):
    with ExitStack() as st:
        sb = scope_sb(st)
        RAW = 4
        SL = KV // RAW
        yn = sb("yn", [P, 2, HEADS * DV])
        yh = sb("yh", [P, KV, SEQ], F32R)
        yl = sb("yl", [P, KV, SEQ], F32R)
        raw = sb("raw3", [P, RAW, SL, P])
        wh = sb("wh3", [P, RAW, SL, P], F32R)
        wl = sb("wl3", [P, RAW, SL, P], F32R)
        ident = sb("ident3", [P, P])

        ident_in, x_in = sem("ident_in"), sem("x_in3")
        y_in = [sem(f"y_in{q}") for q in range(2)]
        turned, turned_hi, turned_lo = sem("y_turned"), sem("y_turned_hi"), sem("y_turned_lo")
        raw_in = [Tally(sem(f"out_raw_in{q}"), 1, unit=16) for q in range(RAW)]
        w_hi = Tally(sem("out_w_hi"), RAW)
        w_lo = Tally(sem("out_w_lo"), RAW, credit=True)
        out_mm = Tally(sem("out_mm"), 1, credit=True)
        w_used = Tally(sem("out_w_used"), RAW - 1, credit=True)
        added = sem("out_added")
        GROUPS = NC * RAW

        with nc.Block() as block:
            @block.sync
            def _(sp):
                pay(sp, w_lo, w_used, out_mm)
                sp.sem_inc(added, 2)
                sp.dma_start(ident[:, :], a["ident"]).then_inc(ident_in, 16)
                for c in range(NC):
                    if c >= 2:
                        sp.wait_ge(turned, RAW * (c - 1))
                    sp.dma_start(yn[:, c % 2, :], y_dram[c]).then_inc(y_in[c % 2], 16)
                sp.dma_start(x[:, :, :], a["xT"]).then_inc(x_in, 16)
                with sp.Fori(0, KD) as m:
                    for q in range(RAW):
                        sp.wait_ge(w_lo.sem, w_lo.at(m, q + 1 - RAW))
                        sp.dma_start(raw[:, q, :, :], a["ret_out"][bass.ds(m, 1), q]
                                     .rearrange("o p t n -> (o p) t n")).then_inc(raw_in[q].sem, 16)

            @block.gpsimd
            def _(pool):
                with pool.Fori(0, KD) as m:
                    for q in range(RAW):
                        pool.wait_ge(w_hi.sem, w_hi.at(m, q + 1))
                        nc.gpsimd.tensor_tensor(wl[:, q], raw[:, q], f32(wh[:, q]), ALU.subtract).then_inc(w_lo.sem, 1)

            @block.scalar
            def _(act):
                for g in range(GROUPS):
                    c, q = g // RAW, g % RAW
                    act.wait_ge(turned, g + 1)
                    nc.scalar.activation(yh[:, q * SL:(q + 1) * SL, c * P:(c + 1) * P],
                                         ps[:, q, :].rearrange("p (t n) -> p t n", n=P), ACT.Copy
                                         ).then_inc(turned_hi, 1)
                with act.Fori(0, KD) as m:
                    for q in range(RAW):
                        if q < RAW - 1:
                            act.wait_ge(w_used.sem, w_used.at(m, q + 1 - (RAW - 1)))
                        else:
                            act.wait_ge(out_mm.sem, out_mm.at(m, 0))
                        act.wait_ge(raw_in[q].sem, raw_in[q].at(m, 1))
                        nc.scalar.activation(wh[:, q], raw[:, q], ACT.Copy).then_inc(w_hi.sem, 1)

            @block.vector
            def _(dve):
                make_gain(nc, gain, mod, vecs, 1, 0, 4, 0, V_N2).then_inc(sem("gain1"), 1)
                for g in range(GROUPS):
                    c, q = g // RAW, g % RAW
                    dve.wait_ge(turned_hi, g + 1)
                    nc.vector.tensor_tensor(yl[:, q * SL:(q + 1) * SL, c * P:(c + 1) * P],
                                            ps[:, q, :].rearrange("p (t n) -> p t n", n=P),
                                            f32(yh[:, q * SL:(q + 1) * SL, c * P:(c + 1) * P]),
                                            ALU.subtract).then_inc(turned_lo, 1)
                dve.wait_ge(x_in, 16)
                for m in range(KD):
                    b = 4 + 2 * (m % 2)
                    dve.wait_ge(out_mm.sem, out_mm.at(m, 1))
                    nc.vector.scalar_tensor_tensor(x[:, m, :], ps[:, b:b + 2, :].rearrange("p s n -> p (s n)"),
                                                   part(0, 2)(m), x[:, m, :], ALU.mult, ALU.add
                                                   ).then_inc(added, 1)

            @block.tensor
            def _(pe):
                pe.wait_ge(ident_in, 16)
                for g in range(GROUPS):
                    c, q = g // RAW, g % RAW
                    if q == 0:
                        pe.wait_ge(y_in[c % 2], 16 * (c // 2 + 1))
                    if g >= RAW:
                        pe.wait_ge(turned_lo, g + 1 - RAW)
                    for t in range(SL):
                        e = (q * SL + t) * P
                        mm = nc.tensor.transpose(ps[:, q, t * P:(t + 1) * P], yn[:, c % 2, e:e + P], ident[:, :])
                    mm.then_inc(turned, 1)
                pe.wait_ge(turned_lo, GROUPS)
                with pe.Fori(0, KD // 2) as i:
                    for r in range(2):
                        m = i * 2 + r
                        b = 4 + 2 * r
                        pe.wait_ge(added, i * 2 + (r + 1))
                        for q in range(RAW):
                            pe.wait_ge(w_lo.sem, w_lo.at(m, q + 1))
                            for t in range(SL):
                                kt = q * SL + t
                                for s in range(2):
                                    tok = slice(s * HALF, (s + 1) * HALF)
                                    mm = mm3(nc, ps[:, b + s, :], wh[:, q, t, :], wl[:, q, t, :], yh[:, kt, tok],
                                             yl[:, kt, tok], kt == 0, kt == KV - 1)
                            if q < RAW - 1:
                                mm.then_inc(w_used.sem, 1)
                        mm.then_inc(out_mm.sem, 1)


class Ffn:

    A0, O0, O1, B0, A1, B1 = range(6)
    SLOT = {A0: 0, B0: 1, A1: 2, B1: 3}

    def __init__(self, sem, keep):
        self.raw = keep("ffn_raw", [P, 3, KD * P])
        self.wih = keep("ffn_wih", [P, 4, KD * P], F32R)
        self.wil = keep("ffn_wil", [P, 4, KD * P], F32R)
        self.raw_in = [sem(f"ffn_raw_in{q}") for q in range(3)]
        self.w_hi, self.w_lo = sem("ffn_w_hi"), sem("ffn_w_lo")
        self.in_mm = Tally(sem("ffn_in_mm"), 4)
        self.silu = Tally(sem("ffn_silu"), 2)
        self.u = Tally(sem("ffn_u"), 2)
        self.u_hi = Tally(sem("ffn_u_hi"), 2)
        self.u_lo = Tally(sem("ffn_u_lo"), 2)
        self.out_mm = Tally(sem("ffn_out_mm"), KD, credit=True)
        self.added = Tally(sem("ffn_added"), KD, credit=True)
        self.ada_in = [Tally(sem(f"ffn_ada_in{q}"), 1, unit=16) for q in range(2)]
        self.ada_step = Tally(sem("ffn_ada_step"), KD)
        self.ada_mm = Tally(sem("ffn_ada_mm"), 1)
        self.ada_out = Tally(sem("ffn_ada_out"), 1)
        self.gains = sem("ffn_gains")

    def split(self, j, r):
        if isinstance(j, int) and j == 0:
            return {self.A0: 1, self.B0: 2, self.A1: 3, self.B1: 4}[r]
        if isinstance(j, int) and j == 2 * IT:
            return j * 6 + r - 2
        return j * 6 + (r - 1)

    def loaded(self, j, r):
        if isinstance(j, int) and j == 0:
            return 16 * {self.A0: 1, self.B0: 2, self.A1: 1, self.B1: 1}[r]
        return j * 32 + 16 * (r // 3 + 1 - (r % 3 > 0))


def phase_ffn(nc, a, scope_sb, ps, norms, f, layer, part, gain, minus_half, x, cond):
    cs, one, mod, vecs, gps = cond
    with ExitStack() as st:
        sb = scope_sb(st)
        hh = sb(f"fhh{layer}", [P, KD, SEQ], F32R)
        hl = sb(f"fhl{layer}", [P, KD, SEQ], F32R)
        with ExitStack() as tmp:
            nb = norms.buffers(scope_sb(tmp), f"fn{layer}", SEQ)
            run_norm(nc, norms, 2 + 2 * layer, nb, a["ident"], ps, x, gain[:, 1 + 2 * layer, :], part(layer, 3), minus_half,
                     lambda k: hh[:, k, :], hl, hh)
        raw, wih, wil = f.raw, f.wih, f.wil
        woh = sb(f"woh{layer}", [P, 2, D], F32R)
        wol = sb(f"wol{layer}", [P, 2, D], F32R)
        uf = sb(f"uf{layer}", [P, 2, SEQ])
        uh = sb(f"uh{layer}", [P, 2, SEQ], F32R)
        ul = sb(f"ul{layer}", [P, 2, SEQ], F32R)
        ada = None if layer else sb("ada1", [P, 2, KD // 2, 512])
        asum = None if layer else sb("ada1_sum", [P, 512])
        INB, OUTB = 0, 4
        j0 = IT * layer
        last = layer == 1

        def halves_of(r):
            if r in (f.O0, f.O1):
                return woh[:, r - f.O0, :], wol[:, r - f.O0, :]
            return wih[:, f.SLOT[r], :], wil[:, f.SLOT[r], :]

        def before(j, r):
            return (j, r - 3) if r >= 3 else (j - 1, r + 3)

        first_rs = (f.A0, f.B0, f.A1, f.B1)
        all_rs = tuple(range(6))
        end_rs = (f.O0, f.O1)

        def blocks(eng, do, ada_block=None):
            if not last:
                for r in first_rs:
                    do(0, r)
            with eng.Fori(j0 + 1, j0 + IT + (0 if last else 1)) as j:
                for r in all_rs:
                    do(j, r)
                    if ada_block is not None and r == f.B0:
                        ada_block(j)
            if last:
                for r in end_rs:
                    do(2 * IT, r)

        with nc.Block() as block:
            @block.sync
            def _(sp):
                if not last:
                    pay(sp, f.out_mm, f.added)

                def load(j, r):
                    if not (isinstance(j, int) and j == 0 and r in (f.A0, f.A1, f.B1)):
                        sp.wait_ge(f.w_lo, f.split(*before(j, r)))
                    src = a["ffn"][j, r] if isinstance(j, int) else a["ffn"][bass.ds(j, 1), r].rearrange(
                        "o p n -> (o p) n")
                    sp.dma_start(raw[:, r % 3, :], src).then_inc(f.raw_in[r % 3], 16)

                def load_ada(n):
                    for q in range(2):
                        if not (isinstance(n, int) and n == 0):
                            sp.wait_ge(f.ada_step.sem, f.ada_step.at(n - 1, (q + 1) * KD // 2))
                        src = a["ada_layer1"][n, q] if isinstance(n, int) else a["ada_layer1"][
                            bass.ds(n, 1), q].rearrange("o p k n -> (o p) k n")
                        sp.dma_start(ada[:, q, :, :], src).then_inc(f.ada_in[q].sem, 16)

                if not last:
                    load_ada(0)
                blocks(sp, load, None if last else load_ada)

            @block.gpsimd
            def _(pool):
                def split_lo(j, r):
                    hi, lo = halves_of(r)
                    pool.wait_ge(f.w_hi, f.split(j, r))
                    nc.gpsimd.tensor_tensor(lo, raw[:, r % 3, :], f32(hi), ALU.subtract).then_inc(f.w_lo, 1)
                blocks(pool, split_lo)

            @block.scalar
            def _(act):
                def split_hi(j, r):
                    hi, lo = halves_of(r)
                    if r in (f.O0, f.O1):
                        act.wait_ge(f.out_mm.sem, f.out_mm.at(j - 1, 0))
                    elif not (isinstance(j, int) and j == 0):
                        act.wait_ge(f.in_mm.sem, f.in_mm.at(j - 1, f.SLOT[r] + 1))
                    act.wait_ge(f.raw_in[r % 3], f.loaded(j, r))
                    nc.scalar.activation(hi, raw[:, r % 3, :], ACT.Copy).then_inc(f.w_hi, 1)

                def gate(i, t):
                    act.wait_ge(f.in_mm.sem, f.in_mm.at(i, 2 * t + 1))
                    nc.scalar.activation(uf[:, t, :], ps[:, INB:INB + 2, :].rearrange("p s n -> p (s n)"),
                                         ACT.Silu).then_inc(f.silu.sem, 1)

                def u_hi(i, t):
                    act.wait_ge(f.u.sem, f.u.at(i, t + 1))
                    nc.scalar.activation(uh[:, t, :], uf[:, t, :], ACT.Copy).then_inc(f.u_hi.sem, 1)

                def iteration(i, rs):
                    gate(i, 0)
                    for r in rs:
                        if r in (f.A0, f.O0, f.O1):
                            split_hi(i + 1, r)
                    u_hi(i, 0)
                    if f.B0 in rs:
                        split_hi(i + 1, f.B0)
                    gate(i, 1)
                    if f.A1 in rs:
                        split_hi(i + 1, f.A1)
                    u_hi(i, 1)
                    if f.B1 in rs:
                        split_hi(i + 1, f.B1)

                if not last:
                    for r in first_rs:
                        split_hi(0, r)
                with act.Fori(j0, j0 + IT - (1 if last else 0)) as i:
                    iteration(i, all_rs)
                if last:
                    iteration(2 * IT - 1, end_rs)

            @block.vector
            def _(dve):
                def output(i):
                    for m in range(KD):
                        b = OUTB + 2 * (m % 2)
                        dve.wait_ge(f.out_mm.sem, f.out_mm.at(i, m + 1))
                        nc.vector.scalar_tensor_tensor(x[:, m, :], ps[:, b:b + 2, :].rearrange("p s n -> p (s n)"),
                                                       part(layer, 5)(m), x[:, m, :], ALU.mult, ALU.add
                                                       ).then_inc(f.added.sem, 1)

                def product(i, t):
                    dve.wait_ge(f.in_mm.sem, f.in_mm.at(i, 2 * t + 2))
                    dve.wait_ge(f.silu.sem, f.silu.at(i, t + 1))
                    nc.vector.tensor_tensor(uf[:, t, :], ps[:, INB + 2:INB + 4, :].rearrange("p s n -> p (s n)"),
                                            uf[:, t, :], ALU.mult).then_inc(f.u.sem, 1)
                    dve.wait_ge(f.u_hi.sem, f.u_hi.at(i, t + 1))
                    nc.vector.tensor_tensor(ul[:, t, :], uf[:, t, :], f32(uh[:, t, :]), ALU.subtract
                                            ).then_inc(f.u_lo.sem, 1)

                def ada_sum(n):
                    for k in range(KD):
                        if k % (KD // 2) == 0:
                            dve.wait_ge(f.ada_in[k * 2 // KD].sem, f.ada_in[k * 2 // KD].at(n, 1))
                        w = ada[:, k * 2 // KD, k % (KD // 2), :]
                        if k == 0:
                            if not (isinstance(n, int) and n == 0):
                                dve.wait_ge(f.ada_mm.sem, f.ada_mm.at(n - 1, 1))
                            nc.vector.tensor_scalar(asum[:, :], w, cs[:, 0, 0:1], None, ALU.mult
                                                    ).then_inc(f.ada_step.sem, 1)
                        else:
                            dve.wait_ge(f.ada_step.sem, f.ada_step.at(n, k))
                            nc.vector.scalar_tensor_tensor(asum[:, :], w, cs[:, k, 0:1], asum[:, :], ALU.mult, ALU.add
                                                           ).then_inc(f.ada_step.sem, 1)

                def ada_add(n):
                    dve.wait_ge(f.ada_mm.sem, f.ada_mm.at(n, 1))
                    to, bias = ((mod[:, 48 + 4 * n:52 + 4 * n, 0], vecs[:, V_AB + 48 + 4 * n:V_AB + 52 + 4 * n])
                                if isinstance(n, int) else
                                (mod[:, bass.ds(n * 4 + 48, 4), 0], vecs[:, bass.ds(n * 4 + (V_AB + 48), 4)]))
                    nc.vector.tensor_tensor(to, ps[:, OUTB + 3, 0:4], bias, ALU.add).then_inc(f.ada_out.sem, 1)

                if not last:
                    ada_sum(0)
                    ada_add(0)
                for t in range(2):
                    product(j0, t)
                with dve.Fori(j0 + 1, j0 + IT) as i:
                    if not last:
                        ada_sum(i)
                        ada_add(i)
                    output(i - 1)
                    for t in range(2):
                        product(i, t)
                if not last:
                    ada_sum(ADA_LAYER1 - 1)
                    ada_add(ADA_LAYER1 - 1)
                output(j0 + IT - 1)
                dve.wait_ge(f.added.sem, f.added.at(j0 + IT - 1, KD))
                if not last:
                    dve.wait_ge(f.ada_out.sem, f.ada_out.at(ADA_LAYER1 - 1, 1))
                    make_gain(nc, gain, mod, vecs, 2, 1, 1, 0, V_N1 + 8).then_inc(f.gains, 1)
                    make_gain(nc, gain, mod, vecs, 3, 1, 4, 0, V_N2 + 8).then_inc(f.gains, 1)
                    nc.vector.tensor_tensor(gps[:, :], mod[:, 48 + 16:48 + 24, 0], vecs[:, V_PS:V_PS + 8],
                                            ALU.mult).then_inc(f.gains, 1)

            @block.tensor
            def _(pe):
                def project(i, n):
                    r = (f.A0, f.B0, f.A1, f.B1)[n]
                    pe.wait_ge(f.w_lo, f.split(i, r))
                    if n >= 2:
                        pe.wait_ge((f.silu, f.u)[n % 2].sem, (f.silu, f.u)[n % 2].at(i, 1))
                    elif not (isinstance(i, int) and i == 0):
                        pe.wait_ge((f.silu, f.u)[n % 2].sem, (f.silu, f.u)[n % 2].at(i, 0))
                    for k in range(KD):
                        for s in range(2):
                            tok = slice(s * HALF, (s + 1) * HALF)
                            cols = slice(k * P, (k + 1) * P)
                            mm = mm3(nc, ps[:, INB + 2 * (n % 2) + s, :], wih[:, n, cols], wil[:, n, cols],
                                     hh[:, k, tok], hl[:, k, tok], k == 0, k == KD - 1)
                    mm.then_inc(f.in_mm.sem, 1)

                def output(i):
                    pe.wait_ge(f.u_lo.sem, f.u_lo.at(i, 2))
                    pe.wait_ge(f.w_lo, f.split(i + 1, f.O1))
                    for m in range(KD):
                        pe.wait_ge(f.added.sem, f.added.at(i, m - 1))
                        if m == 1 and not last:
                            pe.wait_ge(f.ada_out.sem, f.ada_out.at(i + 1, 1))
                        for s in range(2):
                            tok = slice(s * HALF, (s + 1) * HALF)
                            cols = slice(m * P, (m + 1) * P)
                            for t in range(2):
                                mm = mm3(nc, ps[:, OUTB + 2 * (m % 2) + s, :], woh[:, t, cols], wol[:, t, cols],
                                         uh[:, t, tok], ul[:, t, tok], t == 0, t == 1)
                        mm.then_inc(f.out_mm.sem, 1)

                def ada_turn(n):
                    pe.wait_ge(f.ada_step.sem, f.ada_step.at(n, KD))
                    if not (isinstance(n, int) and n == 0):
                        pe.wait_ge(f.added.sem, f.added.at(n - 2, KD))
                    for t in range(4):
                        mm = nc.tensor.matmul(ps[:, OUTB + 3, t:t + 1], asum[:, t * P:(t + 1) * P], one[:, :],
                                              start=True, stop=True)
                    mm.then_inc(f.ada_mm.sem, 1)

                if not last:
                    ada_turn(0)
                for n in range(4):
                    project(j0, n)
                with pe.Fori(j0 + 1, j0 + IT) as i:
                    project(i, 0)
                    if not last:
                        ada_turn(i)
                    output(i - 1)
                    for n in range(1, 4):
                        project(i, n)
                if not last:
                    ada_turn(ADA_LAYER1 - 1)
                output(j0 + IT - 1)


def run_norm(nc, norms, r, nb, ident, ps, x, gain, shift, minus_half, out, lo, hi):
    with nc.Block() as block:
        @block.sync
        def _(sp):
            norms.load(sp, nb, ident, r)

        @block.scalar
        def _(act):
            norms.act_squares(nc, act, r, nb, x)
            norms.act_shift(nc, act, r, nb, shift, out)

        @block.vector
        def _(dve):
            norms.dve_ones(nc, nb)
            norms.dve_sum(nc, dve, r, nb)
            norms.dve_mean(nc, dve, r, nb, ps)
            norms.dve_diag(nc, dve, r, nb)
            norms.dve_scale(nc, dve, r, nb, ps, x, gain, shift, lo, hi)

        @block.tensor
        def _(pe):
            norms.pe_total(nc, pe, r, nb, ps)
            norms.pe_spread(nc, pe, r, nb, ps)

        @block.gpsimd
        def _(pool):
            norms.pool_rstd(nc, pool, r, nb, minus_half)


def phase_pool(nc, a, sem, scope_sb, ps, norms, part, gain, gps, minus_half, x):
    with ExitStack() as st:
        sb = scope_sb(st)
        h = sb("ph_h", [P, KD, PAD + SEQ + PAD])
        with ExitStack() as tmp:
            nb = norms.buffers(scope_sb(tmp), "pn", SEQ)
            run_norm(nc, norms, 3, nb, a["ident"], ps, x, gain[:, 2, :], part(1, 0), minus_half,
                     lambda k: h[:, k, PAD:PAD + SEQ], None, None)
        sums = sb("sums", [P, 2, PAD + SEQ + PAD])
        d = sb("d", [P, 2, SEQ])
        dh = sb("dh", [P, 4, SEQ], F32R)
        dl = sb("dl", [P, 4, SEQ], F32R)
        raw = sb("praw", [P, KD, 2 * P])
        wh = sb("pwh", [P, KD, 2 * P], F32R)
        wl = sb("pwl", [P, KD, 2 * P], F32R)
        edge = sb("edge", [P, 4, 2, PAD])
        pw_in, w_hi, w_lo = sem("pool_in"), sem("pool_w_hi"), sem("pool_w_lo")
        zero, level, diff, fix, fixed = (sem(f"pool_{n}") for n in ("pads", "level", "diff", "edge_mean", "edges"))
        d_hi, d_lo, mm_done, added = sem("pool_d_hi"), sem("pool_d_lo"), sem("pool_mm"), sem("pool_added")

        with nc.Block() as block:
            @block.sync
            def _(sp):
                sp.dma_start(raw[:, :, :], a["pool_w"]).then_inc(pw_in, 16)
                sp.dma_start(edge[:, :, :, :], a["edge"]).then_inc(pw_in, 16)

            @block.gpsimd
            def _(pool):
                pool.wait_ge(w_hi, 1)
                nc.gpsimd.tensor_tensor(wl[:, :, :], raw[:, :, :], f32(wh[:, :, :]), ALU.subtract).then_inc(w_lo, 1)

            @block.scalar
            def _(act):
                act.wait_ge(pw_in, 32)
                nc.scalar.activation(wh[:, :, :], raw[:, :, :], ACT.Copy).then_inc(w_hi, 1)
                for k in range(KD):
                    act.wait_ge(fixed, 2 * (k + 1))
                    act.wait_ge(diff, k + 1)
                    if k >= 4:
                        act.wait_ge(mm_done, 2 * (k // 2 - 1))
                    nc.scalar.activation(dh[:, k % 4, :], d[:, k % 2, :], ACT.Copy).then_inc(d_hi, 1)

            @block.vector
            def _(dve):
                nc.vector.memset(h[:, :, 0:PAD], 0.0).then_inc(zero, 1)
                nc.vector.memset(h[:, :, PAD + SEQ:], 0.0).then_inc(zero, 1)
                dve.wait_ge(zero, 2)
                dve.wait_ge(pw_in, 32)
                levels = fixes = 0
                for k in range(KD):
                    g = k // 2
                    w = WINDOWS[g]
                    src, reach = h[:, k, :], 1
                    n = 0
                    while reach < w:
                        off = reach // 2
                        lo_t, hi_t = -(w // 2 - reach), SEQ + (w // 2 - reach)
                        dst = sums[:, n % 2, :]
                        if reach == 1:
                            a0, a1 = src[:, PAD + lo_t - 1:PAD + hi_t - 1], src[:, PAD + lo_t:PAD + hi_t]
                        else:
                            a0 = src[:, PAD + lo_t - off:PAD + hi_t - off]
                            a1 = src[:, PAD + lo_t + off:PAD + hi_t + off]
                        nc.vector.tensor_tensor(dst[:, PAD + lo_t:PAD + hi_t], a0, a1, ALU.add).then_inc(level, 1)
                        levels += 1
                        dve.wait_ge(level, levels)
                        src, reach, n = dst, 2 * reach, n + 1
                    if k >= 2:
                        dve.wait_ge(d_hi, k - 1)
                    nc.vector.scalar_tensor_tensor(d[:, k % 2, :], src[:, PAD:PAD + SEQ], 1.0 / w,
                                                   h[:, k, PAD:PAD + SEQ], ALU.mult, ALU.subtract).then_inc(diff, 1)
                    dve.wait_ge(diff, k + 1)
                    for s, at in enumerate((0, SEQ - w // 2)):
                        e = slice(PAD + at, PAD + at + w // 2)
                        nc.vector.tensor_tensor(d[:, k % 2, at:at + w // 2], src[:, e], edge[:, g, s, 0:w // 2],
                                                ALU.mult).then_inc(fix, 1)
                        fixes += 1
                        dve.wait_ge(fix, fixes)
                        nc.vector.tensor_tensor(d[:, k % 2, at:at + w // 2], d[:, k % 2, at:at + w // 2], h[:, k, e],
                                                ALU.subtract).then_inc(fixed, 1)
                    dve.wait_ge(d_hi, k + 1)
                    nc.vector.tensor_tensor(dl[:, k % 4, :], d[:, k % 2, :], f32(dh[:, k % 4, :]), ALU.subtract
                                            ).then_inc(d_lo, 1)
                for m in range(KD):
                    b = 2 * (m % 4)
                    dve.wait_ge(mm_done, m + 1)
                    nc.vector.scalar_tensor_tensor(x[:, m, :], ps[:, b:b + 2, :].rearrange("p s n -> p (s n)"),
                                                   gps[:, m:m + 1], x[:, m, :], ALU.mult, ALU.add).then_inc(added, 1)

            @block.tensor
            def _(pe):
                pe.wait_ge(w_lo, 1)
                for m in range(KD):
                    g, b = m // 2, 2 * (m % 4)
                    pe.wait_ge(d_lo, 2 * g + 2)
                    if m >= 4:
                        pe.wait_ge(added, m - 3)
                    for s in range(2):
                        tok = slice(s * HALF, (s + 1) * HALF)
                        for t in range(2):
                            cols = slice((m % 2) * P, (m % 2 + 1) * P)
                            e = (2 * g + t) % 4
                            mm = mm3(nc, ps[:, b + s, :], wh[:, 2 * g + t, cols], wl[:, 2 * g + t, cols],
                                     dh[:, e, tok], dl[:, e, tok], t == 0, t == 1)
                    mm.then_inc(mm_done, 1)


def phase_final(nc, a, sem, scope_sb, ps, norms, vecs, minus_half, x, out):
    with ExitStack() as st:
        sb = scope_sb(st)
        nb = norms.buffers(sb, "on", SEQ)
        stored = sem("out_stored")
        r = 5
        with nc.Block() as block:
            @block.sync
            def _(sp):
                norms.load(sp, nb, a["ident"], r)
                for k in range(KD):
                    sp.wait_ge(norms.scaled.sem, norms.scaled.at(r, k + 1))
                    sp.dma_start(out[:, k, :], x[:, k, :]).then_inc(stored, 16)
                sp.wait_ge(stored, 16 * KD)

            @block.scalar
            def _(act):
                norms.act_squares(nc, act, r, nb, x)

            @block.vector
            def _(dve):
                norms.dve_ones(nc, nb)
                norms.dve_sum(nc, dve, r, nb)
                norms.dve_mean(nc, dve, r, nb, ps)
                norms.dve_diag(nc, dve, r, nb)
                dve.wait_ge(norms.spread.sem, norms.spread.at(r, 1))
                for k in range(KD):
                    nc.vector.scalar_tensor_tensor(x[:, k, :], x[:, k, :], vecs[:, V_FIN + k:V_FIN + k + 1],
                                                   norms.rstd_of(nb, ps), ALU.mult, ALU.mult
                                                   ).then_inc(norms.scaled.sem, 1)

            @block.tensor
            def _(pe):
                norms.pe_total(nc, pe, r, nb, ps)
                norms.pe_spread(nc, pe, r, nb, ps)

            @block.gpsimd
            def _(pool):
                norms.pool_rstd(nc, pool, r, nb, minus_half)



def lay_out(inputs):
    g = {n: np.asarray(v) for n, v in inputs.items()}
    cols = lambda v: v.reshape(-1, P).T
    a = {}
    a["xT"] = g["x"].reshape(SEQ, KD, P).transpose(2, 1, 0)
    a["ctxT"] = g["ctx"].reshape(CTX, KD, P).transpose(2, 1, 0)
    both = np.stack([cols(g["c"]), cols(g["c_ctx"])], axis=2).reshape(P, 16)
    a["vecs"] = np.concatenate([cols(g["norm1_w"]), cols(g["norm2_w"]), cols(g["final_norm_w"]), cols(g["pool_scale"]),
                                both, cols(g["ada_b"])], axis=1)
    a["log_decay"] = g["ret_log_decay"].reshape(2 * HEADS)
    ada = g["ada_w"].reshape(2, KD, P, 6 * D)
    a["ada_first"] = ada[0, :, :, :2 * D].reshape(2, KD // 2, P, ADA_FIRST, 512).transpose(3, 0, 2, 1, 4)
    a["ada_rest"] = ada[0, :, :, 2 * D:].reshape(KD, P, HEADS, 2, 512).transpose(2, 3, 0, 1, 4).reshape(
        HEADS, 2 * KD, P, 512)
    a["ada_layer1"] = ada[1].reshape(2, KD // 2, P, ADA_LAYER1, 512).transpose(3, 0, 2, 1, 4)
    w = g["ret_w_in"][0].reshape(KD, P, 6 * D)
    parts = []
    for h in range(HEADS):
        q, k = w[:, :, h * DK:(h + 1) * DK], w[:, :, D + h * DK:D + (h + 1) * DK]
        v, gg = (w[:, :, 2 * D + o + h * DV:2 * D + o + (h + 1) * DV] for o in (0, 2 * D))
        parts += [np.concatenate([q, k], axis=2), v, gg]
    a["ret_w"] = np.stack(parts + parts[:1])
    a["gn"] = np.broadcast_to(g["ret_gn_w"].reshape(HEADS, 1, DV), (HEADS, P, DV))
    a["ret_out"] = g["ret_w_out"][0].reshape(4, KV // 4, P, KD, P).transpose(3, 0, 2, 1, 4)
    win = g["ffn_w_in"].reshape(2, KD, P, 2, IT, 2, P).transpose(0, 4, 3, 5, 2, 1, 6).reshape(2 * IT, 2, 2, P, KD * P)
    wout = g["ffn_w_out"].reshape(2 * IT, 2, P, D)
    f = np.zeros((2 * IT + 1, 6, P, D), np.float32)
    f[:-1, 0], f[:-1, 3], f[:-1, 4], f[:-1, 5] = win[:, 0, 0], win[:, 1, 0], win[:, 0, 1], win[:, 1, 1]
    f[1:, 1], f[1:, 2] = wout[:, 0], wout[:, 1]
    a["ffn"] = f
    a["pool_w"] = g["pool_w"][0].reshape(KD, P, 2 * P).transpose(1, 0, 2)
    i = np.arange(P, dtype=np.float32)
    full = np.full(P, float(CHUNK), np.float32)
    a["expo"] = np.stack([i + 1, CHUNK - 1 - i, full, CTX - 1 - i, CTX - 1 - P - i,
                          CHUNK - i, i, full, i, i + P], axis=1)
    j, q = i[:, None], i[None, :]
    a["dist"] = np.stack([np.maximum(q - j, 0), np.maximum(j - q, 0)], axis=1)
    a["ident"] = np.eye(P, dtype=np.float32)
    inv = np.float32(10000.0) ** (-np.arange(0, P, 2, dtype=np.float32) / np.float32(P))
    t = np.arange(SEQ).reshape(NC, P).T
    row = (t // GRID_W).astype(np.float32)[:, :, None] * inv
    col = (np.arange(P) % GRID_W).astype(np.float32)[:, None] * inv
    a["cosr"], a["sinr"], a["cosc"], a["sinc"] = np.cos(row), np.sin(row), np.cos(col), np.sin(col)
    edge = np.zeros((P, 4, 2, PAD), np.float32)
    for n, w in enumerate(WINDOWS):
        e = np.arange(w // 2)
        edge[:, n, 0, :w // 2] = 1 / (e + w // 2).astype(np.float32)
        edge[:, n, 1, :w // 2] = 1 / (w - e).astype(np.float32)
    a["edge"] = edge
    return {n: np.ascontiguousarray(v) for n, v in a.items()}


def kernel(**inputs):
    import concourse.bacc as bacc
    from concourse.bass_utils import run_bass_kernel_spmd

    nc = bacc.Bacc("TRN2", target_bir_lowering=False, num_devices=1)
    arrays = lay_out(inputs)
    a = {n: nc.dram_tensor(f"in_{n}", v.shape, F32, kind="ExternalInput").ap() for n, v in arrays.items()}
    out = nc.dram_tensor("out_0", (P, KD, SEQ), F32, kind="ExternalOutput").ap()
    build(nc, a, out)
    r = run_bass_kernel_spmd(nc, [{f"in_{n}": v for n, v in arrays.items()}], core_ids=[0])
    return r.results[0]["out_0"].transpose(2, 1, 0).reshape(1, SEQ, D)
```

```python
from contextlib import ExitStack

import numpy as np

import concourse.bass as bass
from concourse import mybir

F32 = mybir.dt.float32
F32R = mybir.dt.float32r
ALU = mybir.AluOpType
ACT = mybir.ActivationFunctionType

P = 128
D = 1024
KD = D // P
SEQ = 1024
HALF = 512
GRID_W = 64
CTX = 256
CT = CTX // P
CHUNK = 128
NC = SEQ // CHUNK
HEADS = 4
DK = D // HEADS
DV = 2 * D // HEADS
KV = 2 * D // P
HID = 2816
IT = HID // (2 * P)
WINDOWS = (2, 4, 8, 16)
PAD = 8
EPS = 1e-6
GN_EPS = 1e-5
ADA_FIRST = 2 * D // 512
ADA_LAYER1 = 6 * D // 512

V_N1, V_N2, V_FIN, V_PS, V_C, V_AB = 0, 16, 32, 40, 48, 64
V_ALL = V_AB + 96
DECAYS = 10
F_Q, F_K, F_CHUNK, F_CTX, B_Q, B_K, B_CHUNK, B_CTX = 0, 1, 2, 3, 5, 6, 7, 8


class Tally:

    def __init__(self, sem, per, credit=False, unit=1):
        self.sem, self.per, self.credit, self.unit = sem, per, credit, unit

    def at(self, r, n):
        return r * (self.per * self.unit) + (n + self.per * self.credit) * self.unit


def pay(eng, *tallies):
    for t in tallies:
        eng.sem_inc(t.sem, t.per * t.unit)


def mm3(nc, out, w_hi, w_lo, x_hi, x_lo, first, last):
    nc.tensor.matmul(out, w_hi, x_hi, start=first, stop=False)
    nc.tensor.matmul(out, w_hi, x_lo, start=False, stop=False)
    return nc.tensor.matmul(out, w_lo, x_hi, start=False, stop=last)


def f32(ap):
    return ap.bitcast(F32)


def wide(ap, *dims):
    return ap.broadcast_to([P, *dims])


class Norms:

    def __init__(self, sem):
        self.squared = Tally(sem("norm_squared"), KD)
        self.summed = Tally(sem("norm_summed"), KD)
        self.total = Tally(sem("norm_total"), 1)
        self.mean = Tally(sem("norm_mean"), 1)
        self.rstd = Tally(sem("norm_rstd"), 1)
        self.diag = Tally(sem("norm_diagonal"), 1)
        self.spread = Tally(sem("norm_spread"), 1)
        self.scaled = Tally(sem("norm_scaled"), KD)
        self.hi = Tally(sem("norm_hi"), KD)
        self.lo = Tally(sem("norm_lo"), KD)
        self.shifted = Tally(sem("norm_shifted"), KD // 2)
        self.lo_even = Tally(sem("norm_lo_even"), KD // 2)
        self.lo_odd = Tally(sem("norm_lo_odd"), KD // 2)
        self.ones = sem("norm_ones")
        self.ident_in = sem("norm_ident_in")

    def buffers(self, sb, name, n):
        return dict(n=n, t=sb(f"{name}_t", [P, 2, n]), sq=sb(f"{name}_sq", [P, 2, n]), acc=sb(f"{name}_acc", [P, n]),
                    ms=sb(f"{name}_ms", [P, n // P]), rs=sb(f"{name}_rs", [P, n // P]),
                    dg=sb(f"{name}_dg", [P, n]), ones=sb(f"{name}_ones", [P, P]), ident=sb(f"{name}_ident", [P, P]))

    def keep_buffers(self, keep):
        self.acc, self.ones_kept, self.ident_kept = keep("norm_acc", [P, SEQ]), keep("ones", [P, P]), keep("ident",
                                                                                                       [P, P])
        self.ms, self.rs = keep("norm_ms", [P, SEQ // P]), keep("norm_rs", [P, SEQ // P])

    def kept(self, t=None, dg=None, sq=None):
        return dict(n=SEQ, acc=self.acc, ones=self.ones_kept, ident=self.ident_kept, ms=self.ms, rs=self.rs, t=t,
                    dg=dg, sq=sq)

    def act_square(self, nc, act, r, b, x, k):
        if k >= 2:
            act.wait_ge(self.summed.sem, self.summed.at(r, k - 1))
        nc.scalar.activation(b["sq"][:, k % 2, :], x[:, k, :], ACT.Square).then_inc(self.squared.sem, 1)

    def act_squares(self, nc, act, r, b, x):
        for k in range(KD):
            self.act_square(nc, act, r, b, x, k)

    def dve_add(self, nc, dve, r, b, k):
        dve.wait_ge(self.squared.sem, self.squared.at(r, k + 1))
        if k == 0:
            nc.vector.tensor_copy(b["acc"][:, :], b["sq"][:, 0, :]).then_inc(self.summed.sem, 1)
        else:
            dve.wait_ge(self.summed.sem, self.summed.at(r, k))
            nc.vector.tensor_tensor(b["acc"][:, :], b["acc"][:, :], b["sq"][:, k % 2, :],
                                    ALU.add).then_inc(self.summed.sem, 1)

    def dve_sum(self, nc, dve, r, b):
        for k in range(KD):
            self.dve_add(nc, dve, r, b, k)

    def load(self, sp, b, ident, r):
        sp.dma_start(b["ident"][:, :], ident).then_inc(self.ident_in, 16)

    def dve_ones(self, nc, b):
        nc.vector.memset(b["ones"][:, :], 1.0).then_inc(self.ones, 1)

    def pe_total(self, nc, pe, r, b, ps):
        if r < 2:
            pe.wait_ge(self.ones, r + 1)
        pe.wait_ge(self.summed.sem, self.summed.at(r, KD))
        for j in range(b["n"] // P):
            mm = nc.tensor.matmul(ps[:, 0, j:j + 1], b["acc"][:, j * P:(j + 1) * P], b["ones"][:, 0:1],
                                  start=True, stop=True)
        mm.then_inc(self.total.sem, 1)

    def dve_mean(self, nc, dve, r, b, ps):
        dve.wait_ge(self.total.sem, self.total.at(r, 1))
        nc.vector.tensor_scalar(b["ms"][:, :], ps[:, 0, 0:b["n"] // P], 1.0 / D, EPS, ALU.mult, ALU.add
                                ).then_inc(self.mean.sem, 1)

    def pool_rstd(self, nc, pool, r, b, minus_half):
        pool.wait_ge(self.mean.sem, self.mean.at(r, 1))
        nc.gpsimd.tensor_tensor(b["rs"][:, :], b["ms"][:, :], wide(minus_half[:, 0:1], b["n"] // P),
                                ALU.pow).then_inc(self.rstd.sem, 1)

    def dve_diag(self, nc, dve, r, b):
        if r < 2:
            dve.wait_ge(self.ident_in, 16 * (r + 1))
        dve.wait_ge(self.rstd.sem, self.rstd.at(r, 1))
        n = b["n"] // P
        nc.vector.tensor_tensor(b["dg"][:, :].rearrange("p (j t) -> p j t", t=P),
                                b["ident"][:, :].unsqueeze(1).broadcast_to([P, n, P]),
                                b["rs"][:, :].unsqueeze(2).broadcast_to([P, n, P]), ALU.mult
                                ).then_inc(self.diag.sem, 1)

    def pe_spread(self, nc, pe, r, b, ps):
        pe.wait_ge(self.diag.sem, self.diag.at(r, 1))
        w = min(b["n"], HALF)
        for s in range(0, b["n"], w):
            mm = nc.tensor.matmul(ps[:, s // HALF, 0:w], b["ones"][:, :], b["dg"][:, s:s + w], start=True, stop=True)
        mm.then_inc(self.spread.sem, 1)

    def rstd_of(self, b, ps):
        return ps[:, 0, 0:b["n"]] if b["n"] <= HALF else ps[:, 0:2, :].rearrange("p s n -> p (s n)")

    def dve_scale(self, nc, dve, r, b, ps, x, gain, shift, lo, hi):
        dve.wait_ge(self.spread.sem, self.spread.at(r, 1))
        for k in range(KD + 1):
            if k < KD:
                if k >= 2:
                    dve.wait_ge(self.hi.sem, self.hi.at(r, k - 1))
                    if lo is not None:
                        self.lo_made(dve, r, k - 2)
                nc.vector.scalar_tensor_tensor(b["t"][:, k % 2, :], x[:, k, :], gain[:, k:k + 1],
                                               self.rstd_of(b, ps),
                                               ALU.mult, ALU.mult).then_inc(self.scaled.sem, 1)
            if k and lo is not None and (r < 2 or k % 2):
                dve.wait_ge(self.scaled.sem, self.scaled.at(r, k))
                dve.wait_ge(self.hi.sem, self.hi.at(r, k))
                nc.vector.scalar_tensor_tensor(lo[:, k - 1, :], b["t"][:, (k - 1) % 2, :], shift(k - 1),
                                               f32(hi[:, k - 1, :]), ALU.add, ALU.subtract
                                               ).then_inc((self.lo if r < 2 else self.lo_even).sem, 1)

    def pool_lo(self, nc, pool, r, b, lo, hi):
        for k in range(1, KD, 2):
            pool.wait_ge(self.hi.sem, self.hi.at(r, k + 1))
            nc.gpsimd.tensor_tensor(lo[:, k, :], b["t"][:, k % 2, :], f32(hi[:, k, :]), ALU.subtract
                                    ).then_inc(self.lo_odd.sem, 1)

    def lo_made(self, eng, r, k):
        if r < 2:
            eng.wait_ge(self.lo.sem, self.lo.at(r, k + 1))
        else:
            done = (self.lo_even, self.lo_odd)[k % 2]
            eng.wait_ge(done.sem, done.at((r - 2) // 2, k // 2 + 1))

    def act_shift(self, nc, act, r, b, shift, out):
        for k in range(KD):
            act.wait_ge(self.scaled.sem, self.scaled.at(r, k + 1))
            if r in (2, 4) and k % 2:
                t = b["t"][:, k % 2, :]
                nc.scalar.activation(t, t, ACT.Identity, bias=shift(k)).then_inc(self.shifted.sem, 1)
                act.wait_ge(self.shifted.sem, self.shifted.at((r - 2) // 2, k // 2 + 1))
                nc.scalar.activation(out(k), t, ACT.Copy).then_inc(self.hi.sem, 1)
                continue
            nc.scalar.activation(out(k), b["t"][:, k % 2, :], ACT.Identity, bias=shift(k)).then_inc(self.hi.sem, 1)


def make_gain(nc, gain, mod, vecs, n, layer, p, c, w):
    at = layer * 48 + p * 8
    return nc.vector.scalar_tensor_tensor(gain[:, n, :], mod[:, at:at + 8, c], 1.0, vecs[:, w:w + 8],
                                          ALU.add, ALU.mult)


def build(nc, a, out):
    with ExitStack() as whole:
        build_phases(nc, a, out, whole)


def build_phases(nc, a, out, whole):
    def sem(name):
        return whole.enter_context(nc.semaphore(name))

    def scope_sb(stack):
        return lambda name, shape, dt=F32: stack.enter_context(nc.sbuf_tensor(name, shape, dt))

    keep = scope_sb(whole)
    ps = whole.enter_context(nc.psum_tensor("ps", [P, 8, HALF], F32))
    vecs = keep("vecs", [P, V_ALL])
    mod = keep("mod", [P, 96, 2])
    gain = keep("gain", [P, 6, KD])
    gps = keep("gps", [P, KD])
    minus_half = keep("minus_half", [P, 1])
    cs = keep("cs", [P, KD, 2])
    one = keep("one", [P, 1])

    def part(layer, n, ctx=0):
        return lambda k: mod[:, layer * 48 + n * 8 + k, ctx:ctx + 1]

    s0_dram = nc.dram_tensor("s0_dram", [HEADS, 2, P, 2 * DV], F32, kind="Internal").ap()
    head_dram = nc.dram_tensor("head_dram", [HEADS, P, DECAYS + P], F32, kind="Internal").ap()
    y_dram = nc.dram_tensor("y_dram", [NC, P, HEADS * DV], F32, kind="Internal").ap()

    norms = Norms(sem)
    with ExitStack() as first:
        sb1 = scope_sb(first)
        hh = sb1("hh", [P, KD, SEQ], F32R)
        hl = sb1("hl", [P, KD, SEQ], F32R)
        with ExitStack() as second:
            sb2 = scope_sb(second)
            ch = sb2("ch", [P, KD, CTX], F32R)
            cl = sb2("cl", [P, KD, CTX], F32R)
            xT = sb2("xT", [P, KD, SEQ])
            x_rstd = sb2("x_rstd", [P, SEQ])
            nb = dict(n=SEQ, acc=sb2("x_acc", [P, SEQ]), ones=sb2("x_ones", [P, P]), ident=sb2("x_ident", [P, P]),
                      ms=sb2("x_ms", [P, SEQ // P]), rs=sb2("x_rs", [P, SEQ // P]), dg=x_rstd)
            x_in = [sem(f"x_in{q}") for q in range(2)]
            cw_raw = ContextWeights(sem, sb2)
            phase_conditioning(nc, a, sem, scope_sb, ps, norms, vecs, mod, gain, minus_half, one, cs, part,
                               xT, x_in, nb, ch, cl, head_dram, cw_raw)
            phase_context_states(nc, a, sem, scope_sb, ps, norms, minus_half, one, mod, gain, xT, x_in, nb, x_rstd,
                                 hh, hl, ch, cl, head_dram, s0_dram, cw_raw)
        phase_retention(nc, a, sem, scope_sb, ps, minus_half, one, cs, mod, vecs, hh, hl, s0_dram, head_dram,
                        y_dram)
    x = keep("x", [P, KD, SEQ])
    norms.keep_buffers(keep)
    phase_retention_out(nc, a, sem, scope_sb, ps, norms, part, x, y_dram, gain, mod, vecs)
    ffn = Ffn(sem, keep)
    cond = (cs, one, mod, vecs, gps)
    phase_ffn(nc, a, scope_sb, ps, norms, ffn, 0, part, gain, minus_half, x, cond)
    phase_pool(nc, a, sem, scope_sb, ps, norms, part, gain, gps, minus_half, x)
    phase_ffn(nc, a, scope_sb, ps, norms, ffn, 1, part, gain, minus_half, x, cond)
    phase_final(nc, a, sem, scope_sb, ps, norms, vecs, minus_half, x, out)


def phase_conditioning(nc, a, sem, scope_sb, ps, norms, vecs, mod, gain, minus_half, one, cs, part,
                       xT, x_in, nb, ch, cl, head_dram, cw_raw):
    with ExitStack() as st:
        sb = scope_sb(st)
        cT = sb("cT", [P, KD, CTX])
        nb = dict(nb, sq=sb("x_sq", [P, 2, SEQ]))
        nbc = norms.buffers(sb, "nc", CTX)
        ada = sb("ada", [P, 4, KD // 2, 512])
        cw = sb("cw", [P, KD, P])
        rows = sb("rows", [P, ADA_FIRST, 512])
        expo = sb("expo", [P, 10])
        dist = sb("dist", [P, 2, P])
        lg = sb("lg", [P, 2 * HEADS])
        arg = sb("arg", [P, HEADS, P])
        heads = sb("heads", [P, HEADS, DECAYS + P])
        ROWS, TURN, CPS = 0, 4, 5

        small_in, ctx_in = sem("small_in"), sem("ctx_in")
        ada_in = [sem(f"ada_in{q}") for q in range(4)]
        ada_mm, ada_rows, ada_turned, ada_out = sem("ada_mm"), sem("ada_rows"), sem("ada_turned"), sem("ada_out")
        ready = sem("consts_ready")
        c_silu, c_wide = sem("c_silu"), sem("c_wide")
        decay_step = sem("decay_step")
        decays, arg_done, mask_done, mask_out = sem("decays"), sem("arg_done"), sem("mask_done"), sem("mask_out")
        gains = sem("gains")

        with nc.Block() as block:
            @block.sync
            def _(sp):
                sp.dma_start(vecs[:, :], a["vecs"]).then_inc(small_in, 16)
                sp.dma_start(lg[:, :], a["log_decay"].partition_broadcast(P)).then_inc(small_in, 16)
                sp.dma_start(expo[:, :], a["expo"]).then_inc(small_in, 16)
                sp.dma_start(dist[:, :, :], a["dist"]).then_inc(small_in, 16)
                norms.load(sp, nbc, a["ident"], 0)
                for n in range(2 * ADA_FIRST):
                    if n == 2:
                        sp.dma_start(cT[:, :, :], a["ctxT"]).then_inc(ctx_in, 16)
                    if n >= 4:
                        sp.wait_ge(ada_mm, n - 3)
                    sp.dma_start(ada[:, n % 4, :, :], a["ada_first"][n // 2, n % 2]).then_inc(ada_in[n % 4], 16)
                    if n % 4 == 3:
                        q = n // 4
                        t = slice(q * KD // 2, (q + 1) * KD // 2)
                        sp.dma_start(xT[:, t, :], a["xT"][:, t, :]).then_inc(x_in[q], 16)
                for k in range(cw_raw.SLOTS):
                    cw_raw.load(sp, a, 0, k)
                sp.wait_ge(mask_out, 16)

            @block.scalar
            def _(act):
                act.wait_ge(small_in, 64)
                nc.scalar.activation(cs[:, :, :].rearrange("p k c -> p (k c)"), vecs[:, V_C:V_C + 16],
                                     ACT.Silu).then_inc(c_silu, 1)
                act.wait_ge(decays, 2)
                for h in range(HEADS):
                    for d, (e0, e1) in enumerate(((0, 5), (5, 10))):
                        nc.scalar.activation(heads[:, h, e0:e1], expo[:, e0:e1], ACT.Exp,
                                             scale=lg[:, d * HEADS + h:d * HEADS + h + 1]).then_inc(decay_step, 1)
                act.wait_ge(arg_done, 2 * HEADS)
                nc.scalar.activation(heads[:, :, DECAYS:], arg[:, :, :], ACT.Exp).then_inc(mask_done, 1)
                act.wait_ge(mask_done, 1)
                act.wait_ge(decay_step, 2 * HEADS)
                act.dma_start(head_dram.rearrange("h p n -> p h n"), heads[:, :, :]).then_inc(mask_out, 16)
                act.wait_ge(ctx_in, 16)
                norms.act_squares(nc, act, 0, nbc, cT)
                for b in range(ADA_FIRST):
                    act.wait_ge(ada_mm, 2 * (b + 1))
                    nc.scalar.activation(rows[:, b, :], ps[:, ROWS + b % 2, :], ACT.Copy).then_inc(ada_rows, 1)
                    if 1 <= b <= 2:
                        act.wait_ge(x_in[0], 16)
                        for k in (2 * b - 2, 2 * b - 1):
                            norms.act_square(nc, act, 1, nb, xT, k)
                norms.act_shift(nc, act, 0, nbc, part(0, 0, 1), lambda k: ch[:, k, :])

            @block.vector
            def _(dve):
                nc.vector.memset(cw[:, :, :], 0.0).then_inc(c_wide, 1)
                norms.dve_ones(nc, nbc)
                nc.vector.memset(minus_half[:, :], -0.5).then_inc(ready, 1)
                nc.vector.memset(one[:, :], 1.0).then_inc(ready, 1)
                dve.wait_ge(small_in, 64)
                nc.vector.tensor_scalar(arg[:, 0, 0:8], lg[:, :], -1.0, None, ALU.mult).then_inc(decays, 1)
                dve.wait_ge(decays, 1)
                nc.vector.tensor_tensor(lg[:, :], lg[:, :], arg[:, 0, 0:8], ALU.min).then_inc(decays, 1)
                dve.wait_ge(c_silu, 1)
                dve.wait_ge(c_wide, 1)
                nc.vector.tensor_copy(cw[:, :, 0:2], cs[:, :, :]).then_inc(c_wide, 1)
                dve.wait_ge(decays, 2)
                for h in range(HEADS):
                    nc.vector.tensor_scalar(arg[:, h, :], dist[:, 1, :], lg[:, HEADS + h:HEADS + h + 1], None,
                                            ALU.mult).then_inc(arg_done, 1)
                for h in range(HEADS):
                    dve.wait_ge(arg_done, h + 1)
                    nc.vector.scalar_tensor_tensor(arg[:, h, :], dist[:, 0, :], lg[:, h:h + 1], arg[:, h, :],
                                                   ALU.mult, ALU.add).then_inc(arg_done, 1)
                norms.dve_sum(nc, dve, 0, nbc)
                norms.dve_mean(nc, dve, 0, nbc, ps[:, CPS:CPS + 1, :])
                norms.dve_diag(nc, dve, 0, nbc)
                for b in range(ADA_FIRST):
                    dve.wait_ge(ada_turned, b + 1)
                    nc.vector.tensor_tensor(mod[:, 4 * b:4 * b + 4, :], ps[:, TURN, 0:8].rearrange(
                        "p (j c) -> p j c", c=2), vecs[:, V_AB + 4 * b:V_AB + 4 * b + 4].unsqueeze(2)
                        .broadcast_to([P, 4, 2]), ALU.add).then_inc(ada_out, 1)
                    if b < 2:
                        for k in (2 * b, 2 * b + 1):
                            norms.dve_add(nc, dve, 1, nb, k)
                dve.wait_ge(ada_out, ADA_FIRST)
                for n, c in ((0, 0), (4, 1)):
                    make_gain(nc, gain, mod, vecs, n, 0, 1, c, V_N1).then_inc(gains, 1)
                dve.wait_ge(gains, 2)
                norms.dve_scale(nc, dve, 0, nbc, ps[:, CPS:CPS + 1, :], cT, gain[:, 4, :], part(0, 0, 1), cl, ch)

            @block.tensor
            def _(pe):
                def turn(b):
                    pe.wait_ge(ada_rows, b + 1)
                    if b:
                        pe.wait_ge(ada_out, b)
                    else:
                        pe.wait_ge(norms.ident_in, 16)
                    for j in range(4):
                        mm = nc.tensor.matmul(ps[:, TURN, 2 * j:2 * j + 2], rows[:, b, j * P:(j + 1) * P],
                                              nbc["ident"][:, 0:2], start=True, stop=True)
                    mm.then_inc(ada_turned, 1)

                pe.wait_ge(c_wide, 2)
                for b in range(ADA_FIRST):
                    for q in range(2):
                        n = 2 * b + q
                        pe.wait_ge(ada_in[n % 4], 16 * (n // 4 + 1))
                        if q == 0 and b >= 2:
                            pe.wait_ge(ada_rows, b - 1)
                        for k in range(KD // 2):
                            kt = q * KD // 2 + k
                            mm = nc.tensor.matmul(ps[:, ROWS + b % 2, :], cw[:, kt, :], ada[:, n % 4, k, :],
                                                  start=kt == 0, stop=kt == KD - 1)
                        mm.then_inc(ada_mm, 1)
                    if b == 0:
                        norms.pe_total(nc, pe, 0, nbc, ps[:, CPS:CPS + 1, :])
                    else:
                        turn(b - 1)
                        if b == 1:
                            norms.pe_spread(nc, pe, 0, nbc, ps[:, CPS:CPS + 1, :])
                turn(ADA_FIRST - 1)

            @block.gpsimd
            def _(pool):
                pool.wait_ge(ready, 1)
                norms.pool_rstd(nc, pool, 0, nbc, minus_half)


class ContextWeights:

    SLOTS = 4

    def __init__(self, sem, sb):
        self.raw = sb("raw1", [P, self.SLOTS, DK + DV])
        self.raw_in = [Tally(sem(f"ctx_raw_in{q}"), 2, unit=32) for q in range(self.SLOTS)]

    def load(self, sp, a, h, k):
        slot = k % self.SLOTS
        for b, src, dst in ((0, slice(DK, 2 * DK), slice(0, DK)), (1, slice(0, DV), slice(DK, DK + DV))):
            w = a["ret_w"][h * 3 + b, k, :, src] if isinstance(h, int) else a["ret_w"][bass.ds(h * 3 + b, 1), k, :, src].rearrange(
                "o p n -> (o p) n")
            sp.dma_start(self.raw[:, slot, dst], w).then_inc(self.raw_in[slot].sem, 16)


def phase_context_states(nc, a, sem, scope_sb, ps, norms, minus_half, one, mod, gain, xT, x_in, nb, x_rstd,
                         hh, hl, ch, cl, head_dram, s0_dram, cw_raw):
    with ExitStack() as st:
        sb = scope_sb(st)
        WK = DK + DV
        RAW, raw, raw_in = cw_raw.SLOTS, cw_raw.raw, cw_raw.raw_in
        XT = KD // HEADS
        wh = sb("wh1", [P, KD, WK], F32R)
        wl = sb("wl1", [P, KD, WK], F32R)
        vh = sb("vh1", [P, CT, DV], F32R)
        vl = sb("vl1", [P, CT, DV], F32R)
        kh = sb("kh1", [P, 2, CT, DK], F32R)
        kl = sb("kl1", [P, 2, CT, DK], F32R)
        s0 = sb("s0", [P, 2, 2 * DV])
        hd = sb("hd1", [P, DECAYS])
        idle = sb("idle1", [P, XT])
        nb = dict(nb, sq=s0)
        XPS = ps[:, 6:8, :]
        rstd_row = sem("rstd_row")

        hd_in = Tally(sem("ctx_decays_in"), 1, unit=16)
        w_hi = Tally(sem("ctx_w_hi"), KD)
        w_lo = [Tally(sem(f"ctx_w_lo_{n}"), KD // 2, credit=True) for n in ("even", "odd")]
        w_used = Tally(sem("ctx_w_used"), KD - 1, credit=True)
        proj = Tally(sem("ctx_proj"), CT, credit=True)
        hi = Tally(sem("ctx_kv_hi"), 3 * CT)
        lo = Tally(sem("ctx_kv_lo"), 3 * CT, credit=True)
        states = Tally(sem("ctx_states"), 2, credit=True)
        copied = [Tally(sem(f"ctx_copied{d}"), 1, credit=True) for d in range(2)]
        stored = [Tally(sem(f"ctx_stored{d}"), 1, credit=True, unit=16) for d in range(2)]

        def lo_made(eng, h, k):
            eng.wait_ge(w_lo[k % 2].sem, w_lo[k % 2].at(h, k // 2 + 1))

        def tile(ap, h, j):
            return ap[:, bass.ds(h * XT + j, 1), :]

        def column(ap, h, j):
            return ap[:, bass.ds(h * XT + j, 1)]

        with nc.Block() as block:
            @block.sync
            def _(sp):
                pay(sp, *w_lo, w_used, proj, lo, states, *copied, *stored)
                norms.load(sp, nb, a["ident"], 1)
                for k in range(RAW, KD):
                    lo_made(sp, 0, k - RAW)
                    cw_raw.load(sp, a, 0, k)
                sp.dma_start(hd[:, :], head_dram[0, :, 0:DECAYS]).then_inc(hd_in.sem, 16)
                with sp.Fori(1, HEADS) as h:
                    for k in range(KD):
                        lo_made(sp, h, k - RAW)
                        cw_raw.load(sp, a, h, k)
                    sp.wait_ge(lo.sem, lo.at(h, 0))
                    sp.dma_start(hd[:, :], head_dram[bass.ds(h, 1), :, 0:DECAYS]
                                 .rearrange("o p n -> (o p) n")).then_inc(hd_in.sem, 16)

            @block.gpsimd
            def _(pool):
                def split_even(h):
                    for k in range(0, KD, 2):
                        pool.wait_ge(w_hi.sem, w_hi.at(h, k + 1))
                        nc.gpsimd.tensor_tensor(wl[:, k, :], raw[:, k % RAW, :], f32(wh[:, k, :]),
                                                ALU.subtract).then_inc(w_lo[0].sem, 1)

                split_even(0)
                norms.pool_rstd(nc, pool, 1, nb, minus_half)
                with pool.Fori(1, HEADS) as h:
                    split_even(h)

            @block.scalar
            def _(act):
                def split_hi(h, ks):
                    for k in ks:
                        if k < KD - 1:
                            act.wait_ge(w_used.sem, w_used.at(h - 1, k + 1))
                        else:
                            act.wait_ge(proj.sem, proj.at(h - 1, CT))
                        act.wait_ge(raw_in[k % RAW].sem, raw_in[k % RAW].at(h, k // RAW + 1))
                        nc.scalar.activation(wh[:, k, :], raw[:, k % RAW, :], ACT.Copy).then_inc(w_hi.sem, 1)

                def kv_hi(h, t):
                    if t == 0:
                        act.wait_ge(states.sem, states.at(h, 0))
                        act.wait_ge(hd_in.sem, hd_in.at(h, 1))
                    act.wait_ge(proj.sem, proj.at(h, t + 1))
                    nc.scalar.activation(vh[:, t, :], ps[:, 2 + t, :], ACT.Copy).then_inc(hi.sem, 1)
                    for d, e in enumerate((F_CTX, B_CTX)):
                        nc.scalar.activation(kh[:, d, t, :], ps[:, t, 0:DK], ACT.Copy,
                                             scale=hd[:, e + t:e + t + 1]).then_inc(hi.sem, 1)

                def latent_hi(h):
                    for j in range(XT):
                        act.wait_ge(norms.scaled.sem, norms.scaled.at(1, h * XT + (j + 1)))
                        nc.scalar.activation(idle[:, j:j + 1], one[:, :], ACT.Copy)
                        nc.scalar.activation(tile(hh, h, j), tile(xT, h, j), ACT.Identity,
                                             bias=column(mod[:, :, 0], h, j)).then_inc(norms.hi.sem, 1)

                def copy_states(h):
                    act.wait_ge(stored[0].sem, stored[0].at(h, 0))
                    act.wait_ge(states.sem, states.at(h, 1))
                    nc.scalar.activation(s0[:, 0, :], ps[:, 4:6, :].rearrange("p t n -> p (t n)"),
                                         ACT.Copy).then_inc(copied[0].sem, 1)
                    for d in range(2):
                        act.wait_ge(copied[d].sem, copied[d].at(h, 1))
                        act.dma_start(s0_dram[bass.ds(h, 1), d].rearrange("o p n -> (o p) n"),
                                      s0[:, d, :]).then_inc(stored[d].sem, 16)

                split_hi(0, range(KD // 2))
                act.wait_ge(x_in[1], 16)
                for k in range(KD // 2, KD):
                    split_hi(0, (k,))
                    norms.act_square(nc, act, 1, nb, xT, k)
                kv_hi(0, 0)
                act.wait_ge(norms.spread.sem, norms.spread.at(1, 1))
                nc.scalar.activation(x_rstd[:, :], norms.rstd_of(nb, XPS), ACT.Copy).then_inc(rstd_row, 1)
                with act.Fori(0, HEADS - 1) as h:
                    split_hi(h + 1, range(KD // 2))
                    kv_hi(h, 1)
                    split_hi(h + 1, range(KD // 2, KD))
                    latent_hi(h)
                    copy_states(h)
                    kv_hi(h + 1, 0)
                kv_hi(HEADS - 1, 1)
                latent_hi(HEADS - 1)
                copy_states(HEADS - 1)
                for d in range(2):
                    act.wait_ge(stored[d].sem, stored[d].at(HEADS - 1, 1))

            @block.vector
            def _(dve):
                def split_odd(h, ks):
                    for k in ks:
                        dve.wait_ge(w_hi.sem, w_hi.at(h, k + 1))
                        nc.vector.tensor_tensor(wl[:, k, :], raw[:, k % RAW, :], f32(wh[:, k, :]),
                                                ALU.subtract).then_inc(w_lo[1].sem, 1)

                def kv_lo(h, t):
                    dve.wait_ge(hi.sem, hi.at(h, 3 * t + 1))
                    nc.vector.tensor_tensor(vl[:, t, :], ps[:, 2 + t, :], f32(vh[:, t, :]),
                                            ALU.subtract).then_inc(lo.sem, 1)
                    dve.wait_ge(hi.sem, hi.at(h, 3 * t + 3))
                    for d, e in enumerate((F_CTX, B_CTX)):
                        nc.vector.scalar_tensor_tensor(kl[:, d, t, :], ps[:, t, 0:DK], hd[:, e + t:e + t + 1],
                                                       f32(kh[:, d, t, :]), ALU.mult,
                                                       ALU.subtract).then_inc(lo.sem, 1)

                def latent_scaled(h):
                    for j in range(XT):
                        nc.vector.scalar_tensor_tensor(tile(xT, h, j), tile(xT, h, j), column(gain[:, 0, :], h, j),
                                                       x_rstd[:, :].unsqueeze(1), ALU.mult, ALU.mult
                                                       ).then_inc(norms.scaled.sem, 1)

                def latent_lo(h):
                    for j in range(XT):
                        dve.wait_ge(norms.scaled.sem, norms.scaled.at(1, h * XT + (j + 1)))
                        dve.wait_ge(norms.hi.sem, norms.hi.at(1, h * XT + (j + 1)))
                        nc.vector.scalar_tensor_tensor(tile(hl, h, j), tile(xT, h, j), column(mod[:, :, 0], h, j),
                                                       f32(tile(hh, h, j)), ALU.add, ALU.subtract
                                                       ).then_inc(norms.lo.sem, 1)

                def copy_states(h):
                    dve.wait_ge(stored[1].sem, stored[1].at(h, 0))
                    dve.wait_ge(states.sem, states.at(h, 2))
                    nc.vector.tensor_copy(s0[:, 1, :], ps[:, 6:8, :].rearrange("p t n -> p (t n)")
                                          ).then_inc(copied[1].sem, 1)

                norms.dve_ones(nc, nb)
                split_odd(0, (1, 3))
                for k in range(KD // 2, KD):
                    if k % 2:
                        split_odd(0, (k,))
                    norms.dve_add(nc, dve, 1, nb, k)
                norms.dve_mean(nc, dve, 1, nb, XPS)
                norms.dve_diag(nc, dve, 1, nb)
                kv_lo(0, 0)
                dve.wait_ge(rstd_row, 1)
                latent_scaled(0)
                with dve.Fori(0, HEADS - 1) as h:
                    split_odd(h + 1, range(1, KD // 2, 2))
                    kv_lo(h, 1)
                    split_odd(h + 1, range(KD // 2 + 1, KD, 2))
                    latent_lo(h)
                    latent_scaled(h + 1)
                    copy_states(h)
                    kv_lo(h + 1, 0)
                kv_lo(HEADS - 1, 1)
                latent_lo(HEADS - 1)
                copy_states(HEADS - 1)

            @block.tensor
            def _(pe):
                def project(h, t, halfway=None):
                    pe.wait_ge(lo.sem, lo.at(h - 1, 3 * (t + 1)))
                    tok = slice(t * P, (t + 1) * P)
                    for k in range(KD):
                        if t == 0:
                            lo_made(pe, h, k)
                        if halfway and k == KD // 2:
                            halfway()
                        mm3(nc, ps[:, t, 0:DK], ch[:, k, tok], cl[:, k, tok], wh[:, k, 0:DK], wl[:, k, 0:DK],
                            k == 0, k == KD - 1)
                        mm = mm3(nc, ps[:, 2 + t, :], ch[:, k, tok], cl[:, k, tok], wh[:, k, DK:WK],
                                 wl[:, k, DK:WK], k == 0, k == KD - 1)
                        if t == CT - 1 and k < KD - 1:
                            mm.then_inc(w_used.sem, 1)
                    mm.then_inc(proj.sem, 1)

                def make_states(h):
                    pe.wait_ge(lo.sem, lo.at(h, 3 * CT))
                    for d in range(2):
                        pe.wait_ge(copied[d].sem, copied[d].at(h, 0))
                        for dt in range(2):
                            for t in range(CT):
                                cols = slice(dt * P, (dt + 1) * P)
                                mm = mm3(nc, ps[:, 4 + 2 * d + dt, :], kh[:, d, t, cols], kl[:, d, t, cols],
                                         vh[:, t, :], vl[:, t, :], t == 0, t == CT - 1)
                        mm.then_inc(states.sem, 1)

                project(0, 0)
                norms.pe_total(nc, pe, 1, nb, XPS)
                project(0, 1, lambda: norms.pe_spread(nc, pe, 1, nb, XPS))
                pe.wait_ge(rstd_row, 1)
                with pe.Fori(0, HEADS - 1) as h:
                    project(h + 1, 0)
                    make_states(h)
                    project(h + 1, 1)
                make_states(HEADS - 1)


def phase_retention(nc, a, sem, scope_sb, ps, minus_half, one, cs, mod, vecs, hh, hl, s0_dram, head_dram, y_dram):
    with ExitStack() as st:
        sb = scope_sb(st)
        RAW = 4
        BLOCKS = 3
        raw = sb("raw2", [P, RAW, DV])
        wh = sb("wh2", [P, KD, DV], F32R)
        wl = sb("wl2", [P, KD, DV], F32R)
        qTh = sb("qTh", [P, 2, SEQ], F32R)
        qTl = sb("qTl", [P, 2, SEQ], F32R)
        kn = sb("kn", [P, NC, DK])
        vh = sb("vh2", [P, NC, DV], F32R)
        vl = sb("vl2", [P, NC, DV], F32R)
        y = sb("y", [P, NC, DV])
        S = sb("S", [P, 2, DV])
        Sh = sb("Sh", [P, 2, DV], F32R)
        Sl = sb("Sl", [P, 2, DV], F32R)
        kdh = sb("kdh", [P, DK], F32R)
        kdl = sb("kdl", [P, DK], F32R)
        cosr, sinr = sb("cosr", [P, NC, 64]), sb("sinr", [P, NC, 64])
        cosc, sinc = sb("cosc", [P, 64]), sb("sinc", [P, 64])
        ident = sb("ident2", [P, P])
        hd = sb("hd2", [P, DECAYS + P])
        gn = sb("gn", [P, DV])
        t1 = sb("t1", [P, DV])
        t2 = sb("t2", [P, DV])
        kTh = sb("kTh", [P, 2, P], F32R)
        kTl = sb("kTl", [P, 2, P], F32R)
        pf = sb("pf", [P, P])
        ph = sb("ph", [P, P], F32R)
        pl = sb("pl", [P, P], F32R)
        stats = sb("stats", [P, 6])
        mv = sb("mv", [P, 2])
        ve = sb("ve", [P, 1])
        rstd = sb("rstd", [P, 1])
        warm = sb("warm2", [P, 1])
        PT, SC, PV, QS, U = 2, 3, 4, 5, 6

        const_in = sem("ret_const_in")
        ADA = 2 * KD
        raw_in = [Tally(sem(f"ret_raw_in{q}"), (BLOCKS * KD + ADA) // RAW, unit=16) for q in range(RAW)]
        ada_step = Tally(sem("ret_ada_step"), ADA)
        ada_mm = Tally(sem("ret_ada_mm"), 1)
        ada_out = Tally(sem("ret_ada_out"), 1, credit=True)
        w_hi = Tally(sem("ret_w_hi"), BLOCKS * KD)
        w_lo = [Tally(sem(f"ret_w_lo_{n}"), BLOCKS * KD // 2, credit=True) for n in ("even", "odd")]
        w_used = Tally(sem("ret_w_used"), BLOCKS * (KD - 1), credit=True)
        proj = Tally(sem("ret_proj"), BLOCKS * NC, credit=True)
        hd_in = Tally(sem("ret_head_in"), 1, unit=16)
        gn_in = Tally(sem("ret_gn_in"), 1, unit=16)
        s_in = Tally(sem("ret_state_in"), 2, unit=16)
        rope_cos = Tally(sem("rope_cos"), 2 * NC)
        rope_sin = Tally(sem("rope_sin"), 2 * NC)
        rope_out = Tally(sem("rope_out"), 4 * NC)
        qT_mm = Tally(sem("qT_mm"), NC, credit=True)
        qT_hi = Tally(sem("qT_hi"), NC, credit=True)
        qT_lo = Tally(sem("qT_lo"), NC, credit=True)
        kT_mm = Tally(sem("kT_mm"), NC, credit=True)
        kT_hi = Tally(sem("kT_hi"), NC)
        kT_lo = Tally(sem("kT_lo"), NC, credit=True)
        kd_hi = Tally(sem("kd_hi"), 2 * (NC - 1))
        kd_lo = Tally(sem("kd_lo"), 2 * (NC - 1), credit=True)
        v_hi = Tally(sem("v_hi"), NC)
        v_lo = Tally(sem("v_lo"), NC)
        score_mm = Tally(sem("score_mm"), NC)
        p_f = Tally(sem("p_masked"), NC, credit=True)
        p_hi = Tally(sem("p_hi"), NC)
        p_lo = Tally(sem("p_lo"), NC, credit=True)
        qs_mm = Tally(sem("qs_mm"), 2 * NC, credit=True)
        pv_mm = Tally(sem("pv_mm"), NC, credit=True)
        y_pv = Tally(sem("y_pv"), NC, credit=True)
        y_f = Tally(sem("y_forward"), NC, credit=True)
        y_b = Tally(sem("y_backward"), NC, credit=True)
        u_mm = Tally(sem("u_mm"), 2 * (NC - 1), credit=True)
        s_f32 = Tally(sem("s_updated"), 2 * (NC - 1), credit=True)
        s_hi = Tally(sem("s_hi"), 2 * NC, credit=True)
        s_lo = Tally(sem("s_lo"), 2 * NC, credit=True)
        silu = Tally(sem("g_silu"), NC, credit=True)
        gated = Tally(sem("g_weighted"), NC, credit=True)
        st_done = Tally(sem("y_stats"), NC)
        ag_done = Tally(sem("y_mean_var"), NC)
        ve_done = Tally(sem("y_var_eps"), NC)
        rs_done = Tally(sem("y_rstd"), NC)
        yn_done = Tally(sem("y_normed"), NC, credit=True)
        yg_done = Tally(sem("y_gated"), NC, credit=True)
        stored = Tally(sem("y_stored"), NC, credit=True, unit=16)

        def order(d):
            return list(range(NC)) if d == 0 else list(range(NC - 1, -1, -1))

        def loaded(h, b, k):
            n = b * KD + k + (ADA if b else 0)
            return raw_in[k % RAW].at(h, n // RAW + 1)

        def lo_made(eng, h, n):
            w = w_lo[n % 2]
            eng.wait_ge(w.sem, w.at(h, n // 2 + 1))

        def load_slice(sp, h, b, k):
            if b == 1 and k < RAW:
                sp.wait_ge(ada_step.sem, ada_step.at(h, ADA - RAW + k + 1))
            else:
                lo_made(sp, h, b * KD + k - RAW)
            sp.dma_start(raw[:, k % RAW, :], a["ret_w"][bass.ds(h * BLOCKS + b, 1), k, :, :]
                         .rearrange("o p n -> (o p) n")).then_inc(raw_in[k % RAW].sem, 16)

        with nc.Block() as block:
            @block.sync
            def _(sp):
                pay(sp, *w_lo, w_used, proj, qT_mm, qT_hi, qT_lo, kT_mm, kT_lo, kd_lo, p_f, p_lo,
                    qs_mm, pv_mm, y_pv, y_f, y_b, u_mm, s_f32, s_hi, s_lo, silu, gated, yn_done, yg_done, stored, ada_out)
                for k in range(RAW):
                    load_slice(sp, 0, 0, k)
                for dst, name in ((cosr[:, :, :], "cosr"), (sinr[:, :, :], "sinr"), (cosc[:, :], "cosc"),
                                  (sinc[:, :], "sinc"), (ident[:, :], "ident")):
                    sp.dma_start(dst, a[name]).then_inc(const_in, 16)
                for k in range(RAW, KD):
                    load_slice(sp, 0, 0, k)
                with sp.Fori(0, HEADS) as h:
                    sp.wait_ge(y_b.sem, y_b.at(h, 0))
                    sp.dma_start(hd[:, :], head_dram[bass.ds(h, 1)].rearrange("o p n -> (o p) n")
                                 ).then_inc(hd_in.sem, 16)
                    sp.wait_ge(s_lo.sem, s_lo.at(h, 0))
                    sp.dma_start(S[:, :, :].rearrange("p t n -> p (t n)"), s0_dram[bass.ds(h, 1), 0]
                                 .rearrange("o p n -> (o p) n")).then_inc(s_in.sem, 16)
                    sp.wait_ge(gated.sem, gated.at(h, 0))
                    sp.dma_start(gn[:, :], a["gn"][bass.ds(h, 1)].rearrange("o p n -> (o p) n")
                                 ).then_inc(gn_in.sem, 16)
                    for n in range(ADA):
                        if n < RAW:
                            lo_made(sp, h, KD - RAW + n)
                        else:
                            sp.wait_ge(ada_step.sem, ada_step.at(h, n - RAW + 1))
                        sp.dma_start(raw[:, n % RAW, :], a["ada_rest"][bass.ds(h, 1), n]
                                     .rearrange("o p n -> (o p) n")).then_inc(raw_in[n % RAW].sem, 16)
                    for b in (1, 2):
                        for k in range(KD):
                            load_slice(sp, h, b, k)
                    sp.wait_ge(s_lo.sem, s_lo.at(h, NC))
                    sp.dma_start(S[:, :, :].rearrange("p t n -> p (t n)"), s0_dram[bass.ds(h, 1), 1]
                                 .rearrange("o p n -> (o p) n")).then_inc(s_in.sem, 16)
                    for k in range(KD):
                        load_slice(sp, h, BLOCKS, k)

            def split_hi(act, h, b, ks=range(KD)):
                for k in ks:
                    if k < KD - 1:
                        act.wait_ge(w_used.sem, w_used.at(h, (b - 1) * (KD - 1) + k + 1))
                    else:
                        act.wait_ge(proj.sem, proj.at(h, b * NC))
                    act.wait_ge(raw_in[k % RAW].sem, loaded(h, b, k))
                    nc.scalar.activation(wh[:, k, :], raw[:, k % RAW, :], ACT.Copy).then_inc(w_hi.sem, 1)

            def split_even(pool, h, b, ks=(0, 2, 4, 6)):
                for k in ks:
                    pool.wait_ge(w_hi.sem, w_hi.at(h, b * KD + k + 1))
                    nc.gpsimd.tensor_tensor(wl[:, k, :], raw[:, k % RAW, :], f32(wh[:, k, :]),
                                            ALU.subtract).then_inc(w_lo[0].sem, 1)

            def split_odd(dve, h, b, ks=(1, 3, 5, 7)):
                for k in ks:
                    dve.wait_ge(w_hi.sem, w_hi.at(h, b * KD + k + 1))
                    nc.vector.tensor_tensor(wl[:, k, :], raw[:, k % RAW, :], f32(wh[:, k, :]),
                                            ALU.subtract).then_inc(w_lo[1].sem, 1)

            @block.gpsimd
            def _(pool):
                split_even(pool, 0, 0)
                with pool.Fori(0, HEADS) as h:
                    for b in (1, 2):
                        split_even(pool, h, b)
                    for m, c in enumerate(order(1)):
                        if m == NC - 1:
                            split_even(pool, h, BLOCKS, (2,))
                        if m == 0:
                            pool.wait_ge(gn_in.sem, gn_in.at(h, 1))
                        pool.wait_ge(silu.sem, silu.at(h, m + 1))
                        nc.gpsimd.tensor_tensor(t1[:, :], t1[:, :], gn[:, :], ALU.mult).then_inc(gated.sem, 1)
                        if m == NC - 2:
                            split_even(pool, h, BLOCKS, (0,))
                        pool.wait_ge(ve_done.sem, ve_done.at(h, m + 1))
                        nc.gpsimd.tensor_tensor(rstd[:, :], ve[:, :], minus_half[:, :],
                                                ALU.pow).then_inc(rs_done.sem, 1)
                    split_even(pool, h, BLOCKS, (4, 6))

            @block.scalar
            def _(act):
                nc.scalar.activation(warm[:, :], minus_half[:, :], ACT.Silu)

                def split_state(h, d, m):
                    if m == 0:
                        act.wait_ge(s_in.sem, s_in.at(h, d + 1))
                    else:
                        act.wait_ge(s_f32.sem, s_f32.at(h, d * (NC - 1) + m))
                    act.wait_ge(qs_mm.sem, qs_mm.at(h, d * NC + m))
                    nc.scalar.activation(Sh[:, :, :], S[:, :, :], ACT.Copy).then_inc(s_hi.sem, 1)

                def decay_keys(h, d, m, c):
                    n = d * (NC - 1) + m
                    act.wait_ge(u_mm.sem, u_mm.at(h, n))
                    act.wait_ge(rope_out.sem, rope_out.at(h, 4 * (c + 1)))
                    e = F_K if d == 0 else B_K
                    nc.scalar.activation(kdh[:, :], kn[:, c, :], ACT.Copy,
                                         scale=hd[:, e:e + 1]).then_inc(kd_hi.sem, 1)

                def keys_turned(h, c):
                    act.wait_ge(kT_mm.sem, kT_mm.at(h, c + 1))
                    nc.scalar.activation(kTh[:, :, :], ps[:, SC, 0:DK].rearrange("p (t n) -> p t n", t=2),
                                         ACT.Copy).then_inc(kT_hi.sem, 1)

                split_hi(act, 0, 0)
                with act.Fori(0, HEADS) as h:
                    for c in range(NC):
                        if c == NC - 1:
                            split_hi(act, h, 1, range(KD // 2))
                        if c >= 1:
                            act.wait_ge(qT_mm.sem, qT_mm.at(h, c))
                            nc.scalar.activation(qTh[:, :, (c - 1) * P:c * P],
                                                 ps[:, PT, 0:DK].rearrange("p (t n) -> p t n", t=2),
                                                 ACT.Copy, scale=DK ** -0.5).then_inc(qT_hi.sem, 1)
                    split_hi(act, h, 1, range(KD // 2, KD))
                    act.wait_ge(hd_in.sem, hd_in.at(h, 1))
                    split_state(h, 0, 0)
                    for c in range(NC):
                        if c == NC - 1:
                            split_hi(act, h, 2, range(KD // 2))
                        if c < NC - 1:
                            decay_keys(h, 0, c, c)
                        if c == 0:
                            act.wait_ge(qT_mm.sem, qT_mm.at(h, NC))
                            nc.scalar.activation(qTh[:, :, (NC - 1) * P:NC * P],
                                                 ps[:, PT, 0:DK].rearrange("p (t n) -> p t n", t=2),
                                                 ACT.Copy, scale=DK ** -0.5).then_inc(qT_hi.sem, 1)
                            keys_turned(h, 0)
                        act.wait_ge(proj.sem, proj.at(h, NC + c + 1))
                        nc.scalar.activation(vh[:, c, :], ps[:, (NC + c) % 2, :], ACT.Copy).then_inc(v_hi.sem, 1)
                        act.wait_ge(p_f.sem, p_f.at(h, c + 1))
                        nc.scalar.activation(ph[:, :], pf[:, :], ACT.Copy).then_inc(p_hi.sem, 1)
                        if c < NC - 1:
                            keys_turned(h, c + 1)
                        act.wait_ge(pv_mm.sem, pv_mm.at(h, c + 1))
                        if c == 0:
                            act.wait_ge(stored.sem, stored.at(h, 0))
                        nc.scalar.activation(y[:, c, :], ps[:, PV, :], ACT.Copy).then_inc(y_pv.sem, 1)
                        if c < NC - 1:
                            split_state(h, 0, c + 1)
                    split_hi(act, h, 2, range(KD // 2, KD))
                    split_state(h, 1, 0)
                    for m, c in enumerate(order(1)):
                        if m == NC - 1:
                            split_hi(act, h, BLOCKS, range(1, KD // 2))
                        if m < NC - 1:
                            decay_keys(h, 1, m, c)
                        act.wait_ge(proj.sem, proj.at(h, 2 * NC + m + 1))
                        act.wait_ge(yg_done.sem, yg_done.at(h, m))
                        nc.scalar.activation(t1[:, :], ps[:, m % 2, :], ACT.Silu).then_inc(silu.sem, 1)
                        if m >= 1:
                            act.wait_ge(stored.sem, stored.at(h, m - 1))
                            act.dma_start(y_dram[c + 1, :, bass.ds(h * DV, DV)], y[:, c + 1, :]
                                          ).then_inc(stored.sem, 16)
                        if m == NC - 2:
                            split_hi(act, h, BLOCKS, (0,))
                        if m < NC - 1:
                            split_state(h, 1, m + 1)
                    split_hi(act, h, BLOCKS, range(KD // 2, KD))
                    act.wait_ge(yg_done.sem, yg_done.at(h, NC))
                    act.wait_ge(stored.sem, stored.at(h, NC - 1))
                    act.dma_start(y_dram[0, :, bass.ds(h * DV, DV)], y[:, 0, :]).then_inc(stored.sem, 16)
                act.wait_ge(stored.sem, stored.at(HEADS - 1, NC))

            @block.vector
            def _(dve):
                def state_lo(h, d, m):
                    dve.wait_ge(s_hi.sem, s_hi.at(h, d * NC + m + 1))
                    nc.vector.tensor_tensor(Sl[:, :, :], S[:, :, :], f32(Sh[:, :, :]), ALU.subtract
                                            ).then_inc(s_lo.sem, 1)

                def keys_lo(h, d, m, c):
                    n = d * (NC - 1) + m
                    dve.wait_ge(kd_hi.sem, kd_hi.at(h, n + 1))
                    e = F_K if d == 0 else B_K
                    nc.vector.scalar_tensor_tensor(kdl[:, :], kn[:, c, :], hd[:, e:e + 1], f32(kdh[:, :]),
                                                   ALU.mult, ALU.subtract).then_inc(kd_lo.sem, 1)

                def update(h, d, m):
                    n = d * (NC - 1) + m
                    dve.wait_ge(s_lo.sem, s_lo.at(h, d * NC + m + 1))
                    dve.wait_ge(u_mm.sem, u_mm.at(h, n + 1))
                    e = F_CHUNK if d == 0 else B_CHUNK
                    nc.vector.scalar_tensor_tensor(S[:, :, :], S[:, :, :], hd[:, e:e + 1], ps[:, U:U + 2, :],
                                                   ALU.mult, ALU.add).then_inc(s_f32.sem, 1)

                def qT_lo_half(h, c):
                    dve.wait_ge(qT_hi.sem, qT_hi.at(h, c + 1))
                    nc.vector.scalar_tensor_tensor(qTl[:, :, c * P:(c + 1) * P],
                                                   ps[:, PT, 0:DK].rearrange("p (t n) -> p t n", t=2), DK ** -0.5,
                                                   f32(qTh[:, :, c * P:(c + 1) * P]), ALU.mult,
                                                   ALU.subtract).then_inc(qT_lo.sem, 1)

                def keys_turned_lo(h, c):
                    dve.wait_ge(kT_hi.sem, kT_hi.at(h, c + 1))
                    nc.vector.tensor_tensor(kTl[:, :, :], ps[:, SC, 0:DK].rearrange("p (t n) -> p t n", t=2),
                                            f32(kTh[:, :, :]), ALU.subtract).then_inc(kT_lo.sem, 1)

                split_odd(dve, 0, 0)
                dve.wait_ge(const_in, 16 * 5)
                with dve.Fori(0, HEADS) as h:
                    for c in range(NC):
                        if c == NC - 1:
                            split_odd(dve, h, 1, (1, 3))
                        dve.wait_ge(proj.sem, proj.at(h, c + 1))
                        if c == 0:
                            dve.wait_ge(yg_done.sem, yg_done.at(h, 0))
                        else:
                            dve.wait_ge(qT_mm.sem, qT_mm.at(h, c))
                            dve.wait_ge(rope_out.sem, rope_out.at(h, 4 * c))
                        src = ps[:, c % 2, :].rearrange("p (s f x n) -> p s f x n", s=2, f=2, x=2)
                        v1 = t1[:, :].rearrange("p (s f x n) -> p s f x n", s=2, f=2, x=2)
                        v2 = t2[:, :].rearrange("p (s f x n) -> p s f x n", s=2, f=2, x=2)
                        for f, (co, si) in enumerate(((cosr[:, c, :], sinr[:, c, :]), (cosc[:, :], sinc[:, :]))):
                            rep = lambda ap: ap.unsqueeze(1).unsqueeze(1).broadcast_to([P, 2, 2, 64])
                            nc.vector.tensor_tensor(v1[:, :, f], src[:, :, f], rep(co),
                                                    ALU.mult).then_inc(rope_cos.sem, 1)
                            nc.vector.tensor_tensor(v2[:, :, f], src[:, :, f, ::-1, :], rep(si),
                                                    ALU.mult).then_inc(rope_sin.sem, 1)
                        dve.wait_ge(rope_cos.sem, rope_cos.at(h, 2 * c + 2))
                        dve.wait_ge(rope_sin.sem, rope_sin.at(h, 2 * c + 2))
                        kout = kn[:, c, :].rearrange("p (f x n) -> p f x n", f=2, x=2)
                        for s, dst in enumerate((v1[:, 0], kout)):
                            for x, op in enumerate((ALU.subtract, ALU.add)):
                                nc.vector.tensor_tensor(dst[:, :, x], v1[:, s, :, x], v2[:, s, :, x],
                                                               op).then_inc(rope_out.sem, 1)
                        if c == NC - 1:
                            split_odd(dve, h, 1, (5,))
                        if c >= 1:
                            qT_lo_half(h, c - 1)
                        if c == 0:
                            dve.wait_ge(stored.sem, stored.at(h, 2 - NC))
                        for n in range(3 * c, min(3 * c + 3, ADA)):
                            q, k = n // KD, n % KD
                            acc = y[:, NC - 2 + q, :]
                            dve.wait_ge(raw_in[n % RAW].sem, raw_in[n % RAW].at(h, (KD + n) // RAW + 1))
                            if k == 0:
                                nc.vector.tensor_scalar(acc, raw[:, n % RAW, :], cs[:, 0, 0:1], None,
                                                        ALU.mult).then_inc(ada_step.sem, 1)
                            else:
                                dve.wait_ge(ada_step.sem, ada_step.at(h, n))
                                nc.vector.scalar_tensor_tensor(acc, raw[:, n % RAW, :], cs[:, k, 0:1], acc,
                                                               ALU.mult, ALU.add).then_inc(ada_step.sem, 1)
                    split_odd(dve, h, 1, (7,))
                    dve.wait_ge(hd_in.sem, hd_in.at(h, 1))
                    state_lo(h, 0, 0)
                    for c in range(NC):
                        if c == NC - 1:
                            split_odd(dve, h, 2, (1, 3))
                        if c < NC - 1:
                            keys_lo(h, 0, c, c)
                        if c == 0:
                            qT_lo_half(h, NC - 1)
                            keys_turned_lo(h, 0)
                        dve.wait_ge(v_hi.sem, v_hi.at(h, c + 1))
                        nc.vector.tensor_tensor(vl[:, c, :], ps[:, (NC + c) % 2, :], f32(vh[:, c, :]),
                                                ALU.subtract).then_inc(v_lo.sem, 1)
                        if c == 1:
                            dve.wait_ge(ada_mm.sem, ada_mm.at(h, 1))
                            nc.vector.tensor_tensor(mod[:, bass.ds(h * 8 + 16, 8), 0], ps[:, PT, 0:8],
                                                    vecs[:, bass.ds(h * 8 + (V_AB + 16), 8)], ALU.add
                                                    ).then_inc(ada_out.sem, 1)
                        dve.wait_ge(score_mm.sem, score_mm.at(h, c + 1))
                        dve.wait_ge(p_lo.sem, p_lo.at(h, c))
                        nc.vector.tensor_tensor(pf[:, :], ps[:, SC, 0:P], hd[:, DECAYS:], ALU.mult
                                                ).then_inc(p_f.sem, 1)
                        dve.wait_ge(p_hi.sem, p_hi.at(h, c + 1))
                        nc.vector.tensor_tensor(pl[:, :], pf[:, :], f32(ph[:, :]), ALU.subtract
                                                ).then_inc(p_lo.sem, 1)
                        if c < NC - 1:
                            keys_turned_lo(h, c + 1)
                            update(h, 0, c)
                        dve.wait_ge(qs_mm.sem, qs_mm.at(h, c + 1))
                        dve.wait_ge(y_pv.sem, y_pv.at(h, c + 1))
                        nc.vector.scalar_tensor_tensor(y[:, c, :], ps[:, QS, :], hd[:, F_Q:F_Q + 1], y[:, c, :],
                                                       ALU.mult, ALU.add).then_inc(y_f.sem, 1)
                        if c < NC - 1:
                            state_lo(h, 0, c + 1)
                    split_odd(dve, h, 2, (5, 7))
                    state_lo(h, 1, 0)
                    for m, c in enumerate(order(1)):
                        if m == NC - 1:
                            split_odd(dve, h, BLOCKS, (1, 3))
                        if m < NC - 1:
                            keys_lo(h, 1, m, c)
                        dve.wait_ge(qs_mm.sem, qs_mm.at(h, NC + m + 1))
                        if m == 0:
                            dve.wait_ge(y_f.sem, y_f.at(h, NC))
                        nc.vector.scalar_tensor_tensor(y[:, c, :], ps[:, QS, :], hd[:, B_Q:B_Q + 1], y[:, c, :],
                                                       ALU.mult, ALU.add).then_inc(y_b.sem, 1)
                        if m < NC - 1:
                            update(h, 1, m)
                        dve.wait_ge(y_b.sem, y_b.at(h, m + 1))
                        nc.vector.bn_stats(stats[:, :], y[:, c, :]).then_inc(st_done.sem, 1)
                        dve.wait_ge(st_done.sem, st_done.at(h, m + 1))
                        if m < NC - 1:
                            state_lo(h, 1, m + 1)
                        else:
                            nc.vector.memset(ve[:, :], 0.0)
                        nc.vector.bn_aggr(mv[:, :], stats[:, :]).then_inc(ag_done.sem, 1)
                        dve.wait_ge(ag_done.sem, ag_done.at(h, m + 1))
                        nc.vector.tensor_scalar(ve[:, :], mv[:, 1:2], GN_EPS, None, ALU.add).then_inc(ve_done.sem, 1)
                        dve.wait_ge(rs_done.sem, rs_done.at(h, m + 1))
                        nc.vector.tensor_scalar(y[:, c, :], y[:, c, :], mv[:, 0:1], rstd[:, :], ALU.subtract,
                                                ALU.mult).then_inc(yn_done.sem, 1)
                        dve.wait_ge(yn_done.sem, yn_done.at(h, m + 1))
                        dve.wait_ge(gated.sem, gated.at(h, m + 1))
                        nc.vector.tensor_tensor(y[:, c, :], y[:, c, :], t1[:, :], ALU.mult).then_inc(yg_done.sem, 1)
                    split_odd(dve, h, BLOCKS, (5, 7))

            @block.tensor
            def _(pe):
                def project(h, b, m, c):
                    n = b * NC + m
                    if 2 <= n < NC + 2:
                        pe.wait_ge(rope_sin.sem, rope_sin.at(h, 2 * (n - 1)))
                    elif NC + 2 <= n < 2 * NC + 2:
                        pe.wait_ge(v_lo.sem, v_lo.at(h, n - 1 - NC))
                    else:
                        pe.wait_ge(silu.sem, silu.at(h, n - 1 - 2 * NC if n >= 2 else n - 1))
                    tok = slice(c * P, (c + 1) * P)
                    for k in range(KD):
                        if b == 1 and m == 0 and k == 5:
                            turn_q(h, NC - 1)
                            turn_k(h, 0)
                        if m == 0:
                            lo_made(pe, h, b * KD + k)
                        mm = mm3(nc, ps[:, n % 2, :], hh[:, k, tok], hl[:, k, tok], wh[:, k, :], wl[:, k, :],
                                 k == 0, k == KD - 1)
                        if m == NC - 1 and k < KD - 1:
                            mm.then_inc(w_used.sem, 1)
                    mm.then_inc(proj.sem, 1)

                def turn_q(h, c):
                    pe.wait_ge(rope_out.sem, rope_out.at(h, 4 * c + 2))
                    pe.wait_ge(qT_lo.sem, qT_lo.at(h, c))
                    if c == 0:
                        pe.wait_ge(ada_out.sem, ada_out.at(h, 0))
                        pe.wait_ge(const_in, 16 * 5)
                    for t in range(2):
                        mm = nc.tensor.transpose(ps[:, PT, t * P:(t + 1) * P], t1[:, t * P:(t + 1) * P], ident[:, :])
                    mm.then_inc(qT_mm.sem, 1)

                def turn_k(h, c):
                    pe.wait_ge(p_f.sem, p_f.at(h, c))
                    pe.wait_ge(rope_out.sem, rope_out.at(h, 4 * c + 4))
                    for t in range(2):
                        mm = nc.tensor.transpose(ps[:, SC, t * P:(t + 1) * P], kn[:, c, t * P:(t + 1) * P], ident[:, :])
                    mm.then_inc(kT_mm.sem, 1)

                def read_state(h, d, m, c):
                    pe.wait_ge(s_lo.sem, s_lo.at(h, d * NC + m + 1))
                    if d == 0:
                        pe.wait_ge(y_b.sem, y_b.at(h, 0)) if m == 0 else pe.wait_ge(y_f.sem, y_f.at(h, m))
                    else:
                        pe.wait_ge(y_f.sem, y_f.at(h, NC)) if m == 0 else pe.wait_ge(y_b.sem, y_b.at(h, m))
                    for t in range(2):
                        mm = mm3(nc, ps[:, QS, :], qTh[:, t, c * P:(c + 1) * P], qTl[:, t, c * P:(c + 1) * P],
                                 Sh[:, t, :], Sl[:, t, :], t == 0, t == 1)
                    mm.then_inc(qs_mm.sem, 1)

                def make_update(h, d, m, c):
                    n = d * (NC - 1) + m
                    pe.wait_ge(kd_lo.sem, kd_lo.at(h, n + 1))
                    pe.wait_ge(s_f32.sem, s_f32.at(h, n))
                    for t in range(2):
                        mm = mm3(nc, ps[:, U + t, :], kdh[:, t * P:(t + 1) * P], kdl[:, t * P:(t + 1) * P],
                                 vh[:, c, :], vl[:, c, :], True, True)
                    mm.then_inc(u_mm.sem, 1)

                with pe.Fori(0, HEADS) as h:
                    for c in range(NC):
                        project(h, 0, c, c)
                        if c >= 1:
                            turn_q(h, c - 1)
                    for c in range(NC):
                        project(h, 1, c, c)
                        pe.wait_ge(kT_lo.sem, kT_lo.at(h, c + 1))
                        if c == 0:
                            pe.wait_ge(qT_lo.sem, qT_lo.at(h, NC))
                        pe.wait_ge(p_f.sem, p_f.at(h, c))
                        for t in range(2):
                            mm = mm3(nc, ps[:, SC, 0:P], kTh[:, t, :], kTl[:, t, :], qTh[:, t, c * P:(c + 1) * P],
                                     qTl[:, t, c * P:(c + 1) * P], t == 0, t == 1)
                        mm.then_inc(score_mm.sem, 1)
                        if c == 1:
                            pe.wait_ge(ada_step.sem, ada_step.at(h, ADA))
                            for t in range(8):
                                mm = nc.tensor.matmul(ps[:, PT, t:t + 1],
                                                      y[:, NC - 2 + t // 4, (t % 4) * P:(t % 4 + 1) * P], one[:, :],
                                                      start=True, stop=True)
                            mm.then_inc(ada_mm.sem, 1)
                        read_state(h, 0, c, c)
                        if c < NC - 1:
                            turn_k(h, c + 1)
                            pe.wait_ge(v_lo.sem, v_lo.at(h, c + 1))
                            make_update(h, 0, c, c)
                        pe.wait_ge(p_lo.sem, p_lo.at(h, c + 1))
                        pe.wait_ge(v_lo.sem, v_lo.at(h, c + 1))
                        pe.wait_ge(y_pv.sem, y_pv.at(h, c))
                        mm3(nc, ps[:, PV, :], ph[:, :], pl[:, :], vh[:, c, :], vl[:, c, :], True,
                            True).then_inc(pv_mm.sem, 1)
                    for m, c in enumerate(order(1)):
                        project(h, 2, m, c)
                        read_state(h, 1, m, c)
                        if m < NC - 1:
                            make_update(h, 1, m, c)


def phase_retention_out(nc, a, sem, scope_sb, ps, norms, part, x, y_dram, gain, mod, vecs):
    with ExitStack() as st:
        sb = scope_sb(st)
        RAW = 4
        SL = KV // RAW
        STAGES = KD * SEQ // (HEADS * DV)
        yn = x[:, :, :].rearrange("p (q t) n -> p q (t n)", q=STAGES)
        yh = sb("yh", [P, KV, SEQ], F32R)
        yl = sb("yl", [P, KV, SEQ], F32R)
        raw = sb("raw3", [P, RAW, SL, P])
        wh = sb("wh3", [P, RAW, SL, P], F32R)
        wl = sb("wl3", [P, RAW, SL, P], F32R)
        ident = norms.ident_kept
        nb = norms.kept(sq=sb("sq3", [P, 2, SEQ]))

        ident_in, x_in = sem("ident_in"), sem("x_in3")
        y_in = [sem(f"y_in{q}") for q in range(STAGES)]
        turned, turned_hi, turned_lo = sem("y_turned"), sem("y_turned_hi"), sem("y_turned_lo")
        raw_in = [Tally(sem(f"out_raw_in{q}"), 1, unit=16) for q in range(RAW)]
        w_hi = Tally(sem("out_w_hi"), RAW)
        w_lo = Tally(sem("out_w_lo"), RAW, credit=True)
        out_mm = Tally(sem("out_mm"), 1, credit=True)
        w_used = Tally(sem("out_w_used"), RAW - 1, credit=True)
        added = sem("out_added")
        GROUPS = NC * RAW

        with nc.Block() as block:
            @block.sync
            def _(sp):
                pay(sp, w_lo, w_used, out_mm)
                sp.sem_inc(added, 2)
                sp.dma_start(ident[:, :], a["ident"]).then_inc(ident_in, 16)
                for c in range(NC):
                    if c >= STAGES:
                        sp.wait_ge(turned, RAW * (c - STAGES + 1))
                    sp.dma_start(yn[:, c % STAGES, :], y_dram[c]).then_inc(y_in[c % STAGES], 16)
                    if c == 0:
                        for q in range(RAW):
                            sp.dma_start(raw[:, q, :, :], a["ret_out"][0, q]).then_inc(raw_in[q].sem, 16)
                for q in range(RAW):
                    sp.wait_ge(w_lo.sem, w_lo.at(1, q + 1 - RAW))
                    sp.dma_start(raw[:, q, :, :], a["ret_out"][1, q]).then_inc(raw_in[q].sem, 16)
                sp.wait_ge(turned, RAW * NC)
                sp.dma_start(x[:, :, :], a["xT"]).then_inc(x_in, 16)
                with sp.Fori(2, KD) as m:
                    for q in range(RAW):
                        sp.wait_ge(w_lo.sem, w_lo.at(m, q + 1 - RAW))
                        sp.dma_start(raw[:, q, :, :], a["ret_out"][bass.ds(m, 1), q]
                                     .rearrange("o p t n -> (o p) t n")).then_inc(raw_in[q].sem, 16)

            @block.gpsimd
            def _(pool):
                with pool.Fori(0, KD) as m:
                    for q in range(RAW):
                        pool.wait_ge(w_hi.sem, w_hi.at(m, q + 1))
                        nc.gpsimd.tensor_tensor(wl[:, q], raw[:, q], f32(wh[:, q]), ALU.subtract).then_inc(w_lo.sem, 1)

            @block.scalar
            def _(act):
                def split_hi(m):
                    for q in range(RAW):
                        if q < RAW - 1:
                            act.wait_ge(w_used.sem, w_used.at(m, q + 1 - (RAW - 1)))
                        else:
                            act.wait_ge(out_mm.sem, out_mm.at(m, 0))
                        act.wait_ge(raw_in[q].sem, raw_in[q].at(m, 1))
                        nc.scalar.activation(wh[:, q], raw[:, q], ACT.Copy).then_inc(w_hi.sem, 1)

                for g in range(GROUPS):
                    c, q = g // RAW, g % RAW
                    if g == 2 * RAW:
                        split_hi(0)
                    act.wait_ge(turned, g + 1)
                    nc.scalar.activation(yh[:, q * SL:(q + 1) * SL, c * P:(c + 1) * P],
                                         ps[:, q, :].rearrange("p (t n) -> p t n", n=P), ACT.Copy
                                         ).then_inc(turned_hi, 1)
                for m in range(KD):
                    if m:
                        split_hi(m)
                        act.wait_ge(added, 2 + m)
                        norms.act_square(nc, act, 2, nb, x, m - 1)
                act.wait_ge(added, 2 + KD)
                norms.act_square(nc, act, 2, nb, x, KD - 1)

            @block.vector
            def _(dve):
                nc.vector.memset(norms.ones_kept[:, :], 1.0).then_inc(norms.ones, 1)
                make_gain(nc, gain, mod, vecs, 1, 0, 4, 0, V_N2).then_inc(norms.ones, 1)
                for g in range(GROUPS):
                    c, q = g // RAW, g % RAW
                    dve.wait_ge(turned_hi, g + 1)
                    nc.vector.tensor_tensor(yl[:, q * SL:(q + 1) * SL, c * P:(c + 1) * P],
                                            ps[:, q, :].rearrange("p (t n) -> p t n", n=P),
                                            f32(yh[:, q * SL:(q + 1) * SL, c * P:(c + 1) * P]),
                                            ALU.subtract).then_inc(turned_lo, 1)
                dve.wait_ge(x_in, 16)
                for m in range(KD):
                    b = 4 + 2 * (m % 2)
                    dve.wait_ge(out_mm.sem, out_mm.at(m, 1))
                    nc.vector.scalar_tensor_tensor(x[:, m, :], ps[:, b:b + 2, :].rearrange("p s n -> p (s n)"),
                                                   part(0, 2)(m), x[:, m, :], ALU.mult, ALU.add
                                                   ).then_inc(added, 1)
                    if m:
                        norms.dve_add(nc, dve, 2, nb, m - 1)
                norms.dve_add(nc, dve, 2, nb, KD - 1)

            @block.tensor
            def _(pe):
                def turn(c):
                    pe.wait_ge(y_in[c % STAGES], 16 * (c // STAGES + 1))
                    for q in range(RAW):
                        if c:
                            pe.wait_ge(turned_lo, (c - 1) * RAW + q + 1)
                        for t in range(SL):
                            e = (q * SL + t) * P
                            mm = nc.tensor.transpose(ps[:, q, t * P:(t + 1) * P], yn[:, c % STAGES, e:e + P],
                                                     ident[:, :])
                        mm.then_inc(turned, 1)

                def products(b, q, ss):
                    for t in range(SL):
                        kt = q * SL + t
                        for s in ss:
                            tok = slice(s * HALF, (s + 1) * HALF)
                            mm = mm3(nc, ps[:, b + s, :], wh[:, q, t, :], wl[:, q, t, :], yh[:, kt, tok],
                                     yl[:, kt, tok], kt == 0, kt == KV - 1)
                    return mm

                def tile(m, b):
                    for q in range(RAW):
                        pe.wait_ge(w_lo.sem, w_lo.at(m, q + 1))
                        mm = products(b, q, (0, 1))
                        if q < RAW - 1:
                            mm.then_inc(w_used.sem, 1)
                    mm.then_inc(out_mm.sem, 1)

                pe.wait_ge(ident_in, 16)
                for c in range(NC // 2):
                    turn(c)
                pe.wait_ge(turned_lo, GROUPS // 2)
                for q in range(RAW):
                    pe.wait_ge(w_lo.sem, w_lo.at(0, q + 1))
                    products(4, q, (0,))
                    turn(NC // 2 + q)
                pe.wait_ge(turned_lo, GROUPS)
                for q in range(RAW):
                    mm = products(4, q, (1,))
                    if q < RAW - 1:
                        mm.then_inc(w_used.sem, 1)
                mm.then_inc(out_mm.sem, 1)
                tile(1, 6)
                with pe.Fori(1, KD // 2) as i:
                    for r in range(2):
                        pe.wait_ge(added, i * 2 + (r + 1))
                        tile(i * 2 + r, 4 + 2 * r)


class Ffn:

    A0, O0, O1, B0, A1, B1 = range(6)
    SLOT = {A0: 0, B0: 1, A1: 2, B1: 3}

    def __init__(self, sem, keep):
        self.raw = keep("ffn_raw", [P, 3, KD * P])
        self.wih = keep("ffn_wih", [P, 4, KD * P], F32R)
        self.wil = keep("ffn_wil", [P, 4, KD * P], F32R)
        self.raw_in = [sem(f"ffn_raw_in{q}") for q in range(3)]
        self.w_hi, self.w_lo = sem("ffn_w_hi"), sem("ffn_w_lo")
        self.in_mm = Tally(sem("ffn_in_mm"), 4)
        self.silu = Tally(sem("ffn_silu"), 2)
        self.u = Tally(sem("ffn_u"), 2)
        self.u_hi = Tally(sem("ffn_u_hi"), 2)
        self.u_lo = Tally(sem("ffn_u_lo"), 2)
        self.out_mm = Tally(sem("ffn_out_mm"), KD, credit=True)
        self.added = Tally(sem("ffn_added"), KD, credit=True)
        self.ada_in = [Tally(sem(f"ffn_ada_in{q}"), 1, unit=16) for q in range(2)]
        self.ada_step = Tally(sem("ffn_ada_step"), KD)
        self.ada_mm = Tally(sem("ffn_ada_mm"), 1)
        self.ada_out = Tally(sem("ffn_ada_out"), 1)
        self.gains = sem("ffn_gains")

    def split(self, j, r):
        if isinstance(j, int) and j == 0:
            return {self.A0: 1, self.B0: 2, self.A1: 3, self.B1: 4}[r]
        if isinstance(j, int) and j == 2 * IT:
            return j * 6 + r - 2
        return j * 6 + (r - 1)

    def loaded(self, j, r):
        if isinstance(j, int) and j == 0:
            return 16 * {self.A0: 1, self.B0: 2, self.A1: 1, self.B1: 1}[r]
        return j * 32 + 16 * (r // 3 + 1 - (r % 3 > 0))


def phase_ffn(nc, a, scope_sb, ps, norms, f, layer, part, gain, minus_half, x, cond):
    cs, one, mod, vecs, gps = cond
    with ExitStack() as st:
        sb = scope_sb(st)
        hh = sb(f"fhh{layer}", [P, KD, SEQ], F32R)
        hl = sb(f"fhl{layer}", [P, KD, SEQ], F32R)
        raw, wih, wil = f.raw, f.wih, f.wil
        woh = sb(f"woh{layer}", [P, 2, D], F32R)
        wol = sb(f"wol{layer}", [P, 2, D], F32R)
        uf = sb(f"uf{layer}", [P, 2, SEQ])
        uh = sb(f"uh{layer}", [P, 2, SEQ], F32R)
        ul = sb(f"ul{layer}", [P, 2, SEQ], F32R)
        ada = None if layer else sb("ada1", [P, 2, KD // 2, 512])
        asum = None if layer else sb("ada1_sum", [P, 512])
        nb = norms.kept(t=uf, dg=sb("fdg1", [P, SEQ]) if layer else ada[:, 0, 0:2, :].rearrange("p k n -> p (k n)"))
        nb_next = norms.kept(sq=uf)
        r0 = 2 + 2 * layer
        INB, OUTB = 0, 4
        NPS = ps[:, OUTB:OUTB + 2, :]
        shift = part(layer, 3)
        j0 = IT * layer
        last = layer == 1

        def halves_of(r):
            if r in (f.O0, f.O1):
                return woh[:, r - f.O0, :], wol[:, r - f.O0, :]
            return wih[:, f.SLOT[r], :], wil[:, f.SLOT[r], :]

        def before(j, r):
            return (j, r - 3) if r >= 3 else (j - 1, r + 3)

        first_rs = (f.A0, f.B0, f.A1, f.B1)
        all_rs = tuple(range(6))
        end_rs = (f.O0, f.O1)

        def blocks(eng, do, ada_block=None, skip=0):
            if not last:
                for r in first_rs[skip:]:
                    do(0, r)
            with eng.Fori(j0 + 1, j0 + IT + (0 if last else 1)) as j:
                for r in all_rs:
                    do(j, r)
                    if ada_block is not None and r == f.B0:
                        ada_block(j)
            if last:
                for r in end_rs:
                    do(2 * IT, r)

        with nc.Block() as block:
            @block.sync
            def _(sp):
                if not last:
                    pay(sp, f.out_mm, f.added)

                def load(j, r):
                    if not (isinstance(j, int) and j == 0 and r in (f.A0, f.A1, f.B1)):
                        sp.wait_ge(f.w_lo, f.split(*before(j, r)))
                    src = a["ffn"][j, r] if isinstance(j, int) else a["ffn"][bass.ds(j, 1), r].rearrange(
                        "o p n -> (o p) n")
                    sp.dma_start(raw[:, r % 3, :], src).then_inc(f.raw_in[r % 3], 16)

                def load_ada(n):
                    for q in range(2):
                        if not (isinstance(n, int) and n == 0):
                            sp.wait_ge(f.ada_step.sem, f.ada_step.at(n - 1, (q + 1) * KD // 2))
                        src = a["ada_layer1"][n, q] if isinstance(n, int) else a["ada_layer1"][
                            bass.ds(n, 1), q].rearrange("o p k n -> (o p) k n")
                        sp.dma_start(ada[:, q, :, :], src).then_inc(f.ada_in[q].sem, 16)

                if not last:
                    for r in first_rs:
                        load(0, r)
                    sp.wait_ge(norms.spread.sem, norms.spread.at(r0, 1))
                    load_ada(0)
                blocks(sp, load, None if last else load_ada, skip=4)

            @block.gpsimd
            def _(pool):
                def split_lo(j, r):
                    hi, lo = halves_of(r)
                    pool.wait_ge(f.w_hi, f.split(j, r))
                    nc.gpsimd.tensor_tensor(lo, raw[:, r % 3, :], f32(hi), ALU.subtract).then_inc(f.w_lo, 1)

                norms.pool_rstd(nc, pool, r0, nb, minus_half)
                if not last:
                    split_lo(0, f.A0)
                norms.pool_lo(nc, pool, r0, nb, hl, hh)
                blocks(pool, split_lo, skip=1)

            @block.scalar
            def _(act):
                def split_hi(j, r):
                    hi, lo = halves_of(r)
                    if r in (f.O0, f.O1):
                        act.wait_ge(f.out_mm.sem, f.out_mm.at(j - 1, 0))
                    elif not (isinstance(j, int) and j == 0):
                        act.wait_ge(f.in_mm.sem, f.in_mm.at(j - 1, f.SLOT[r] + 1))
                    act.wait_ge(f.raw_in[r % 3], f.loaded(j, r))
                    nc.scalar.activation(hi, raw[:, r % 3, :], ACT.Copy).then_inc(f.w_hi, 1)

                def gate(i, t):
                    act.wait_ge(f.in_mm.sem, f.in_mm.at(i, 2 * t + 1))
                    nc.scalar.activation(uf[:, t, :], ps[:, INB:INB + 2, :].rearrange("p s n -> p (s n)"),
                                         ACT.Silu).then_inc(f.silu.sem, 1)

                def u_hi(i, t):
                    act.wait_ge(f.u.sem, f.u.at(i, t + 1))
                    nc.scalar.activation(uh[:, t, :], uf[:, t, :], ACT.Copy).then_inc(f.u_hi.sem, 1)

                def iteration(i, rs):
                    gate(i, 0)
                    for r in rs:
                        if r in (f.A0, f.O0, f.O1):
                            split_hi(i + 1, r)
                    u_hi(i, 0)
                    if f.B0 in rs:
                        split_hi(i + 1, f.B0)
                    gate(i, 1)
                    if f.A1 in rs:
                        split_hi(i + 1, f.A1)
                    u_hi(i, 1)
                    if f.B1 in rs:
                        split_hi(i + 1, f.B1)

                if not last:
                    split_hi(0, f.A0)
                norms.act_shift(nc, act, r0, nb, shift, lambda k: hh[:, k, :])
                if not last:
                    for r in first_rs[1:]:
                        split_hi(0, r)
                with act.Fori(j0, j0 + IT - (1 if last else 0)) as i:
                    iteration(i, all_rs)
                if last:
                    iteration(2 * IT - 1, end_rs)
                for m in range(KD):
                    act.wait_ge(f.u_lo.sem, f.u_lo.at(j0 + IT - 1, 2))
                    act.wait_ge(f.added.sem, f.added.at(j0 + IT - 1, m + 1))
                    norms.act_square(nc, act, r0 + 1, nb_next, x, m)

            @block.vector
            def _(dve):
                def output(i, end=False):
                    for m in range(KD):
                        b = OUTB + 2 * (m % 2)
                        dve.wait_ge(f.out_mm.sem, f.out_mm.at(i, m + 1))
                        nc.vector.scalar_tensor_tensor(x[:, m, :], ps[:, b:b + 2, :].rearrange("p s n -> p (s n)"),
                                                       part(layer, 5)(m), x[:, m, :], ALU.mult, ALU.add
                                                       ).then_inc(f.added.sem, 1)
                        if end and m:
                            norms.dve_add(nc, dve, r0 + 1, nb_next, m - 1)
                    if end:
                        norms.dve_add(nc, dve, r0 + 1, nb_next, KD - 1)

                def product(i, t):
                    dve.wait_ge(f.in_mm.sem, f.in_mm.at(i, 2 * t + 2))
                    dve.wait_ge(f.silu.sem, f.silu.at(i, t + 1))
                    nc.vector.tensor_tensor(uf[:, t, :], ps[:, INB + 2:INB + 4, :].rearrange("p s n -> p (s n)"),
                                            uf[:, t, :], ALU.mult).then_inc(f.u.sem, 1)
                    dve.wait_ge(f.u_hi.sem, f.u_hi.at(i, t + 1))
                    nc.vector.tensor_tensor(ul[:, t, :], uf[:, t, :], f32(uh[:, t, :]), ALU.subtract
                                            ).then_inc(f.u_lo.sem, 1)

                def ada_sum(n):
                    for k in range(KD):
                        if k % (KD // 2) == 0:
                            dve.wait_ge(f.ada_in[k * 2 // KD].sem, f.ada_in[k * 2 // KD].at(n, 1))
                        w = ada[:, k * 2 // KD, k % (KD // 2), :]
                        if k == 0:
                            if not (isinstance(n, int) and n == 0):
                                dve.wait_ge(f.ada_mm.sem, f.ada_mm.at(n - 1, 1))
                            nc.vector.tensor_scalar(asum[:, :], w, cs[:, 0, 0:1], None, ALU.mult
                                                    ).then_inc(f.ada_step.sem, 1)
                        else:
                            dve.wait_ge(f.ada_step.sem, f.ada_step.at(n, k))
                            nc.vector.scalar_tensor_tensor(asum[:, :], w, cs[:, k, 0:1], asum[:, :], ALU.mult, ALU.add
                                                           ).then_inc(f.ada_step.sem, 1)

                def ada_add(n):
                    dve.wait_ge(f.ada_mm.sem, f.ada_mm.at(n, 1))
                    to, bias = ((mod[:, 48 + 4 * n:52 + 4 * n, 0], vecs[:, V_AB + 48 + 4 * n:V_AB + 52 + 4 * n])
                                if isinstance(n, int) else
                                (mod[:, bass.ds(n * 4 + 48, 4), 0], vecs[:, bass.ds(n * 4 + (V_AB + 48), 4)]))
                    nc.vector.tensor_tensor(to, ps[:, OUTB + 3, 0:4], bias, ALU.add).then_inc(f.ada_out.sem, 1)

                norms.dve_mean(nc, dve, r0, nb, NPS)
                norms.dve_diag(nc, dve, r0, nb)
                norms.dve_scale(nc, dve, r0, nb, NPS, x, gain[:, 1 + 2 * layer, :], shift, hl, hh)
                if not last:
                    ada_sum(0)
                    ada_add(0)
                product(j0, 0)
                if not last:
                    ada_sum(1)
                product(j0, 1)
                with dve.Fori(j0 + 1, j0 + IT) as i:
                    if not last:
                        ada_add(i)
                    output(i - 1)
                    product(i, 0)
                    if not last:
                        ada_sum(i + 1)
                    product(i, 1)
                if not last:
                    ada_add(ADA_LAYER1 - 1)
                output(j0 + IT - 1, end=True)
                if not last:
                    dve.wait_ge(f.ada_out.sem, f.ada_out.at(ADA_LAYER1 - 1, 1))
                    make_gain(nc, gain, mod, vecs, 2, 1, 1, 0, V_N1 + 8).then_inc(f.gains, 1)
                    make_gain(nc, gain, mod, vecs, 3, 1, 4, 0, V_N2 + 8).then_inc(f.gains, 1)
                    nc.vector.tensor_tensor(gps[:, :], mod[:, 48 + 16:48 + 24, 0], vecs[:, V_PS:V_PS + 8],
                                            ALU.mult).then_inc(f.gains, 1)

            @block.tensor
            def _(pe):
                def project(i, n):
                    r = (f.A0, f.B0, f.A1, f.B1)[n]
                    pe.wait_ge(f.w_lo, f.split(i, r))
                    if n >= 2:
                        pe.wait_ge((f.silu, f.u)[n % 2].sem, (f.silu, f.u)[n % 2].at(i, 1))
                    elif not (isinstance(i, int) and i == 0):
                        pe.wait_ge((f.silu, f.u)[n % 2].sem, (f.silu, f.u)[n % 2].at(i, 0))
                    for k in range(KD):
                        if isinstance(i, int) and n == 0:
                            norms.lo_made(pe, r0, k)
                        for s in range(2):
                            tok = slice(s * HALF, (s + 1) * HALF)
                            cols = slice(k * P, (k + 1) * P)
                            mm = mm3(nc, ps[:, INB + 2 * (n % 2) + s, :], wih[:, n, cols], wil[:, n, cols],
                                     hh[:, k, tok], hl[:, k, tok], k == 0, k == KD - 1)
                    mm.then_inc(f.in_mm.sem, 1)

                def output(i, end=False):
                    if end:
                        pe.wait_ge(f.u_lo.sem, f.u_lo.at(i, 1))
                        pe.wait_ge(f.w_lo, f.split(i + 1, f.O1))
                        for m in range(2):
                            pe.wait_ge(f.added.sem, f.added.at(i, m - 1))
                            if m == 1 and not last:
                                pe.wait_ge(f.ada_out.sem, f.ada_out.at(i + 1, 1))
                            for s in range(2):
                                tok = slice(s * HALF, (s + 1) * HALF)
                                cols = slice(m * P, (m + 1) * P)
                                mm3(nc, ps[:, OUTB + 2 * m + s, :], woh[:, 0, cols], wol[:, 0, cols],
                                    uh[:, 0, tok], ul[:, 0, tok], True, False)
                    pe.wait_ge(f.u_lo.sem, f.u_lo.at(i, 2))
                    pe.wait_ge(f.w_lo, f.split(i + 1, f.O1))
                    for m in range(KD):
                        pe.wait_ge(f.added.sem, f.added.at(i, m - 1))
                        if m == 1 and not last:
                            pe.wait_ge(f.ada_out.sem, f.ada_out.at(i + 1, 1))
                        for s in range(2):
                            tok = slice(s * HALF, (s + 1) * HALF)
                            cols = slice(m * P, (m + 1) * P)
                            for t in range(1 if end and m < 2 else 0, 2):
                                mm = mm3(nc, ps[:, OUTB + 2 * (m % 2) + s, :], woh[:, t, cols], wol[:, t, cols],
                                         uh[:, t, tok], ul[:, t, tok], t == 0, t == 1)
                        mm.then_inc(f.out_mm.sem, 1)

                def ada_turn(n):
                    pe.wait_ge(f.ada_step.sem, f.ada_step.at(n, KD))
                    if not (isinstance(n, int) and n == 0):
                        pe.wait_ge(f.added.sem, f.added.at(n - 2, KD))
                    for t in range(4):
                        mm = nc.tensor.matmul(ps[:, OUTB + 3, t:t + 1], asum[:, t * P:(t + 1) * P], one[:, :],
                                              start=True, stop=True)
                    mm.then_inc(f.ada_mm.sem, 1)

                norms.pe_total(nc, pe, r0, nb, NPS)
                norms.pe_spread(nc, pe, r0, nb, NPS)
                project(j0, 0)
                if not last:
                    ada_turn(0)
                for n in range(1, 4):
                    project(j0, n)
                with pe.Fori(j0 + 1, j0 + IT) as i:
                    project(i, 0)
                    if not last:
                        ada_turn(i)
                    output(i - 1)
                    for n in range(1, 4):
                        project(i, n)
                if not last:
                    ada_turn(ADA_LAYER1 - 1)
                output(j0 + IT - 1, end=True)


def phase_pool(nc, a, sem, scope_sb, ps, norms, part, gain, gps, minus_half, x):
    with ExitStack() as st:
        sb = scope_sb(st)
        h = sb("ph_h", [P, KD, PAD + SEQ + PAD])
        sums = {"dve": sb("sums", [P, 2, PAD + SEQ + PAD]), "pool": sb("sums_pool", [P, 2, PAD + SEQ + PAD])}
        d = sb("d", [P, 2, SEQ])
        dh = sb("dh", [P, 4, SEQ], F32R)
        dl = sb("dl", [P, 4, SEQ], F32R)
        raw = sb("praw", [P, KD, 2 * P])
        wh = sb("pwh", [P, KD, 2 * P], F32R)
        wl = sb("pwl", [P, KD, 2 * P], F32R)
        edge = sb("edge", [P, 4, 2, PAD])
        nb = norms.kept(t=d, dg=sb("pool_dg", [P, SEQ]))
        nb_next = norms.kept(sq=d)
        r = 3
        NPS = ps[:, 6:8, :]
        pw_in, w_hi, w_lo = sem("pool_in"), sem("pool_w_hi"), sem("pool_w_lo")
        zero, diff, fix, fixed = (sem(f"pool_{n}") for n in ("pads", "diff", "edge_mean", "edges"))
        level = {"dve": sem("pool_level_dve"), "pool": sem("pool_level_gpsimd")}
        d_hi, mm_done, added = sem("pool_d_hi"), sem("pool_mm"), sem("pool_added")
        d_lo = [sem(f"pool_d_lo_{n}") for n in ("even", "odd")]
        GPSIMD_TILES = (3, 5, 7)

        def steps(k):
            return k // 2 + 1

        def window_sums(to, eng, who, k, before):
            w = WINDOWS[k // 2]
            src, reach = h[:, k, :], 1
            for n in range(steps(k)):
                off = reach // 2
                lo_t, hi_t = -(w // 2 - reach), SEQ + (w // 2 - reach)
                dst = sums[who][:, n % 2, :]
                if reach == 1:
                    a0, a1 = src[:, PAD + lo_t - 1:PAD + hi_t - 1], src[:, PAD + lo_t:PAD + hi_t]
                else:
                    a0 = src[:, PAD + lo_t - off:PAD + hi_t - off]
                    a1 = src[:, PAD + lo_t + off:PAD + hi_t + off]
                if n:
                    eng.wait_ge(level[who], before + n)
                to.tensor_tensor(dst[:, PAD + lo_t:PAD + hi_t], a0, a1, ALU.add).then_inc(level[who], 1)
                src, reach = dst, 2 * reach

        def lo_of(to, eng, k):
            eng.wait_ge(diff, k + 1)
            eng.wait_ge(fixed, 2 * (k + 1))
            eng.wait_ge(d_hi, k + 1)
            to.tensor_tensor(dl[:, k % 4, :], d[:, k % 2, :], f32(dh[:, k % 4, :]), ALU.subtract
                             ).then_inc(d_lo[k % 2], 1)

        with nc.Block() as block:
            @block.sync
            def _(sp):
                sp.dma_start(raw[:, :, :], a["pool_w"]).then_inc(pw_in, 16)
                sp.dma_start(edge[:, :, :, :], a["edge"]).then_inc(pw_in, 16)

            @block.gpsimd
            def _(pool):
                norms.pool_rstd(nc, pool, r, nb, minus_half)
                pool.wait_ge(w_hi, 1)
                nc.gpsimd.tensor_tensor(wl[:, :, :], raw[:, :, :], f32(wh[:, :, :]), ALU.subtract).then_inc(w_lo, 1)
                pool.wait_ge(zero, 2)
                before = 0
                for k in GPSIMD_TILES:
                    pool.wait_ge(norms.hi.sem, norms.hi.at(r, k + 1))
                    if before:
                        pool.wait_ge(fixed, 2 * (k - 1))
                        pool.wait_ge(diff, k - 1)
                    window_sums(nc.gpsimd, pool, "pool", k, before)
                    before += steps(k)
                    for even in {3: (0, 2), 5: (4,), 7: (6,)}[k]:
                        lo_of(nc.gpsimd, pool, even)

            @block.scalar
            def _(act):
                act.wait_ge(pw_in, 32)
                nc.scalar.activation(wh[:, :, :], raw[:, :, :], ACT.Copy).then_inc(w_hi, 1)
                norms.act_shift(nc, act, r, nb, part(1, 0), lambda k: h[:, k, PAD:PAD + SEQ])
                for k in range(KD):
                    act.wait_ge(fixed, 2 * (k + 1))
                    act.wait_ge(diff, k + 1)
                    if k >= 4:
                        act.wait_ge(mm_done, 2 * (k // 2 - 1))
                    nc.scalar.activation(dh[:, k % 4, :], d[:, k % 2, :], ACT.Copy).then_inc(d_hi, 1)
                act.wait_ge(d_lo[0], KD // 2)
                act.wait_ge(d_lo[1], KD // 2)
                for m in range(KD):
                    act.wait_ge(added, m + 1)
                    norms.act_square(nc, act, r + 1, nb_next, x, m)

            @block.vector
            def _(dve):
                nc.vector.memset(h[:, :, 0:PAD], 0.0).then_inc(zero, 1)
                nc.vector.memset(h[:, :, PAD + SEQ:], 0.0).then_inc(zero, 1)
                norms.dve_mean(nc, dve, r, nb, NPS)
                norms.dve_diag(nc, dve, r, nb)
                norms.dve_scale(nc, dve, r, nb, NPS, x, gain[:, 2, :], part(1, 0), None, None)
                dve.wait_ge(zero, 2)
                dve.wait_ge(pw_in, 32)
                before = {"dve": 0, "pool": 0}
                for k in range(KD):
                    g = k // 2
                    w = WINDOWS[g]
                    who = "pool" if k in GPSIMD_TILES else "dve"
                    dve.wait_ge(norms.hi.sem, norms.hi.at(r, k + 1))
                    if who == "dve":
                        window_sums(nc.vector, dve, who, k, before[who])
                    before[who] += steps(k)
                    dve.wait_ge(level[who], before[who])
                    src = sums[who][:, (steps(k) - 1) % 2, :]
                    if k < 2:
                        dve.wait_ge(norms.hi.sem, norms.hi.at(r, KD - 1 + k))
                    else:
                        dve.wait_ge(d_hi, k - 1)
                        dve.wait_ge(d_lo[k % 2], k // 2)
                    nc.vector.scalar_tensor_tensor(d[:, k % 2, :], src[:, PAD:PAD + SEQ], 1.0 / w,
                                                   h[:, k, PAD:PAD + SEQ], ALU.mult, ALU.subtract).then_inc(diff, 1)
                    dve.wait_ge(diff, k + 1)
                    for s, at in enumerate((0, SEQ - w // 2)):
                        e = slice(PAD + at, PAD + at + w // 2)
                        nc.vector.tensor_tensor(d[:, k % 2, at:at + w // 2], src[:, e], edge[:, g, s, 0:w // 2],
                                                ALU.mult).then_inc(fix, 1)
                    for s, at in enumerate((0, SEQ - w // 2)):
                        e = slice(PAD + at, PAD + at + w // 2)
                        dve.wait_ge(fix, 2 * k + s + 1)
                        nc.vector.tensor_tensor(d[:, k % 2, at:at + w // 2], d[:, k % 2, at:at + w // 2], h[:, k, e],
                                                ALU.subtract).then_inc(fixed, 1)
                    if k % 2 == 0 and k:
                        lo_of(nc.vector, dve, k - 1)
                lo_of(nc.vector, dve, KD - 1)
                for m in range(KD):
                    b = 2 * (m % 4)
                    dve.wait_ge(mm_done, m + 1)
                    nc.vector.scalar_tensor_tensor(x[:, m, :], ps[:, b:b + 2, :].rearrange("p s n -> p (s n)"),
                                                   gps[:, m:m + 1], x[:, m, :], ALU.mult, ALU.add).then_inc(added, 1)
                    if m:
                        norms.dve_add(nc, dve, r + 1, nb_next, m - 1)
                norms.dve_add(nc, dve, r + 1, nb_next, KD - 1)

            @block.tensor
            def _(pe):
                norms.pe_total(nc, pe, r, nb, NPS)
                norms.pe_spread(nc, pe, r, nb, NPS)
                pe.wait_ge(w_lo, 1)
                for m in range(KD):
                    g, b = m // 2, 2 * (m % 4)
                    for n in range(2):
                        pe.wait_ge(d_lo[n], g + 1)
                    if m >= 4:
                        pe.wait_ge(added, m - 3)
                    for s in range(2):
                        tok = slice(s * HALF, (s + 1) * HALF)
                        for t in range(2):
                            cols = slice((m % 2) * P, (m % 2 + 1) * P)
                            e = (2 * g + t) % 4
                            mm = mm3(nc, ps[:, b + s, :], wh[:, 2 * g + t, cols], wl[:, 2 * g + t, cols],
                                     dh[:, e, tok], dl[:, e, tok], t == 0, t == 1)
                    mm.then_inc(mm_done, 1)


def phase_final(nc, a, sem, scope_sb, ps, norms, vecs, minus_half, x, out):
    with ExitStack() as st:
        sb = scope_sb(st)
        nb = norms.kept(dg=sb("final_dg", [P, SEQ]))
        stored = sem("out_stored")
        r = 5
        with nc.Block() as block:
            @block.sync
            def _(sp):
                for k in range(KD):
                    sp.wait_ge(norms.scaled.sem, norms.scaled.at(r, k + 1))
                    sp.dma_start(out[:, k, :], x[:, k, :]).then_inc(stored, 16)
                sp.wait_ge(stored, 16 * KD)

            @block.vector
            def _(dve):
                norms.dve_mean(nc, dve, r, nb, ps)
                norms.dve_diag(nc, dve, r, nb)
                dve.wait_ge(norms.spread.sem, norms.spread.at(r, 1))
                for k in range(KD):
                    nc.vector.scalar_tensor_tensor(x[:, k, :], x[:, k, :], vecs[:, V_FIN + k:V_FIN + k + 1],
                                                   norms.rstd_of(nb, ps), ALU.mult, ALU.mult
                                                   ).then_inc(norms.scaled.sem, 1)

            @block.tensor
            def _(pe):
                norms.pe_total(nc, pe, r, nb, ps)
                norms.pe_spread(nc, pe, r, nb, ps)

            @block.gpsimd
            def _(pool):
                norms.pool_rstd(nc, pool, r, nb, minus_half)



def lay_out(inputs):
    g = {n: np.asarray(v) for n, v in inputs.items()}
    cols = lambda v: v.reshape(-1, P).T
    a = {}
    a["xT"] = g["x"].reshape(SEQ, KD, P).transpose(2, 1, 0)
    a["ctxT"] = g["ctx"].reshape(CTX, KD, P).transpose(2, 1, 0)
    both = np.stack([cols(g["c"]), cols(g["c_ctx"])], axis=2).reshape(P, 16)
    a["vecs"] = np.concatenate([cols(g["norm1_w"]), cols(g["norm2_w"]), cols(g["final_norm_w"]), cols(g["pool_scale"]),
                                both, cols(g["ada_b"])], axis=1)
    a["log_decay"] = g["ret_log_decay"].reshape(2 * HEADS)
    ada = g["ada_w"].reshape(2, KD, P, 6 * D)
    a["ada_first"] = ada[0, :, :, :2 * D].reshape(2, KD // 2, P, ADA_FIRST, 512).transpose(3, 0, 2, 1, 4)
    a["ada_rest"] = ada[0, :, :, 2 * D:].reshape(KD, P, HEADS, 2, 512).transpose(2, 3, 0, 1, 4).reshape(
        HEADS, 2 * KD, P, 512)
    a["ada_layer1"] = ada[1].reshape(2, KD // 2, P, ADA_LAYER1, 512).transpose(3, 0, 2, 1, 4)
    w = g["ret_w_in"][0].reshape(KD, P, 6 * D)
    parts = []
    for h in range(HEADS):
        q, k = w[:, :, h * DK:(h + 1) * DK], w[:, :, D + h * DK:D + (h + 1) * DK]
        v, gg = (w[:, :, 2 * D + o + h * DV:2 * D + o + (h + 1) * DV] for o in (0, 2 * D))
        parts += [np.concatenate([q, k], axis=2), v, gg]
    a["ret_w"] = np.stack(parts + parts[:1])
    a["gn"] = np.broadcast_to(g["ret_gn_w"].reshape(HEADS, 1, DV), (HEADS, P, DV))
    a["ret_out"] = g["ret_w_out"][0].reshape(4, KV // 4, P, KD, P).transpose(3, 0, 2, 1, 4)
    win = g["ffn_w_in"].reshape(2, KD, P, 2, IT, 2, P).transpose(0, 4, 3, 5, 2, 1, 6).reshape(2 * IT, 2, 2, P, KD * P)
    wout = g["ffn_w_out"].reshape(2 * IT, 2, P, D)
    f = np.zeros((2 * IT + 1, 6, P, D), np.float32)
    f[:-1, 0], f[:-1, 3], f[:-1, 4], f[:-1, 5] = win[:, 0, 0], win[:, 1, 0], win[:, 0, 1], win[:, 1, 1]
    f[1:, 1], f[1:, 2] = wout[:, 0], wout[:, 1]
    a["ffn"] = f
    a["pool_w"] = g["pool_w"][0].reshape(KD, P, 2 * P).transpose(1, 0, 2)
    i = np.arange(P, dtype=np.float32)
    full = np.full(P, float(CHUNK), np.float32)
    a["expo"] = np.stack([i + 1, CHUNK - 1 - i, full, CTX - 1 - i, CTX - 1 - P - i,
                          CHUNK - i, i, full, i, i + P], axis=1)
    j, q = i[:, None], i[None, :]
    a["dist"] = np.stack([np.maximum(q - j, 0), np.maximum(j - q, 0)], axis=1)
    a["ident"] = np.eye(P, dtype=np.float32)
    inv = np.float32(10000.0) ** (-np.arange(0, P, 2, dtype=np.float32) / np.float32(P))
    t = np.arange(SEQ).reshape(NC, P).T
    row = (t // GRID_W).astype(np.float32)[:, :, None] * inv
    col = (np.arange(P) % GRID_W).astype(np.float32)[:, None] * inv
    a["cosr"], a["sinr"], a["cosc"], a["sinc"] = np.cos(row), np.sin(row), np.cos(col), np.sin(col)
    edge = np.zeros((P, 4, 2, PAD), np.float32)
    for n, w in enumerate(WINDOWS):
        e = np.arange(w // 2)
        edge[:, n, 0, :w // 2] = 1 / (e + w // 2).astype(np.float32)
        edge[:, n, 1, :w // 2] = 1 / (w - e).astype(np.float32)
    a["edge"] = edge
    return {n: np.ascontiguousarray(v) for n, v in a.items()}


def kernel(**inputs):
    import concourse.bacc as bacc
    from concourse.bass_utils import run_bass_kernel_spmd

    nc = bacc.Bacc("TRN2", target_bir_lowering=False, num_devices=1)
    arrays = lay_out(inputs)
    a = {n: nc.dram_tensor(f"in_{n}", v.shape, F32, kind="ExternalInput").ap() for n, v in arrays.items()}
    out = nc.dram_tensor("out_0", (P, KD, SEQ), F32, kind="ExternalOutput").ap()
    build(nc, a, out)
    r = run_bass_kernel_spmd(nc, [{f"in_{n}": v for n, v in arrays.items()}], core_ids=[0])
    return r.results[0]["out_0"].transpose(2, 1, 0).reshape(1, SEQ, D)
```
